# Optimizing a Trainium2 kernel written in Bass

```python
import math
import jax, jax.numpy as jnp
from jax import lax
import numpy as np

D_MODEL = 1024
BATCH = 1
SEQ = 256
DEPTH = 2

GRID_W = 64
CTX_LEN = 256
N_EVEN = (DEPTH + 1) // 2
N_ODD = DEPTH // 2
EPS = 1e-6
ROPE_BASE = 10000.0
BLOCK = 128

F_GROUPS = 4
F_GROUP_DIM = 128
F_WIDTH = F_GROUPS * F_GROUP_DIM

MLA_HEADS = 8
MLA_NOPE = 64
MLA_ROPE = 32
MLA_V = 64
MLA_Q_RANK = 384
MLA_KV_RANK = 256
MLA_WIDTH = MLA_HEADS * MLA_V
MLA_SCALE = 1.0 / math.sqrt(MLA_NOPE + MLA_ROPE)
EVEN_SPLITS = (F_WIDTH, F_WIDTH, MLA_Q_RANK, MLA_KV_RANK, MLA_ROPE, MLA_WIDTH)
EVEN_IN = sum(EVEN_SPLITS)
KV_COL0 = 2 * F_WIDTH + MLA_Q_RANK
KV_COL1 = KV_COL0 + MLA_KV_RANK + MLA_ROPE
EVEN_OUT = F_WIDTH + MLA_WIDTH

GQA_HEADS = 16
GQA_KV_HEADS = 4
GQA_GROUP = GQA_HEADS // GQA_KV_HEADS
GQA_HEAD_DIM = 64
WINDOW = 128
GQA_Q = GQA_HEADS * GQA_HEAD_DIM
GQA_KV = GQA_KV_HEADS * GQA_HEAD_DIM
GQA_WIDTH = GQA_Q
GQA_SCALE = 1.0 / math.sqrt(GQA_HEAD_DIM)
ODD_SPLITS = (GQA_Q, GQA_KV, GQA_KV, GQA_WIDTH)
ODD_IN = sum(ODD_SPLITS)


def split_cols(p, sizes):
    out = []
    start = 0
    for s in sizes:
        out.append(p[..., start:start + s])
        start += s
    return out

def rmsnorm(x, g):
    x32 = x.astype(jnp.float32)
    y = x32 * lax.rsqrt(jnp.mean(x32 * x32, axis=-1, keepdims=True) + EPS)
    return (y * g.astype(jnp.float32)).astype(x.dtype)

def axial_rope_tables(n, rot_dim):
    rows = n // GRID_W
    row = jnp.broadcast_to(jnp.arange(rows)[:, None], (rows, GRID_W)).reshape(-1).astype(jnp.float32)
    col = jnp.broadcast_to(jnp.arange(GRID_W)[None, :], (rows, GRID_W)).reshape(-1).astype(jnp.float32)
    nf = rot_dim // 4
    inv = ROPE_BASE ** (-jnp.arange(nf, dtype=jnp.float32) / nf)
    ang = jnp.concatenate([row[:, None] * inv, col[:, None] * inv], axis=-1)
    return jnp.cos(ang), jnp.sin(ang)

def apply_rope(x, cos, sin):
    extra = x.ndim - 3
    shp = (cos.shape[0],) + (1,) * extra + (cos.shape[1],)
    cs, sn = cos.reshape(shp), sin.reshape(shp)
    x32 = x.astype(jnp.float32)
    half = x.shape[-1] // 2
    x1, x2 = x32[..., :half], x32[..., half:]
    return jnp.concatenate([x1 * cs - x2 * sn, x2 * cs + x1 * sn], axis=-1).astype(x.dtype)

def dense_attention(q, k, v, scale):
    s = jnp.einsum('bqhd,bkhd->bhqk', q, k).astype(jnp.float32) * scale
    p = jax.nn.softmax(s, axis=-1).astype(v.dtype)
    return jnp.einsum('bhqk,bkhd->bqhd', p, v)

def blocked_dense_attention(q, k, v, scale):
    b, n, h, d = q.shape
    nb = n // BLOCK
    qb = q.reshape(b, nb, BLOCK, h, d).swapaxes(0, 1)
    o = lax.map(lambda qblk: dense_attention(qblk, k, v, scale), qb)
    return o.swapaxes(0, 1).reshape(b, n, h, v.shape[-1])

def fourier_mix(u):
    b, n, _ = u.shape
    f = jnp.fft.fft2(u.reshape(b, n, F_GROUPS, F_GROUP_DIM).astype(jnp.float32), axes=(1, 3), norm='ortho')
    return f.real.reshape(b, n, F_WIDTH).astype(u.dtype)

def mla_q(q_a, q_norm, w_qb, rope):
    b, n = q_a.shape[:2]
    q = (rmsnorm(q_a, q_norm) @ w_qb).reshape(b, n, MLA_HEADS, MLA_NOPE + MLA_ROPE)
    q_nope, q_pe = q[..., :MLA_NOPE], q[..., MLA_NOPE:]
    if rope is not None:
        q_pe = apply_rope(q_pe, *rope)
    return jnp.concatenate([q_nope, q_pe], axis=-1)

def mla_kv(kv_a, k_pe, kv_norm, w_kvb, rope):
    b, n = kv_a.shape[:2]
    kv = (rmsnorm(kv_a, kv_norm) @ w_kvb).reshape(b, n, MLA_HEADS, MLA_NOPE + MLA_V)
    k_nope, v = kv[..., :MLA_NOPE], kv[..., MLA_NOPE:]
    k_pe = k_pe[:, :, None, :]
    if rope is not None:
        k_pe = apply_rope(k_pe, *rope)
    k = jnp.concatenate([k_nope, jnp.broadcast_to(k_pe, (b, n, MLA_HEADS, MLA_ROPE))], axis=-1)
    return k, v

def even_layer(h_lat, h_ctx, w_in, q_norm, w_qb, kv_norm, w_kvb, w_out, rope, ctx_out):
    b, n, _ = h_lat.shape
    f_in, f_gate, q_a, kv_a, k_pe, m_gate = split_cols(h_lat @ w_in, EVEN_SPLITS)
    if ctx_out:
        cf_in, cf_gate, cq_a, ckv_a, ck_pe, cm_gate = split_cols(h_ctx @ w_in, EVEN_SPLITS)
    else:
        ckv_a, ck_pe = split_cols(h_ctx @ w_in[:, KV_COL0:KV_COL1], (MLA_KV_RANK, MLA_ROPE))
    k_c, v_c = mla_kv(ckv_a, ck_pe, kv_norm, w_kvb, None)
    k_l, v_l = mla_kv(kv_a, k_pe, kv_norm, w_kvb, rope)
    q_l = mla_q(q_a, q_norm, w_qb, rope)
    a_l = blocked_dense_attention(q_l, jnp.concatenate([k_c, k_l], axis=1),
                                  jnp.concatenate([v_c, v_l], axis=1), MLA_SCALE)
    y_l = jnp.concatenate([fourier_mix(f_in) * jax.nn.silu(f_gate),
                           a_l.reshape(b, n, MLA_WIDTH) * jax.nn.silu(m_gate)], axis=-1) @ w_out
    if not ctx_out:
        return y_l, None
    cb, cn, _ = h_ctx.shape
    q_c = mla_q(cq_a, q_norm, w_qb, None)
    a_c = dense_attention(q_c, k_c, v_c, MLA_SCALE)
    y_c = jnp.concatenate([fourier_mix(cf_in) * jax.nn.silu(cf_gate),
                           a_c.reshape(cb, cn, MLA_WIDTH) * jax.nn.silu(cm_gate)], axis=-1) @ w_out
    return y_l, y_c

def windowed_gqa(q, k, v, kc, vc, sink):
    b, n = q.shape[:2]
    nb = n // BLOCK
    pad = ((0, 0), (BLOCK, BLOCK), (0, 0), (0, 0))

    def band(t):
        tp = jnp.pad(t, pad).reshape(b, nb + 2, BLOCK, *t.shape[2:])
        return jnp.concatenate([tp[:, :-2], tp[:, 1:-1], tp[:, 2:]], axis=2)

    kb, vb = band(k), band(v)
    qb = q.reshape(b, nb, BLOCK, GQA_KV_HEADS, GQA_GROUP, GQA_HEAD_DIM)
    s_ctx = jnp.einsum('bnqhgd,bchd->bnhgqc', qb, kc).astype(jnp.float32) * GQA_SCALE
    s_band = jnp.einsum('bnqhgd,bnkhd->bnhgqk', qb, kb).astype(jnp.float32) * GQA_SCALE
    blk = jnp.arange(nb)[:, None, None] * BLOCK
    qpos = blk + jnp.arange(BLOCK)[None, :, None]
    kpos = blk - BLOCK + jnp.arange(3 * BLOCK)[None, None, :]
    valid = (jnp.abs(qpos - kpos) <= WINDOW) & (kpos >= 0) & (kpos < n)
    s_band = jnp.where(valid[None, :, None, None], s_band, -jnp.inf)
    s_sink = jnp.broadcast_to(sink[None, None, :, :, None, None], s_ctx.shape[:-1] + (1,))
    p = jax.nn.softmax(jnp.concatenate([s_ctx, s_band, s_sink], axis=-1), axis=-1).astype(v.dtype)
    nc = kc.shape[1]
    o = (jnp.einsum('bnhgqc,bchd->bnqhgd', p[..., :nc], vc)
         + jnp.einsum('bnhgqk,bnkhd->bnqhgd', p[..., nc:nc + 3 * BLOCK], vb))
    return o.reshape(b, n, GQA_WIDTH)

def ctx_gqa(q, k, v, sink):
    b, n = q.shape[:2]
    s = jnp.einsum('bqhgd,bchd->bhgqc', q, k).astype(jnp.float32) * GQA_SCALE
    s_sink = jnp.broadcast_to(sink[None, :, :, None, None], s.shape[:-1] + (1,))
    p = jax.nn.softmax(jnp.concatenate([s, s_sink], axis=-1), axis=-1)[..., :-1].astype(v.dtype)
    return jnp.einsum('bhgqc,bchd->bqhgd', p, v).reshape(b, n, GQA_WIDTH)

def odd_layer(h_lat, h_ctx, w_in, sink, w_out, rope, ctx_out):
    b, n, _ = h_lat.shape
    cb, cn, _ = h_ctx.shape
    q, k, v, g = split_cols(h_lat @ w_in, ODD_SPLITS)
    q = apply_rope(q.reshape(b, n, GQA_KV_HEADS, GQA_GROUP, GQA_HEAD_DIM), *rope)
    k = apply_rope(k.reshape(b, n, GQA_KV_HEADS, GQA_HEAD_DIM), *rope)
    v = v.reshape(b, n, GQA_KV_HEADS, GQA_HEAD_DIM)
    if ctx_out:
        cq, ck, cv, cg = split_cols(h_ctx @ w_in, ODD_SPLITS)
    else:
        ck, cv = split_cols(h_ctx @ w_in[:, GQA_Q:GQA_Q + 2 * GQA_KV], (GQA_KV, GQA_KV))
    ck = ck.reshape(cb, cn, GQA_KV_HEADS, GQA_HEAD_DIM)
    cv = cv.reshape(cb, cn, GQA_KV_HEADS, GQA_HEAD_DIM)
    sink_hg = sink.reshape(GQA_KV_HEADS, GQA_GROUP).astype(jnp.float32)
    y_l = (windowed_gqa(q, k, v, ck, cv, sink_hg) * jax.nn.silu(g)) @ w_out
    if not ctx_out:
        return y_l, None
    cq = cq.reshape(cb, cn, GQA_KV_HEADS, GQA_GROUP, GQA_HEAD_DIM)
    y_c = (ctx_gqa(cq, ck, cv, sink_hg) * jax.nn.silu(cg)) @ w_out
    return y_l, y_c

def first_inputs(seed: int = 0) -> dict:
    key = jax.random.key(seed)
    ks = jax.random.split(key, 17)

    def nrm(k, shape, scale):
        return jax.random.normal(k, shape, jnp.float32) * scale

    return {
        'x': nrm(ks[0], (BATCH, SEQ, D_MODEL), 1.0),
        'c': nrm(ks[1], (BATCH, D_MODEL), 1.0),
        'ctx': nrm(ks[2], (BATCH, CTX_LEN, D_MODEL), 1.0),
        'c_ctx': nrm(ks[3], (D_MODEL,), 1.0),
        'w_mod': nrm(ks[4], (DEPTH, D_MODEL, 3 * D_MODEL), 0.5 * D_MODEL ** -0.5),
        'b_mod': nrm(ks[5], (DEPTH, 3 * D_MODEL), 0.02),
        'norm_g': 1.0 + nrm(ks[6], (DEPTH, D_MODEL), 0.02),
        'e_w_in': nrm(ks[7], (N_EVEN, D_MODEL, EVEN_IN), D_MODEL ** -0.5),
        'e_q_norm': 1.0 + nrm(ks[8], (N_EVEN, MLA_Q_RANK), 0.02),
        'e_w_qb': nrm(ks[9], (N_EVEN, MLA_Q_RANK, MLA_HEADS * (MLA_NOPE + MLA_ROPE)), MLA_Q_RANK ** -0.5),
        'e_kv_norm': 1.0 + nrm(ks[10], (N_EVEN, MLA_KV_RANK), 0.02),
        'e_w_kvb': nrm(ks[11], (N_EVEN, MLA_KV_RANK, MLA_HEADS * (MLA_NOPE + MLA_V)), MLA_KV_RANK ** -0.5),
        'e_w_out': nrm(ks[12], (N_EVEN, EVEN_OUT, D_MODEL), EVEN_OUT ** -0.5),
        'o_w_in': nrm(ks[13], (N_ODD, D_MODEL, ODD_IN), D_MODEL ** -0.5),
        'o_sink': nrm(ks[14], (N_ODD, GQA_HEADS), 0.5),
        'o_w_out': nrm(ks[15], (N_ODD, GQA_WIDTH, D_MODEL), GQA_WIDTH ** -0.5),
        'final_g': 1.0 + nrm(ks[16], (D_MODEL,), 0.02),
    }

def first_block(x, c, ctx, c_ctx, w_mod, b_mod, norm_g, e_w_in, e_q_norm, e_w_qb, e_kv_norm,
              e_w_kvb, e_w_out, o_w_in, o_sink, o_w_out, final_g):
    n = x.shape[1]
    rope_mla = axial_rope_tables(n, MLA_ROPE)
    rope_gqa = axial_rope_tables(n, GQA_HEAD_DIM)
    silu_c = jax.nn.silu(c)
    silu_cc = jax.nn.silu(c_ctx)
    for l in range(DEPTH):
        last = l == DEPTH - 1
        mod_l = silu_c @ w_mod[l] + b_mod[l]
        mod_c = silu_cc @ w_mod[l] + b_mod[l]
        sh_l, sc_l, g_l = jnp.split(mod_l, 3, axis=-1)
        sh_c, sc_c, g_c = jnp.split(mod_c, 3, axis=-1)
        h_l = rmsnorm(x, norm_g[l]) * (1 + sc_l[:, None]) + sh_l[:, None]
        h_c = rmsnorm(ctx, norm_g[l]) * (1 + sc_c) + sh_c
        i = l // 2
        if l % 2 == 0:
            y_l, y_c = even_layer(h_l, h_c, e_w_in[i], e_q_norm[i], e_w_qb[i], e_kv_norm[i],
                                  e_w_kvb[i], e_w_out[i], rope_mla, not last)
        else:
            y_l, y_c = odd_layer(h_l, h_c, o_w_in[i], o_sink[i], o_w_out[i], rope_gqa, not last)
        x = x + g_l[:, None] * y_l
        if not last:
            ctx = ctx + g_c * y_c
    return rmsnorm(x, final_g)


HEAD_DIM = 64
N_BRANCH = 4
BRANCH_WIDTH = D_MODEL // N_BRANCH
POOL_WINDOWS = (2, 4, 8, 16)
N_POOL_GROUPS = len(POOL_WINDOWS)
POOL_GROUP = BRANCH_WIDTH // N_POOL_GROUPS
CONV_K = 3
MOBA_HEADS = BRANCH_WIDTH // HEAD_DIM
MOBA_BLOCK = 256
MOBA_TOPK = 3
MOBA_Q_CHUNK = 64
FOX_HEADS = BRANCH_WIDTH // HEAD_DIM
FOX_Q_BLOCK = 128
D_FF = 4 * D_MODEL
ROPE_THETA = 500000.0
ROPE_DIM = HEAD_DIM // 4
ALPHA = (2 * DEPTH) ** 0.25
BETA = (8 * DEPTH) ** -0.25
LN_EPS = 1e-5
FORGET_BIAS_INIT = 2.0
IN_SPLIT_WIDTHS = (BRANCH_WIDTH,) * 10 + (FOX_HEADS, N_BRANCH * D_MODEL)
IN_WIDTH = 10 * BRANCH_WIDTH + FOX_HEADS + N_BRANCH * D_MODEL
FORGET_COL0 = 10 * BRANCH_WIDTH


def _in_split_points():
    pts, acc = [], 0
    for w in IN_SPLIT_WIDTHS[:-1]:
        acc += w
        pts.append(acc)
    return pts

def layer_norm(x):
    xf = x.astype(jnp.float32)
    mu = jnp.mean(xf, axis=-1, keepdims=True)
    var = jnp.mean(jnp.square(xf - mu), axis=-1, keepdims=True)
    return ((xf - mu) * lax.rsqrt(var + LN_EPS)).astype(x.dtype)

def rotary_tables(positions):
    inv = ROPE_THETA ** (-jnp.arange(0, ROPE_DIM, 2, dtype=jnp.float32) / ROPE_DIM)
    ang = positions.astype(jnp.float32)[..., None] * inv
    return jnp.cos(ang)[:, None], jnp.sin(ang)[:, None]

def apply_partial_rotary(t, cos, sin):
    half = ROPE_DIM // 2
    t1, t2, rest = t[..., :half], t[..., half:ROPE_DIM], t[..., ROPE_DIM:]
    r1 = (t1 * cos - t2 * sin).astype(t.dtype)
    r2 = (t2 * cos + t1 * sin).astype(t.dtype)
    return jnp.concatenate([r1, r2, rest], axis=-1)

def to_heads(t, n_heads):
    b, s, _ = t.shape
    return t.reshape(b, s, n_heads, HEAD_DIM).transpose(0, 2, 1, 3)

def from_heads(t):
    b, h, s, d = t.shape
    return t.transpose(0, 2, 1, 3).reshape(b, s, h * d)

def pool_mixer(p, w_pool, pool_scale):
    s = p.shape[1]
    t = jnp.arange(s)
    groups = jnp.split(p, N_POOL_GROUPS, axis=-1)
    outs = []
    for g, w in zip(groups, POOL_WINDOWS):
        cs = jnp.cumsum(g.astype(jnp.float32), axis=1)
        cs_prev = jnp.pad(cs, ((0, 0), (w, 0), (0, 0)))[:, :s]
        cnt = jnp.minimum(t + 1, w).astype(jnp.float32)[None, :, None]
        outs.append(((cs - cs_prev) / cnt).astype(p.dtype) - g)
    pooled = jnp.stack(outs, axis=2)
    mixed = jnp.einsum('bsgc,gcd->bsgd', pooled, w_pool)
    return mixed.reshape(p.shape) * pool_scale

def short_conv_mixer(gate_b, gate_c, h, conv_w):
    v = gate_c * h
    z = lax.conv_general_dilated(
        v, conv_w[:, None, :], window_strides=(1,), padding=[(CONV_K - 1, 0)],
        dimension_numbers=('NWC', 'WIO', 'NWC'), feature_group_count=v.shape[-1])
    return gate_b * z

def moba_attention(q, k, v):
    b, h, s, hd = q.shape
    nblk = -(-s // MOBA_BLOCK)
    s_pad = nblk * MOBA_BLOCK
    pad = ((0, 0), (0, 0), (0, s_pad - s), (0, 0))
    kb = jnp.pad(k, pad).reshape(b, h, nblk, MOBA_BLOCK, hd)
    vb = jnp.pad(v, pad).reshape(b, h, nblk, MOBA_BLOCK, hd)
    kbar = jnp.mean(kb.astype(jnp.float32), axis=3)
    n_sel = min(MOBA_TOPK, nblk)
    scale = HEAD_DIM ** -0.5
    bi = jnp.arange(b)[:, None, None, None]
    hi = jnp.arange(h)[None, :, None, None]
    blk_ids = jnp.arange(nblk)
    n_chunks = s // MOBA_Q_CHUNK

    def chunk(ci):
        t0 = ci * MOBA_Q_CHUNK
        qc = lax.dynamic_slice_in_dim(q, t0, MOBA_Q_CHUNK, axis=2)
        tq = t0 + jnp.arange(MOBA_Q_CHUNK)
        own = t0 // MOBA_BLOCK
        score = jnp.einsum('bhqd,bhnd->bhqn', qc.astype(jnp.float32), kbar)
        score = jnp.where(blk_ids < own, score, -jnp.inf)
        _, idx = lax.top_k(score, n_sel)
        sel_valid = idx < own
        k_sel = kb[bi, hi, idx]
        v_sel = vb[bi, hi, idx]
        l_sel = jnp.einsum('bhqd,bhqkld->bhqkl', qc, k_sel).astype(jnp.float32) * scale
        l_sel = jnp.where(sel_valid[..., None], l_sel, -jnp.inf)
        k_own = lax.dynamic_index_in_dim(kb, own, axis=2, keepdims=False)
        v_own = lax.dynamic_index_in_dim(vb, own, axis=2, keepdims=False)
        l_own = jnp.einsum('bhqd,bhld->bhql', qc, k_own).astype(jnp.float32) * scale
        pos_own = own * MOBA_BLOCK + jnp.arange(MOBA_BLOCK)
        l_own = jnp.where(pos_own[None, :] <= tq[:, None], l_own, -jnp.inf)
        n_k = n_sel * MOBA_BLOCK
        logits = jnp.concatenate([l_sel.reshape(b, h, MOBA_Q_CHUNK, n_k), l_own], axis=-1)
        p = jax.nn.softmax(logits, axis=-1)
        p_sel = p[..., :n_k].reshape(b, h, MOBA_Q_CHUNK, n_sel, MOBA_BLOCK).astype(v.dtype)
        p_own = p[..., n_k:].astype(v.dtype)
        return (jnp.einsum('bhqkl,bhqkld->bhqd', p_sel, v_sel)
                + jnp.einsum('bhql,bhld->bhqd', p_own, v_own))

    out = lax.map(chunk, jnp.arange(n_chunks))
    return out.transpose(1, 2, 0, 3, 4).reshape(b, h, s, hd)

def forgetting_attention(q, k, v, log_f):
    b, h, s, hd = q.shape
    cum = jnp.cumsum(log_f, axis=-1)
    scale = HEAD_DIM ** -0.5
    s_pos = jnp.arange(s)

    def block(qi):
        t0 = qi * FOX_Q_BLOCK
        qb = lax.dynamic_slice_in_dim(q, t0, FOX_Q_BLOCK, axis=2)
        cq = lax.dynamic_slice_in_dim(cum, t0, FOX_Q_BLOCK, axis=2)
        tq = t0 + jnp.arange(FOX_Q_BLOCK)
        logits = (jnp.einsum('bhqd,bhkd->bhqk', qb, k).astype(jnp.float32) * scale
                  + cq[..., :, None] - cum[..., None, :])
        logits = jnp.where(s_pos[None, :] <= tq[:, None], logits, -jnp.inf)
        p = jax.nn.softmax(logits, axis=-1)
        return jnp.einsum('bhqk,bhkd->bhqd', p.astype(v.dtype), v)

    out = lax.map(block, jnp.arange(s // FOX_Q_BLOCK))
    return out.transpose(1, 2, 0, 3, 4).reshape(b, h, s, hd)

def hybrid_layer(x, cond_act, cos, sin, w_ada, b_ada, w_in, b_in, w_pool, pool_scale, conv_w,
                 w_branch, w_o, ln1_g, ln1_b, w_up, b_up, w_down, ln2_g, ln2_b):
    ada = (cond_act @ w_ada + b_ada)[:, None, :]
    sh1, sc1, g1, sh2, sc2, g2 = jnp.split(ada, 6, axis=-1)

    u = layer_norm(x) * (1 + sc1) + sh1
    proj = u @ w_in + b_in
    (p_in, c_b, c_c, c_h, mq, mk, mv, fq, fk, fv, f_logit, gate_logit) = jnp.split(
        proj, _in_split_points(), axis=-1)

    y_pool = pool_mixer(p_in, w_pool, pool_scale)
    y_conv = short_conv_mixer(c_b, c_c, c_h, conv_w)
    q_m = apply_partial_rotary(to_heads(mq, MOBA_HEADS), cos, sin)
    k_m = apply_partial_rotary(to_heads(mk, MOBA_HEADS), cos, sin)
    y_moba = from_heads(moba_attention(q_m, k_m, to_heads(mv, MOBA_HEADS)))
    log_f = jax.nn.log_sigmoid(f_logit.astype(jnp.float32)).transpose(0, 2, 1)
    y_fox = from_heads(forgetting_attention(to_heads(fq, FOX_HEADS), to_heads(fk, FOX_HEADS),
                                            to_heads(fv, FOX_HEADS), log_f))

    gates = jax.nn.sigmoid(gate_logit)
    branches = (y_pool, y_conv, y_moba, y_fox)
    merged = None
    for n in range(N_BRANCH):
        term = gates[..., n * D_MODEL:(n + 1) * D_MODEL] * (branches[n] @ w_branch[n])
        merged = term if merged is None else merged + term
    mixed = merged @ w_o
    x = layer_norm(ALPHA * x + g1 * mixed) * ln1_g + ln1_b

    u2 = layer_norm(x) * (1 + sc2) + sh2
    hdn = jnp.square(jax.nn.relu(u2 @ w_up + b_up))
    x = layer_norm(ALPHA * x + g2 * (hdn @ w_down)) * ln2_g + ln2_b
    return x

def second_inputs(seed: int = 0) -> dict:
    key = jax.random.key(seed)
    ks = jax.random.split(key, 24)
    f32 = jnp.float32
    nrm = lambda k, shape, s: jax.random.normal(k, shape, f32) * s
    x = jax.random.normal(ks[0], (BATCH, SEQ, D_MODEL), f32)
    c = jax.random.normal(ks[1], (BATCH, D_MODEL), f32)
    offsets = jax.random.randint(ks[2], (BATCH, 1), 0, 1024, dtype=jnp.int32)
    positions = jnp.arange(SEQ, dtype=jnp.int32)[None, :] + offsets
    w_ada = nrm(ks[3], (DEPTH, D_MODEL, 6 * D_MODEL), D_MODEL ** -0.5)
    b_ada = nrm(ks[4], (DEPTH, 6 * D_MODEL), 0.01)
    w_in = nrm(ks[5], (DEPTH, D_MODEL, IN_WIDTH), D_MODEL ** -0.5)
    b_in_raw = nrm(ks[6], (DEPTH, IN_WIDTH), 0.01)
    forget_b = FORGET_BIAS_INIT + nrm(ks[7], (DEPTH, FOX_HEADS), 0.1)
    b_in = jnp.concatenate([b_in_raw[:, :FORGET_COL0], forget_b,
                            b_in_raw[:, FORGET_COL0 + FOX_HEADS:]], axis=-1)
    w_pool = nrm(ks[8], (DEPTH, N_POOL_GROUPS, POOL_GROUP, POOL_GROUP), POOL_GROUP ** -0.5)
    pool_scale = 1.0 + nrm(ks[9], (DEPTH, BRANCH_WIDTH), 0.02)
    conv_w = nrm(ks[10], (DEPTH, CONV_K, BRANCH_WIDTH), CONV_K ** -0.5)
    w_branch = nrm(ks[11], (DEPTH, N_BRANCH, BRANCH_WIDTH, D_MODEL), BRANCH_WIDTH ** -0.5)
    w_o = nrm(ks[12], (DEPTH, D_MODEL, D_MODEL), BETA * D_MODEL ** -0.5)
    ln1_g = 1.0 + nrm(ks[13], (DEPTH, D_MODEL), 0.02)
    ln1_b = nrm(ks[14], (DEPTH, D_MODEL), 0.02)
    w_up = nrm(ks[15], (DEPTH, D_MODEL, D_FF), D_MODEL ** -0.5)
    b_up = nrm(ks[16], (DEPTH, D_FF), 0.01)
    w_down = nrm(ks[17], (DEPTH, D_FF, D_MODEL), BETA * D_FF ** -0.5)
    ln2_g = 1.0 + nrm(ks[18], (DEPTH, D_MODEL), 0.02)
    ln2_b = nrm(ks[19], (DEPTH, D_MODEL), 0.02)
    return {"x": x, "c": c, "positions": positions, "w_ada": w_ada, "b_ada": b_ada,
            "w_in": w_in, "b_in": b_in, "w_pool": w_pool, "pool_scale": pool_scale,
            "conv_w": conv_w, "w_branch": w_branch, "w_o": w_o, "ln1_g": ln1_g, "ln1_b": ln1_b,
            "w_up": w_up, "b_up": b_up, "w_down": w_down, "ln2_g": ln2_g, "ln2_b": ln2_b}

def second_block(x, c, positions, w_ada, b_ada, w_in, b_in, w_pool, pool_scale, conv_w, w_branch,
              w_o, ln1_g, ln1_b, w_up, b_up, w_down, ln2_g, ln2_b):
    cos, sin = rotary_tables(positions)
    cond_act = jax.nn.silu(c)
    for l in range(DEPTH):
        x = hybrid_layer(x, cond_act, cos, sin, w_ada[l], b_ada[l], w_in[l], b_in[l], w_pool[l],
                         pool_scale[l], conv_w[l], w_branch[l], w_o[l], ln1_g[l], ln1_b[l],
                         w_up[l], b_up[l], w_down[l], ln2_g[l], ln2_b[l])
    return x


def setup_inputs(seed=0):
    out = dict(first_inputs(seed))
    for name, value in second_inputs(seed + 1).items():
        if name != "x":
            out[name + "_2"] = value
    return out


def reference(
    x, c, ctx, c_ctx, w_mod, b_mod, norm_g, e_w_in, e_q_norm, e_w_qb, e_kv_norm, e_w_kvb,
    e_w_out, o_w_in, o_sink, o_w_out, final_g, c_2, positions_2, w_ada_2, b_ada_2, w_in_2,
    b_in_2, w_pool_2, pool_scale_2, conv_w_2, w_branch_2, w_o_2, ln1_g_2, ln1_b_2, w_up_2,
    b_up_2, w_down_2, ln2_g_2, ln2_b_2,
):
    x = first_block(
        x, c, ctx, c_ctx, w_mod, b_mod, norm_g, e_w_in, e_q_norm, e_w_qb, e_kv_norm, e_w_kvb,
        e_w_out, o_w_in, o_sink, o_w_out, final_g,
    )
    return second_block(
        x, c_2, positions_2, w_ada_2, b_ada_2, w_in_2, b_in_2, w_pool_2, pool_scale_2, conv_w_2,
        w_branch_2, w_o_2, ln1_g_2, ln1_b_2, w_up_2, b_up_2, w_down_2, ln2_g_2, ln2_b_2,
    )


_drawn_inputs = setup_inputs


def setup_inputs(seed=0):
    import zlib

    import numpy as np

    out = dict(_drawn_inputs(seed))
    spreads = {}
    factors = {'ctx': 3.235,
     'b_mod': 4.642,
     'norm_g': 8.0,
     'e_q_norm': 8.0,
     'e_w_qb': 4.067,
     'e_kv_norm': 8.0,
     'o_sink': 8.0,
     'b_ada_2': 3.238,
     'pool_scale_2': 24.47,
     'b_up_2': 8.0}
    for name, (base, spread) in spreads.items():
        noise = np.random.default_rng([zlib.crc32(name.encode()), seed]).standard_normal(out[name].shape)
        drawn = base * np.exp(spread * noise) if base else spread * noise
        out[name] = __import__('jax').numpy.asarray(drawn.astype(out[name].dtype))
    for name, factor in factors.items():
        out[name] = (out[name] * factor).astype(out[name].dtype)
    return out
```

```python
from contextlib import ExitStack

import concourse.bass as bass
from concourse import mybir

F32 = mybir.dt.float32
I32 = mybir.dt.int32
ALU = mybir.AluOpType
ACT = mybir.ActivationFunctionType
AX_X = mybir.AxisListType.X

P = 128
D = 1024
KD = D // P
N = 256
TC = N // P
TALL = 2 * TC
COLS = 512
FW, QR, KVR, ROPE = 512, 384, 256, 32
MH, NOPE = 8, 64
MHD = NOPE + ROPE
GH, GKV, HD = 16, 4, 64
BW = 256
FH = 4
FORGET0 = 10 * BW
GATE0 = FORGET0 + FH
DFF = 4 * D
LAYERS = 2
POOLW = (2, 4, 8, 16)
RMS_EPS, LN_EPS = 1e-6, 1e-5
ALPHA = (2 * LAYERS) ** 0.25
MLA_SCALE = float(MHD) ** -0.5
HEAD_SCALE = float(HD) ** -0.5
NEG = -1e30
RSQRT_BITS = 0x5F3759DF
TWO_PI_1 = 6.28125
TWO_PI_2 = 0.0019350051879882812
TWO_PI_3 = 3.0198696e-07
ROUND = 1.5 * 2.0 ** 23

V_C, V_CC, V_C2, V_NG, V_QN, V_KN, V_N = 0, 8, 16, 24, 40, 43, 45
R_CB, R_FQ, R_GT, R_UP, R_CW, R_PS, R_N = 0, 6, 10, 42, 74, 80, 82

K_ID, K_ONE, K_CAUSAL, K_WIN, K_ROPE = 0, 128, 256, 384, 512
K_INV = K_ROPE + TC * 96
K_N = K_INV + 8
KE_CH, KE_SEQ = 0, 2 * P
KE_N = KE_SEQ + TC * 2 * N
KH_POOL, KH_SEL = 0, TC * 4 * N
KH_N = KH_SEL + FH * N

WSLOTS, WCOLS = 6, 4 * COLS


def halves(*names):
    return [(name, h) for name in names for h in range(2)]


FIRST_SLABS = (halves("fin", "fgate", "qa", "kva", "mgate", "qb") + [("kvb", 0)]
               + halves("eout0", "eout1", "oq0", "oq1", "okv", "og0", "og1", "oout0", "oout1"))
LAYER_SLABS = (halves("in0", "in1", "in2", "in3", "in4", "forget")
               + [s for j in range(8) for s in halves(f"gate{j}") + [(f"branch{j}", 0)]]
               + halves("o0", "o1") + [s for j in range(8) for s in halves(f"up{j}", f"down{j}")])
assert len(LAYER_SLABS) % WSLOTS == 0

FIRST_MODS = [("shift0", 2, False), ("scale0", 2, False), ("gate0", 2, True),
              ("shift1", 2, False), ("scale1", 2, False), ("gate1", 1, True),
              ("next shift", 1, False), ("next scale", 1, False)]
LAYER_MODS = [("g1", 1, True), ("sh2", 1, False), ("sc2", 1, False), ("g2", 1, True),
              ("next shift", 1, False), ("next scale", 1, False)]


def mod_jobs(mods, c, group):
    _, streams, rows = mods[c]
    if not rows:
        return [(("mod", c), group)]
    return [(("mod", c, v, h), group) for v in range(streams) for h in range(2)]


def first_jobs():
    lo, hi, last = (0, 1, 2, 3), (4, 5, 6, 7), (7,)
    jobs = [(("vec",), last)] + mod_jobs(FIRST_MODS, 0, last) + mod_jobs(FIRST_MODS, 1, last)
    jobs += [(("xT", k), lo) for k in range(KD)]
    jobs += [(("fin", m), hi) for m in range(4)] + [(("fgate", m), lo) for m in range(4)]
    jobs += [(("qa", t), hi) for t in range(TALL)] + [(("kva", t), lo) for t in range(TALL)]
    for g in range(5):
        if g < 4:
            jobs += [(("f1", g, h), (4, 5)) for h in range(2)]
        if g > 0:
            jobs += [(("f2", g - 1), (6,))]
    jobs += [(("mgate", m), lo) for m in range(4)] + mod_jobs(FIRST_MODS, 2, (4, 5, 6, 7))
    jobs += [(("qaT", k), (4, 5)) for k in range(3)] + [(("kvaT", k), (4, 5)) for k in range(2)]
    jobs += [(("qb", h, t), lo) for h in range(2) for t in range(TALL)]
    jobs += [(("kvb", t, h), (6, 7)) for t in range(TALL) for h in range(2)]
    for h in range(MH):
        jobs += [(("qT", h), (0, 1)), (("kT", h), (2, 3))]
    for h in range(MH + 2):
        if h < MH:
            jobs += [(("S", h, i), (0, 1)) for i in range(3)]
        if 1 <= h <= MH:
            jobs += [(("PT", h - 1, i), (2, 3, 4)) for i in range(3)]
        if h >= 2 and h % 2 == 0:
            jobs += [(("PV", (h - 2) // 2), (5, 6))]
        if h in (1, 5):
            jobs += mod_jobs(FIRST_MODS, 3 + h // 4, last)
    jobs += [(("eout", h, t), lo) for h in range(2) for t in range(TALL)]
    jobs += mod_jobs(FIRST_MODS, 5, last)
    jobs += [(("oxT", k), lo) for k in range(KD)]
    jobs += [(("oq", h, t), hi) for h in range(2) for t in range(TC)]
    jobs += [(("okv", t), lo) for t in range(TALL)] + [(("og", m), hi) for m in range(4)]
    jobs += [(("oqT", i), lo) for i in range(4)] + [(("okT", g), lo) for g in range(GKV)]
    for h in range(GH + 2):
        if h < GH:
            jobs += [(("OS", h, i), (0, 1)) for i in range(2)]
        if 1 <= h <= GH:
            jobs += [(("OPT", h - 1, i), (2, 3, 4)) for i in range(2)]
        if h >= 2 and h % 2 == 0:
            jobs += [(("OPV", (h - 2) // 2), (5, 6))]
        if h == 6:
            jobs += mod_jobs(FIRST_MODS, 6, last)
    jobs += [(("oout", h, t), lo) for h in range(2) for t in range(TC)]
    return jobs + mod_jobs(FIRST_MODS, 7, last)


def layer_jobs():
    lo, hi = (0, 1, 2, 3), (4, 5, 6, 7)
    jobs = [(("xT", i), lo) for i in range(4)] + [(("cols",), (7,))]
    jobs += [((s,), lo) for s in ("pin", "cb", "cc", "ch")] + [(("mqk", t), lo) for t in range(TC)]
    jobs += [((s,), lo) for s in ("mv", "fq", "fk", "fv", "forget")]
    jobs += [(("poolT", m), (4, 5)) for m in range(2)] + [(("mixT",), (6,))]
    jobs += [(("mqT",), (4,)), (("mkT",), (5,))]
    for a in range(10):
        if a < 8:
            jobs += [(("S", a), (4, 5))]
        if a in GATES_BESIDE:
            jobs += gate_jobs(GATES_BESIDE.index(a), lo)
        if 1 <= a <= 8:
            jobs += [(("PT", a - 1), (6,))]
        if a >= 2 and a % 2 == 0:
            jobs += [(("PV", (a - 2) // 2), (7,))]
        if a in MODS_BESIDE:
            jobs += mod_jobs(LAYER_MODS, MODS_BESIDE.index(a), lo)
    jobs += gate_jobs(6, lo) + gate_jobs(7, lo)
    jobs += [(("o", h, t), lo) for h in range(2) for t in range(TC)]
    jobs += [(("x2T", i), hi) for i in range(4)] + mod_jobs(LAYER_MODS, 3, lo)
    for j in range(9):
        if j < 8:
            jobs += [(("up", j, i), lo) for i in range(2)]
        if j == 1:
            jobs += [(("down", t, h), (4 + 2 * t + h,)) for t in range(TC) for h in range(2)]
        if j in (6, 8):
            jobs += mod_jobs(LAYER_MODS, j // 2 + 1, lo)
    return jobs


GATES_BESIDE = (0, 1, 2, 3, 7, 8)
MODS_BESIDE = (1, 5, 9)


def gate_jobs(j, group):
    return [((s, j, i), group) for s in ("gate", "prod") for i in range(2)]


def place_jobs(jobs):
    turn, held, place = {}, [0] * 8, {}
    for name, group in jobs:
        n = turn.get(group, 0)
        turn[group] = n + 1
        bank = group[n % len(group)]
        assert name not in place, name
        place[name] = (bank, held[bank])
        held[bank] += 1
    return place, held


FIRST_PLACE, FIRST_HELD = place_jobs(first_jobs())
LAYER_PLACE, LAYER_HELD = place_jobs(layer_jobs())

COUNTS = {
    "dve_order": (0, 0), "act_order": (0, 0), "pool_order": (0, 0),
    "xn_ready": (2 * TALL, 2 * TC), "acc_used": (len(FIRST_MODS), len(LAYER_MODS)),
    "tanh_done": (12, 0), "q_lat": (4 + 4, 0), "kpe_ready": (1 + 2, 0), "okv_act": (2, 0),
    "max_ready": (3 * MH + GH, 8), "exp_done": (GH, 0), "p_ready": (MH + GH, 8),
    "x_out": (1, 1), "cols_ready": (0, 1), "angles_ready": (1, 0), "rotary_ready": (1, 0),
    "ctanh_done": (1, 0), "rotated": (0, 2), "forget_act": (0, 1), "forget_ready": (0, 1),
    "conv_ready": (0, 1), "merged": (0, 12), "norm1": (0, 1), "hdn_ready": (0, 8),
}


class Section:

    def __init__(self, layer=None):
        self.layer = layer
        self.place = FIRST_PLACE if layer is None else LAYER_PLACE
        self.mods = FIRST_MODS if layer is None else LAYER_MODS
        self.slabs = FIRST_SLABS if layer is None else LAYER_SLABS

    def of(self, before, per, n):
        return n if self.layer is None else self.layer * per + (before + n)

    def at(self, name, n):
        return self.of(*COUNTS[name], n)

    def bank(self, job, n):
        b, i = self.place[job]
        return b, self.of(FIRST_HELD[b], LAYER_HELD[b], i + n)

    def slab(self, name):
        n = self.slabs.index(name)
        if self.layer is None:
            return n % WSLOTS, n // WSLOTS
        s = (len(FIRST_SLABS) + n) % WSLOTS
        return s, self.of(len(FIRST_SLABS[s::WSLOTS]), len(LAYER_SLABS) // WSLOTS, n // WSLOTS)

    def chunk(self, c, q):
        return q % 2, self.of(2 * len(FIRST_MODS), 2 * len(LAYER_MODS), 2 * c + q // 2)

    def part(self, c, n):
        return self.of(len(FIRST_MODS) // 2, len(LAYER_MODS) // 2, c // 2 + n)


class Order:

    def __init__(self, eng, sem):
        self.eng, self.sem, self.n, self.start, self.sec = eng, sem, 0, 0, None

    def section(self, sec, per=0):
        self.sec, self.per = sec, per
        self.start, self.n = self.start + self.n, 0

    def link(self, ins):
        self.n += 1
        ins.then_inc(self.sem, 1)
        self.eng.wait_ge(self.sem, self.sec.of(self.start, self.per, self.n))

    def end_layer(self, layer_body=True):
        assert self.n == self.per, f"{self.sem}: {self.n} links in a layer, not {self.per}"


DVE_LINKS, ACT_LINKS, POOL_LINKS = 155, 1, 6


def program(nc, t, out):
    ctx = ExitStack()
    with ctx:
        def sb(name, shape, dt=F32, where=ctx):
            return where.enter_context(nc.sbuf_tensor(name, shape, dt))

        def sem(name):
            return ctx.enter_context(nc.semaphore(name))

        bank = [ctx.enter_context(nc.psum_tensor(f"bank{b}", [P, COLS], F32)) for b in range(8)]

        kst = sb("constants", [P, K_N])
        wring = sb("weight_ring", [P, WSLOTS, WCOLS])
        mring = sb("modulation_ring", [P, 2, 4 * COLS])
        acc = sb("modulation_sums", [P, 2, 2, D])
        x = sb("x", [P, TALL, D])
        vcol = sb("vector_columns", [P, V_N])
        ccol = sb("silu_c_columns", [P, 24])
        ctanh = sb("silu_c_tanh", [P, 24])
        mcol = sb("modulation_columns", [P, 2, 2 * KD])
        mcol2 = sb("modulation_columns_2", [P, 2, KD])
        grow1 = sb("gate_row", [P, D])
        stat = sb("statistics", [P, TALL, 12])
        mv = sb("mean_variance", [P, TALL, 2])
        nwt = sb("newton", [P, 4, TALL])
        nwi = sb("newton_bits", [P, 2, TALL], I32)
        negmax = sb("negated_maxima", [P, 2, TALL])
        esum = sb("exp_sums", [P, 2, TALL])
        rsum = sb("reciprocal_sums", [P, 2, TALL])
        esink = sb("exp_sinks", [P, 2, TC])
        rotary = sb("rotary_angles", [P, 6, TC * 8])
        posi = sb("positions", [P, TC], I32)
        idle = sb("carriers_of_waits", [P, 8 + TALL])
        posf = sb("positions_float", [P, TC])

        ident = kst[:, K_ID:K_ID + P]
        ones = kst[:, K_ONE:K_ONE + P]
        causal = kst[:, K_CAUSAL:K_CAUSAL + P]
        window = kst[:, K_WIN:K_WIN + P]
        rope_t = kst[:, K_ROPE:K_INV].rearrange("p (t n) -> p t n", t=TC)

        even = ExitStack()
        bigA = sb("even_A", [P, 4 * D], where=even)
        bigB = sb("even_B", [P, 4 * D], where=even)
        bigC = sb("even_C", [P, 4 * D], where=even)
        bigE = sb("even_E", [P, 4 * D], where=even)
        nT = sb("even_latentsT", [P, 5, 2 * N], where=even)
        ev = sb("even_v", [P, TALL, MH * NOPE], where=even)
        eyT = sb("even_yT", [P, 8, 2 * N], where=even)
        kE = sb("even_constants", [P, KE_N], where=even)
        even.close()
        A3, B3, C3, E3 = (v[:, :] for v in (bigA, bigB, bigC, bigE))
        xn_e = A3.rearrange("p (t n) -> p t n", t=TALL)
        hT_e = B3.rearrange("p (k n) -> p k n", k=KD)
        fT = C3[:, 0:4 * 2 * N].rearrange("p (k n) -> p k n", k=4)
        dft1 = C3[:, 4 * 2 * N:].rearrange("p (b t n) -> p b t n", b=2, t=TALL)
        qrow = A3[:, 0:TALL * MH * MHD].rearrange("p (t h n) -> p t h n", t=TALL, h=MH)
        krow = B3[:, 0:TALL * MH * MHD].rearrange("p (t h n) -> p t h n", t=TALL, h=MH)
        grow_e = [A3[:, 3 * D:4 * D], B3[:, 3 * D:4 * D]]
        qn = E3[:, 0:TALL * QR].rearrange("p (t n) -> p t n", t=TALL)
        kvn = E3[:, TALL * QR:TALL * (QR + KVR)].rearrange("p (t n) -> p t n", t=TALL)
        kpe = E3[:, TALL * (QR + KVR):TALL * (QR + KVR + 3 * ROPE)].rearrange(
            "p (t s n) -> p t s n", t=TALL, s=3)
        vrow = bigE
        qT_e = bigC[0:MHD, :].rearrange("p (h n) -> p h n", h=MH)
        kT_e = bigE[0:MHD, :].rearrange("p (h n) -> p h n", h=MH)
        prob_e = A3[:, 0:2 * 3 * COLS].rearrange("p (b n) -> p b n", b=2)
        probT_e = B3[:, 0:2 * 3 * COLS].rearrange("p (b i n) -> p b i n", b=2, i=3)
        tanh_e = A3[:, 0:2 * COLS].rearrange("p (b n) -> p b n", b=2)
        etmp = A3[:, 0:2 * COLS].rearrange("p (b n) -> p b n", b=2)
        qrot = E3[:, TALL * (QR + KVR + 3 * ROPE):TALL * (QR + KVR + 3 * ROPE) + 2 * 4 * ROPE].rearrange(
            "p (s n) -> p s n", s=2)

        odd = ExitStack()
        xn_o = sb("odd_xn", [P, TALL, D], where=odd)
        hT_o = sb("odd_hT", [P, KD, 2 * N], where=odd)
        oq = sb("odd_q", [P, TC, D], where=odd)
        okr = sb("odd_k", [P, TALL, GKV, 2, HD], where=odd)
        ov = sb("odd_v", [P, TALL, GKV * HD], where=odd)
        oqT = sb("odd_qT", [P, KD, N], where=odd)
        okT = sb("odd_kT", [P, GKV, 2 * N], where=odd)
        oyT = sb("odd_yT", [P, KD, N], where=odd)
        oprobT = sb("odd_probT", [P, 2, 2, 2 * N], where=odd)
        orot = sb("odd_rotary_products", [P, 2, GH, HD // 2], where=odd)
        sink = sb("sinks", [P, 2, GH], where=odd)
        odd.close()
        oflat = xn_o[:, :, :].rearrange("p t n -> p (t n)")
        oprob = oflat[:, 0:2 * 2 * COLS].rearrange("p (b i n) -> p b i n", b=2, i=2)
        otanh = oflat[:, 2 * 2 * COLS:3 * 2 * COLS].rearrange("p (b n) -> p b n", b=2)
        otmp = oflat[:, 2 * 2 * COLS:3 * 2 * COLS].rearrange("p (b n) -> p b n", b=2)
        fing = oflat[:, 3 * 2 * COLS:4 * 2 * COLS]

        hyb = ExitStack()
        kH = sb("hybrid_constants", [P, KH_N], where=hyb)
        xn = sb("xn", [P, TC, D], where=hyb)
        uT = sb("uT", [P, KD, N], where=hyb)
        merged = sb("mergedT", [P, KD, N], where=hyb)
        lnrow = sb("norm_rows", [P, 2, D], where=hyb)
        brow = sb("bias_rows", [P, 5, BW], where=hyb)
        lrow = sb("layer_rows", [R_N, P], where=hyb)
        lcol = sb("layer_columns", [P, R_N], where=hyb)
        hcol = sb("halved_gate_bias", [P, 32], where=hyb)
        fbias = sb("forget_bias", [FH, 1], where=hyb)
        wpool = sb("pool_weights", [P, 2, P], where=hyb)
        cc = sb("conv_c", [P, 2, N], where=hyb)
        chh = sb("conv_h", [P, 2, N], where=hyb)
        conv = sb("conv_v", [P, 2, N + 2], where=hyb)
        pooled = sb("pooledT", [P, 2, N], where=hyb)
        qT = sb("qT", [P, 4, N], where=hyb)
        kT = sb("kT", [P, 4, N], where=hyb)
        vr = sb("v", [P, TC, 8, HD], where=hyb)
        forget = sb("forget", [FH, 6, N], where=hyb)
        prob = sb("prob", [P, 2, 3 * P], where=hyb)
        probT = sb("probT", [P, 2, 3 * P], where=hyb)
        tanhg = sb("gate_tanh", [P, 2, COLS], where=hyb)
        term = sb("branch_terms", [P, 2, COLS], where=hyb)
        hdn = sb("hidden", [P, 2, 4, N], where=hyb)
        rtmp = sb("rotary_products", [P, 2, 8, 16], where=hyb)
        hyb.close()
        xflat = xn[:, :, :].rearrange("p t n -> p (t n)")
        mqk = xflat[:, 0:TC * COLS].rearrange("p (t n) -> p t n", t=TC)
        pin = xflat[:, TC * COLS:TC * COLS + TC * BW].rearrange("p (t n) -> p t n", t=TC)
        cb = xflat[:, TC * (COLS + BW):TC * (COLS + 2 * BW)].rearrange("p (m n) -> p m n", m=2)
        yT = x[:, TC:TALL, :].rearrange("p t n -> p (t n)").rearrange("p (b m n) -> p b m n", b=4, m=2)
        selh = kH[0:FH, KH_SEL:KH_N].rearrange("p (h n) -> p h n", h=FH)
        poolm = kH[:, KH_POOL:KH_SEL].rearrange("p (t g n) -> p t g n", t=TC, g=4)

        w_full = [sem(f"w_full{s}") for s in range(WSLOTS)]
        w_free = [sem(f"w_free{s}") for s in range(WSLOTS)]
        m_full = [sem(f"m_full{s}") for s in range(2)]
        m_free = [sem(f"m_free{s}") for s in range(2)]
        acc_init = [sem(f"acc_init{s}") for s in range(2)]
        full = [sem(f"bank_full{b}") for b in range(8)]
        free = [sem(f"bank_free{b}") for b in range(8)]
        consts_in, vecs_in, x_in, sink_in, fing_in, kE_in, kH_in, pos_in = (sem(s) for s in (
            "consts_in", "vecs_in", "x_in", "sink_in", "fing_in", "kE_in", "kH_in", "pos_in"))
        out_stored, wpool_zero, wpool_in, ln_in, bias_in, lrow_in = (sem(s) for s in (
            "out_stored", "wpool_zero", "wpool_in", "ln_in", "bias_in", "lrow_in"))
        S = {name: sem(name) for name in COUNTS}

        def w_slab(name, h, l):
            def cut(w, c0, n, k0, kn):
                return w.rearrange("(k p) n -> p k n", p=P)[:, k0:k0 + kn, c0:c0 + n], kn, n

            def layer(w):
                return w[bass.ds(l, 1)].rearrange("o k n -> (o k) n")

            e, o = t["e_w_in"][0], t["o_w_in"][0]
            split = [0, FW, 2 * FW, 2 * FW + QR, 2 * FW + QR + KVR + ROPE]
            if name in ("fin", "fgate", "qa", "kva", "mgate"):
                i = ("fin", "fgate", "qa", "kva", "mgate").index(name)
                return cut(e, split[i], (FW, FW, QR, KVR + ROPE, FW)[i], 4 * h, 4)
            if name == "qb":
                return cut(t["e_w_qb"][0], 4 * MHD * h, 4 * MHD, 0, 3)
            if name == "kvb":
                return cut(t["e_w_kvb"][0], 0, 2 * COLS, 0, 2)
            if name[:4] in ("eout", "oout"):
                w = t["e_w_out"][0] if name[0] == "e" else t["o_w_out"][0]
                return cut(w, COLS * int(name[4]), COLS, 4 * h, 4)
            if name in ("oq0", "oq1", "okv", "og0", "og1"):
                return cut(o, COLS * ("oq0", "oq1", "okv", "og0", "og1").index(name), COLS, 4 * h, 4)
            if name[:2] == "in":
                return cut(layer(t["w_in_2"]), COLS * int(name[2]), COLS, 4 * h, 4)
            if name == "forget":
                return cut(layer(t["w_in_2"]), FORGET0, FH, 4 * h, 4)
            if name[:4] == "gate":
                return cut(layer(t["w_in_2"]), GATE0 + COLS * int(name[4]), COLS, 4 * h, 4)
            if name[:6] == "branch":
                j = int(name[6])
                w = t["w_branch_2"][bass.ds(l, 1)].rearrange("o b k n -> (o b k) n")
                return cut(w, COLS * (j % 2), COLS, 2 * (j // 2), 2)
            if name[0] == "o":
                return cut(layer(t["w_o_2"]), COLS * int(name[1]), COLS, 4 * h, 4)
            if name[:2] == "up":
                return cut(layer(t["w_up_2"]), COLS * int(name[2]), COLS, 4 * h, 4)
            return cut(layer(t["w_down_2"]), 0, D, 4 * int(name[4]) + 2 * h, 2)

        def w_view(sec, name, h):
            slot = sec.slab((name, h))[0]
            _, kn, n = w_slab(name, h, 0)
            return wring[:, slot, 0:kn * n].rearrange("p (k n) -> p k n", k=kn)

        def mod_source(sec, c):
            name = sec.mods[c][0]
            if sec.layer is None and c < 6:
                return t["w_mod"][c // 3], t["b_mod"][c // 3], D * (c % 3)
            at = {"next shift": 0, "next scale": 1, "g1": 2, "sh2": 3, "sc2": 4, "g2": 5}[name]
            if sec.layer is None:
                return t["w_ada_2"][0], t["b_ada_2"][0], D * at
            l = sec.next_layer if at < 2 else sec.layer
            return (t["w_ada_2"][bass.ds(l, 1)].rearrange("o k n -> (o k) n"),
                    t["b_ada_2"][bass.ds(l, 1)].rearrange("o n -> (o n)"), D * at)

        block = ctx.enter_context(nc.Block())

        @block.sync
        def _(sp):
            def load(sec, name, h):
                slot, before = sec.slab((name, h))
                if sec.layer is not None or before > 0:
                    sp.wait_ge(w_free[slot], before)
                src, _, _ = w_slab(name, h, sec.layer)
                sp.dma_start(w_view(sec, name, h), src).then_inc(w_full[slot], 16)

            sec = Section()
            sp.dma_start(vrow[0:V_NG, 0:P][V_C:V_CC], t["c"].rearrange("o (k p) -> (o k) p", p=P)).then_inc(vecs_in, 16)
            sp.dma_start(vrow[V_CC:V_C2, 0:P], t["c_ctx"].rearrange("(k p) -> k p", p=P)).then_inc(vecs_in, 16)
            sp.dma_start(vrow[V_C2:V_NG, 0:P], t["c_2"].rearrange("o (k p) -> (o k) p", p=P)).then_inc(vecs_in, 16)
            sp.dma_start(vrow[V_NG:V_QN, 0:P], t["norm_g"].rearrange("l (k p) -> (l k) p", p=P)).then_inc(vecs_in, 16)
            sp.dma_start(vrow[V_QN:V_KN, 0:P], t["e_q_norm"].rearrange("o (k p) -> (o k) p", p=P)).then_inc(vecs_in, 16)
            sp.dma_start(vrow[V_KN:V_N, 0:P], t["e_kv_norm"].rearrange("o (k p) -> (o k) p", p=P)).then_inc(vecs_in, 16)
            sp.dma_start(x[:, 0:TC, :], t["x"][0].rearrange("(t p) n -> p t n", p=P)).then_inc(x_in, 16)
            sp.dma_start(x[:, TC:TALL, :], t["ctx"][0].rearrange("(t p) n -> p t n", p=P)).then_inc(x_in, 16)
            for name, h in FIRST_SLABS:
                load(sec, name, h)
            with sp.Fori(0, LAYERS) as l:
                sec = Section(l)
                for name, h in LAYER_SLABS:
                    load(sec, name, h)
            sp.wait_ge(S["x_out"], COUNTS["x_out"][0] + LAYERS)
            sp.dma_start(out[0].rearrange("(t p) n -> p t n", p=P), x[:, 0:TC, :]).then_inc(out_stored, 16)
            sp.wait_ge(out_stored, 16)

        @block.gpsimd
        def _(pool):
            order = Order(pool, S["pool_order"])

            def take_wait(n):
                if sec.layer is not None:
                    pool.tensor_tensor(idle[:, n:n + 1], ones[:, 0:1], ones[:, 0:1], ALU.mult)

            def mod_part(sec, c):
                b = c % 2
                if sec.layer is not None or c >= 2:
                    pool.wait_ge(S["acc_used"], sec.at("acc_used", c - 1))
                take_wait(0)
                order.link(pool.memset(acc[:, b, :, :], 0.0))
                w, bias, c0 = mod_source(sec, c)
                take_wait(1)
                pool.dma_start(acc[0:1, b, :, :], bias[c0:c0 + D].unsqueeze(0).unsqueeze(0).broadcast_to([1, 2, D])
                               ).then_inc(acc_init[b], 16)
                for q in range(4):
                    slot, before = sec.chunk(c, q)
                    if sec.layer is not None or 2 * c + q // 2 > 0:
                        pool.wait_ge(m_free[slot], before)
                    take_wait(2 + q)
                    col = c0 + COLS * (q // 2)
                    pool.dma_start(mring[:, slot, :].rearrange("p (k n) -> p k n", k=4),
                                   w.rearrange("(k p) n -> p k n", p=P)[:, 4 * (q % 2):4 * (q % 2) + 4, col:col + COLS]
                                   ).then_inc(m_full[slot], 16)

            sec = Section()
            order.section(sec)
            for c in range(len(FIRST_MODS)):
                mod_part(sec, c)
            with pool.Fori(0, LAYERS) as l:
                sec = Section(l)
                sec.next_layer = l * 0 + (LAYERS - 1)
                order.section(sec, POOL_LINKS)

                def add_terms(j, i):
                    n = 2 * (j - 2) + i
                    m = 4 * (j % 2) + 2 * i
                    b, done_ = sec.bank(("prod", j, i), 1)
                    pool.wait_ge(free[b], done_)
                    pool.tensor_tensor(merged[:, m:m + 2, :], merged[:, m:m + 2, :],
                                       term[:, i, :].rearrange("p (m n) -> p m n", m=2), ALU.add
                                       ).then_inc(S["merged"], 1)

                mod_part(sec, 0)
                mod_part(sec, 1)
                mod_part(sec, 2)
                for j in range(2, 8):
                    for i in range(2):
                        add_terms(j, i)
                    if j == 3:
                        mod_part(sec, 3)
                mod_part(sec, 4)
                mod_part(sec, 5)
                order.end_layer()

        @block.tensor
        def _(pe):
            sec = Section()

            def start(job):
                b, before = sec.bank(job, 0)
                if sec.layer is not None or before > 0:
                    pe.wait_ge(free[b], before)
                return bank[b]

            owed, last = [], [None, True]

            def track(ins):
                if owed and not last[1]:
                    last[0].then_inc(owed.pop(0), 1)
                last[0], last[1] = ins, False
                return ins

            def product(*args, **kw):
                return track(pe.matmul(*args, **kw))

            def signal(ins, sem):
                assert ins is last[0]
                if last[1]:
                    owed.append(sem)
                else:
                    ins.then_inc(sem, 1)
                    last[1] = True

            def done(ins, job):
                signal(ins, full[sec.bank(job, 0)[0]])

            def copied(job):
                b, n = sec.bank(job, 1)
                pe.wait_ge(free[b], n)

            def pay_owed(job):
                copied(job)
                o = bank[sec.bank(job, 0)[0]]
                while owed:
                    product(o[:, 0:1], ones, ones[:, 0:1], start=True, stop=True)
                    last[0].then_inc(owed.pop(0), 1)
                    last[1] = True

            def slab(name, h):
                slot, before = sec.slab((name, h))
                pe.wait_ge(w_full[slot], before * 16 + 16)
                return w_view(sec, name, h)

            def used(ins, name, h):
                signal(ins, w_free[sec.slab((name, h))[0]])

            def reduce_part(c):
                _, streams, rows = sec.mods[c]
                slot, before = sec.chunk(c, 3)
                pe.wait_ge(m_free[slot], before + 1)
                if rows:
                    for v in range(streams):
                        for h in range(2):
                            o = start(("mod", c, v, h))
                            ins = product(o[:, :], ones, acc[:, c % 2, v, COLS * h:COLS * h + COLS],
                                            start=True, stop=True)
                            done(ins, ("mod", c, v, h))
                else:
                    o = start(("mod", c))
                    for v in range(streams):
                        for k in range(KD):
                            ins = product(o[:, v * KD + k:v * KD + k + 1], acc[:, c % 2, v, P * k:P * k + P],
                                            ones[:, 0:1], start=True, stop=True)
                    done(ins, ("mod", c))
                signal(ins, S["acc_used"])

            def features_out(names, jobs, src, ntok, per, width=P):
                outs = [start(j) for j in jobs]
                for h in range(2):
                    w = slab(*names[h])
                    for m in range(len(jobs) * per):
                        o = outs[m // per][0:width, (m % per) * ntok:(m % per + 1) * ntok]
                        for k in range(4):
                            ins = product(o, w[:, k, m * width:(m + 1) * width], src(4 * h + k),
                                            start=(h + k + m % per == 0), stop=(h == 1 and k == 3),
                                            skip_group_check=per > 1)
                        if h == 1 and m % per == per - 1:
                            done(ins, jobs[m // per])
                    used(ins, *names[h])

            def tokens_out(names, jobs, src, width, c0=0, kn=4, wait=lambda k: None):
                outs = [start(j) for j in jobs]
                nh = len(names)
                for h in range(nh):
                    w = slab(*names[h])
                    for i, o in enumerate(outs):
                        for k in range(kn):
                            if i == 0:
                                wait(kn * h + k)
                            ins = product(o[:, 0:width], src(kn * h + k, i), w[:, k, c0:c0 + width],
                                            start=(h == 0 and k == 0), stop=(h == nh - 1 and k == kn - 1))
                        if h == nh - 1:
                            done(ins, jobs[i])
                    used(ins, *names[h])

            def turn(o, src, n, rows=P):
                return track(pe.transpose(o, src, ident[0:rows, 0:rows]))

            pe.wait_ge(consts_in, 16)
            pe.wait_ge(vecs_in, 16 * 6)
            done(turn(start(("vec",))[:, 0:V_N], vrow[0:V_N, 0:P], P, rows=V_N), ("vec",))
            reduce_part(0)
            reduce_part(1)

            def turn_x(name, src, k0, n0):
                pe.wait_ge(S["xn_ready"], sec.at("xn_ready", n0))
                for k in range(KD):
                    o = start((name, k))
                    for i in range(TALL):
                        ins = turn(o[:, P * i:P * i + P], src[:, i, P * k:P * k + P], P)
                    done(ins, (name, k))

            turn_x("xT", xn_e, 0, TALL)
            for k in range(KD):
                copied(("xT", k))

            def both(h):
                return [(h, 0), (h, 1)]

            features_out(both("fin"), [("fin", m) for m in range(4)], lambda k: hT_e[:, k, :], 2 * N, 1)
            features_out(both("fgate"), [("fgate", m) for m in range(4)], lambda k: hT_e[:, k, :], 2 * N, 1)
            tokens_out(both("qa"), [("qa", i) for i in range(TALL)], lambda k, i: hT_e[:, k, P * i:P * i + P], QR)
            tokens_out(both("kva"), [("kva", i) for i in range(TALL)], lambda k, i: hT_e[:, k, P * i:P * i + P],
                       KVR + ROPE)
            pe.wait_ge(kE_in, 16)
            for g in range(5):
                if g < 4:
                    copied(("fin", g))
                    for h in range(2):
                        o = start(("f1", g, h))
                        for i in range(2):
                            tt = 2 * h + i
                            ins = product(o[:, 2 * P * i:2 * P * (i + 1)], fT[:, g, P * tt:P * tt + P],
                                            kE[:, KE_CH:KE_CH + 2 * P], start=True, stop=True)
                        done(ins, ("f1", g, h))
                if g > 0:
                    copied(("f1", g - 1, 0))
                    copied(("f1", g - 1, 1))
                    o = start(("f2", g - 1))
                    for s in range(2):
                        for i in range(TC):
                            for part in range(2):
                                seq = KE_SEQ + (2 * i + part) * N
                                ins = product(o[:, N * s:N * s + N],
                                                dft1[:, (g - 1) % 2, TC * s + i, P * part:P * part + P],
                                                kE[:, seq:seq + N], start=(i + part == 0), stop=(i + part == 2))
                    done(ins, ("f2", g - 1))
            features_out(both("mgate"), [("mgate", m) for m in range(4)], lambda k: hT_e[:, k, :], 2 * N, 1)
            reduce_part(2)
            for i in range(TALL):
                copied(("qa", i))
                copied(("kva", i))
            for name, n, src in (("qaT", 3, qn), ("kvaT", 2, kvn)):
                for k in range(n):
                    o = start((name, k))
                    for i in range(TALL):
                        ins = turn(o[:, P * i:P * i + P], src[:, i, P * k:P * k + P], P)
                    done(ins, (name, k))
            for k in range(3):
                copied(("qaT", k))
            for h in range(2):
                tokens_out([("qb", h)], [("qb", h, i) for i in range(TALL)],
                           lambda k, i: nT[:, k, P * i:P * i + P], 4 * MHD, kn=3)
            for k in range(2):
                copied(("kvaT", k))
            w = slab("kvb", 0)
            for i in range(TALL):
                for h in range(2):
                    o = start(("kvb", i, h))
                    for k in range(2):
                        ins = product(o[:, :], nT[:, 3 + k, P * i:P * i + P], w[:, k, COLS * h:COLS * h + COLS],
                                        start=(k == 0), stop=(k == 1))
                    done(ins, ("kvb", i, h))
            used(ins, "kvb", 0)
            pe.wait_ge(S["q_lat"], 4)
            for h in range(2):
                for i in range(TC, TALL):
                    copied(("qb", h, i))
                for i in range(TALL):
                    copied(("kvb", i, h))
            pe.wait_ge(S["kpe_ready"], 1)
            for h in range(MH):
                for name, src in (("qT", qrow), ("kT", krow)):
                    o = start((name, h))
                    for i in range(TALL):
                        ins = turn(o[0:MHD, P * i:P * i + P], src[:, i, h, :], P)
                    done(ins, (name, h))
            for h in range(MH + 2):
                if h < MH:
                    copied(("qT", h))
                    copied(("kT", h))
                    for i in range(TC):
                        o = start(("S", h, i))
                        done(product(o[:, :], qT_e[:, h, P * i:P * i + P], kT_e[:, h, :], start=True, stop=True),
                             ("S", h, i))
                    o = start(("S", h, 2))
                    for i in range(TC):
                        ins = product(o[:, N * i:N * i + N], qT_e[:, h, N + P * i:N + P * i + P],
                                        kT_e[:, h, N:2 * N], start=True, stop=True)
                    done(ins, ("S", h, 2))
                if 1 <= h <= MH:
                    a = h - 1
                    pe.wait_ge(S["p_ready"], a + 1)
                    for i in range(3):
                        o = start(("PT", a, i))
                        for j in range(2):
                            for q in range(2):
                                c = COLS * q + P * (2 * i + j) if i < 2 else 2 * COLS + N * q + P * j
                                ins = turn(o[:, N * j + P * q:N * j + P * q + P], prob_e[:, a % 2, c:c + P], P)
                        done(ins, ("PT", a, i))
                if h >= 2:
                    a = h - 2
                    r = HD * (a % 2)
                    if a % 2 == 0:
                        pv = start(("PV", a // 2))
                    copied(("PT", a, 0))
                    copied(("PT", a, 1))
                    for kb in range(TALL):
                        ins = product(pv[r:r + HD, 0:N], ev[:, kb, NOPE * a:NOPE * a + NOPE],
                                        probT_e[:, a % 2, kb // 2, N * (kb % 2):N * (kb % 2) + N],
                                        start=(kb == 0), stop=(kb == 3))
                    copied(("PT", a, 2))
                    for j in range(2):
                        ins = product(pv[r:r + HD, N:2 * N], ev[:, TC + j, NOPE * a:NOPE * a + NOPE],
                                        probT_e[:, a % 2, 2, N * j:N * j + N], start=(j == 0), stop=(j == 1))
                    if a % 2 == 1:
                        done(ins, ("PV", a // 2))
                if h in (1, 5):
                    reduce_part(3 + h // 4)
            for g in range(4):
                copied(("f2", g))
                copied(("PV", g))
            for h in range(2):
                tokens_out(both(f"eout{h}"), [("eout", h, i) for i in range(TALL)],
                           lambda k, i: eyT[:, k, P * i:P * i + P], COLS)
            reduce_part(5)

            turn_x("oxT", xn_o, KD, 2 * TALL)
            for k in range(KD):
                copied(("oxT", k))
            for h in range(2):
                tokens_out(both(f"oq{h}"), [("oq", h, i) for i in range(TC)],
                           lambda k, i: hT_o[:, k, P * i:P * i + P], COLS)
            tokens_out(both("okv"), [("okv", i) for i in range(TALL)],
                       lambda k, i: hT_o[:, k, P * i:P * i + P], COLS)
            for g in range(2):
                features_out(both(f"og{g}"), [("og", 2 * g), ("og", 2 * g + 1)], lambda k: hT_o[:, k, 0:N], N, 2)
            pe.wait_ge(S["q_lat"], 8)
            for i in range(4):
                o = start(("oqT", i))
                for pr in range(2):
                    for tt in range(TC):
                        ins = turn(o[:, N * pr + P * tt:N * pr + P * tt + P],
                                   oq[:, tt, P * (2 * i + pr):P * (2 * i + pr) + P], P)
                done(ins, ("oqT", i))
            pe.wait_ge(S["kpe_ready"], 3)
            for i in range(TALL):
                copied(("okv", i))
            for g in range(GKV):
                o = start(("okT", g))
                for i in range(TALL):
                    ins = turn(o[:, P * i:P * i + P], okr[:, i, g, :, :].rearrange("p a b -> p (a b)"), P)
                done(ins, ("okT", g))
            for h in range(GH + 2):
                if h < GH:
                    r, g = HD * (h % 2), h // (GH // GKV)
                    copied(("oqT", h // 4))
                    copied(("okT", g))
                    for i in range(TC):
                        o = start(("OS", h, i))
                        product(o[:, :], oqT[r:r + HD, h // 2, P * i:P * i + P], okT[r:r + HD, g, :],
                                  start=True, stop=True)
                        other = P * (1 - i)
                        ins = product(o[:, other:other + P], ident, causal if i == 0 else window,
                                        start=False, stop=True, skip_group_check=True)
                        done(ins, ("OS", h, i))
                if 1 <= h <= GH:
                    a = h - 1
                    pe.wait_ge(S["p_ready"], MH + a + 1)
                    for i in range(2):
                        o = start(("OPT", a, i))
                        for j in range(2):
                            for q in range(2):
                                c = P * (2 * i + j)
                                ins = turn(o[:, N * j + P * q:N * j + P * q + P], oprob[:, a % 2, q, c:c + P], P)
                        done(ins, ("OPT", a, i))
                if h >= 2:
                    a = h - 2
                    r, g = HD * (a % 2), a // (GH // GKV)
                    if a % 2 == 0:
                        pv = start(("OPV", a // 2))
                    copied(("OPT", a, 0))
                    copied(("OPT", a, 1))
                    for kb in range(TALL):
                        ins = product(pv[r:r + HD, 0:N], ov[:, kb, HD * g:HD * g + HD],
                                        oprobT[:, a % 2, kb // 2, N * (kb % 2):N * (kb % 2) + N],
                                        start=(kb == 0), stop=(kb == 3))
                    if a % 2 == 1:
                        done(ins, ("OPV", a // 2))
                if h == 6:
                    reduce_part(6)
            for g in range(8):
                copied(("OPV", g))
            for h in range(2):
                tokens_out(both(f"oout{h}"), [("oout", h, i) for i in range(TC)],
                           lambda k, i: oyT[:, k, P * i:P * i + P], COLS)
            reduce_part(7)
            pay_owed(("mod", 7))

            pe.wait_ge(kH_in, 16)
            with pe.Fori(0, LAYERS) as l:
                sec = Section(l)
                u = lambda k: uT[:, k, :]
                ui = lambda k, i: uT[:, k, P * i:P * i + P]

                def turn_xn(name, n0):
                    pe.wait_ge(S["xn_ready"], sec.at("xn_ready", n0))
                    for i in range(4):
                        o = start((name, i))
                        for j in range(2):
                            for tt in range(TC):
                                ins = turn(o[:, N * j + P * tt:N * j + P * tt + P],
                                           xn[:, tt, P * (2 * i + j):P * (2 * i + j) + P], P)
                        done(ins, (name, i))

                turn_xn("xT", TC)
                pe.wait_ge(lrow_in, l * (16 * 6) + 16 * 6)
                done(turn(start(("cols",))[:, 0:R_N], lrow[:, :], P, rows=R_N), ("cols",))
                for i in range(4):
                    copied(("xT", i))

                def mixed_tile(name, parts):
                    outs = [start(p[0]) for p in parts]
                    for h in range(2):
                        w = slab(name, h)
                        for (job, c0, n, tok), o in zip(parts, outs):
                            for m in range(2):
                                for k in range(4):
                                    first, final = h + k == 0, h == 1 and k == 3
                                    if tok:
                                        ins = product(o[:, n * m:n * m + n], ui(4 * h + k, m), w[:, k, c0:c0 + n],
                                                        start=first and m == 0, stop=final, skip_group_check=True)
                                    else:
                                        ins = product(o[:, N * m:N * m + N], w[:, k, c0 + P * m:c0 + P * m + P],
                                                        u(4 * h + k), start=first and m == 0, stop=final,
                                                        skip_group_check=True)
                            if h == 1:
                                done(ins, job)
                        used(ins, name, h)

                mixed_tile("in0", [(("pin",), 0, BW, True), (("cb",), BW, BW, False)])
                mixed_tile("in1", [(("cc",), 0, BW, False), (("ch",), BW, BW, False)])
                tokens_out(both("in2"), [("mqk", i) for i in range(TC)], ui, COLS)
                mixed_tile("in3", [(("mv",), 0, BW, True), (("fq",), BW, BW, False)])
                mixed_tile("in4", [(("fk",), 0, BW, False), (("fv",), BW, BW, True)])
                o = start(("forget",))
                for h in range(2):
                    w = slab("forget", h)
                    for k in range(4):
                        ins = product(o[0:FH, 0:N], w[:, k, :], u(4 * h + k), start=(h + k == 0),
                                        stop=(h == 1 and k == 3))
                    if h == 1:
                        done(ins, ("forget",))
                    used(ins, "forget", h)
                copied(("pin",))
                for m in range(2):
                    o = start(("poolT", m))
                    for g in range(2):
                        for i in range(TC):
                            c = HD * (2 * m + g)
                            ins = product(o[HD * g:HD * g + HD, 0:N], pin[:, i, c:c + HD],
                                            poolm[:, i, 2 * m + g, :], start=(i == 0), stop=(i == TC - 1))
                    done(ins, ("poolT", m))
                pe.wait_ge(wpool_in, l * (16 * 4) + 16 * 4)
                copied(("poolT", 0))
                copied(("poolT", 1))
                o = start(("mixT",))
                for m in range(2):
                    ins = product(o[:, N * m:N * m + N], wpool[:, m, :], pooled[:, m, :], start=True, stop=True)
                done(ins, ("mixT",))
                pe.wait_ge(S["rotated"], sec.at("rotated", 2))
                for n, name in enumerate(("mqT", "mkT")):
                    o = start((name,))
                    for pr in range(2):
                        for tt in range(TC):
                            c = BW * n + P * pr
                            ins = turn(o[:, N * pr + P * tt:N * pr + P * tt + P], mqk[:, tt, c:c + P], P)
                    done(ins, (name,))

                def gate_tile(j):
                    features_out(both(f"gate{j}"), [("gate", j, 0), ("gate", j, 1)], u, N, 2)
                    n = j // 2
                    w = slab(f"branch{j}", 0)
                    if n == 1:
                        pe.wait_ge(S["conv_ready"], sec.at("conv_ready", 1))
                    for job in ([("mixT",)], [], [("PV", 1)], [("PV", 3)])[n]:
                        copied(job)
                    for i in range(2):
                        o = start(("prod", j, i))
                        for m in range(2):
                            for k in range(2):
                                c = P * (2 * i + m)
                                ins = product(o[:, N * m:N * m + N], w[:, k, c:c + P], yT[:, n, k, :],
                                                start=(k == 0), stop=(k == 1))
                        done(ins, ("prod", j, i))
                    used(ins, f"branch{j}", 0)

                for a in range(10):
                    if a < 8:
                        r, pr = HD * (a % 2), a // 2
                        if a == 0:
                            copied(("mqT",))
                            copied(("mkT",))
                        if a == 4:
                            pe.wait_ge(S["forget_ready"], sec.at("forget_ready", 1))
                        o = start(("S", a))
                        for i in range(TC):
                            c, n = P * i, P * (i + 1)
                            product(o[:, c:c + n], qT[r:r + HD, pr, P * i:P * i + P], kT[r:r + HD, pr, 0:n],
                                      start=(i == 0), stop=True, skip_group_check=True)
                            if a >= 4:
                                f = a - 4
                                product(o[:, c:c + n], forget[:, 4, P * i:P * i + P], selh[:, f, 0:n],
                                          start=False, stop=True, skip_group_check=True)
                                product(o[:, c:c + n], selh[:, f, 0:P], forget[:, 5, 0:n],
                                          start=False, stop=True, skip_group_check=True)
                            ins = product(o[:, c + n - P:c + n], ident, causal, start=False, stop=True,
                                            skip_group_check=True)
                        done(ins, ("S", a))
                    if a in GATES_BESIDE:
                        gate_tile(GATES_BESIDE.index(a))
                    if 1 <= a <= 8:
                        b = a - 1
                        pe.wait_ge(S["p_ready"], sec.at("p_ready", b + 1))
                        o = start(("PT", b))
                        for i in range(3):
                            ins = turn(o[:, P * i:P * i + P], prob[:, b % 2, P * i:P * i + P], P)
                        done(ins, ("PT", b))
                    if a >= 2:
                        b = a - 2
                        r = HD * (b % 2)
                        if b % 2 == 0:
                            pv = start(("PV", b // 2))
                        copied(("PT", b))
                        product(pv[r:r + HD, 0:N], vr[:, 0, b, :], probT[:, b % 2, 0:N],
                                  start=True, stop=True, skip_group_check=True)
                        ins = product(pv[r:r + HD, P:N], vr[:, 1, b, :], probT[:, b % 2, N:N + P],
                                        start=False, stop=True, skip_group_check=True)
                        if b % 2 == 1:
                            done(ins, ("PV", b // 2))
                    if a in MODS_BESIDE:
                        reduce_part(MODS_BESIDE.index(a))
                gate_tile(6)
                gate_tile(7)
                for h in range(2):
                    if h == 0:
                        pe.wait_ge(S["merged"], sec.at("merged", 12))
                    tokens_out(both(f"o{h}"), [("o", h, i) for i in range(TC)],
                               lambda k, i: merged[:, k, P * i:P * i + P], COLS)
                turn_xn("x2T", 2 * TC)
                reduce_part(3)
                for i in range(4):
                    copied(("x2T", i))
                for j in range(9):
                    if j < 8:
                        features_out(both(f"up{j}"), [("up", j, 0), ("up", j, 1)], u, N, 2)
                    if j == 8:
                        reduce_part(5)
                    if j == 1:
                        downs = {(i, h): start(("down", i, h)) for i in range(TC) for h in range(2)}
                    if j >= 1:
                        d = j - 1
                        pe.wait_ge(S["hdn_ready"], sec.at("hdn_ready", d + 1))
                        for s in range(2):
                            w = slab(f"down{d}", s)
                            for i in range(TC):
                                for h in range(2):
                                    for k in range(2):
                                        ins = product(downs[i, h][:, :], hdn[:, d % 2, 2 * s + k, P * i:P * i + P],
                                                        w[:, k, COLS * h:COLS * h + COLS],
                                                        start=(d + s + k == 0), stop=(d == 7 and s + k == 2))
                                    if d == 7 and s == 1:
                                        done(ins, ("down", i, h))
                            used(ins, f"down{d}", s)
                    if j == 6:
                        reduce_part(4)
                pay_owed(("mod", 5))

        @block.scalar
        def _(act):
            sec = Section()
            order = Order(act, S["act_order"])
            order.section(sec)

            def ready(job):
                b, n = sec.bank(job, 1)
                act.wait_ge(full[b], n)
                return bank[b]

            def release(ins, job):
                ins.then_inc(free[sec.bank(job, 0)[0]], 1)

            act.dma_start(kst[:, :], t["constants"]).then_inc(consts_in, 16)
            act.dma_start(kE[:, :], t["even_constants"]).then_inc(kE_in, 16)
            with nc.allow_non_contiguous_dma(reason="256 positions, one to a partition"):
                act.dma_start(posi[:, :], t["positions_2"].rearrange("o (t p) -> p (o t)", p=P)).then_inc(pos_in, 16)

            def copied(job):
                b, n = sec.bank(job, 1)
                act.wait_ge(free[b], n)

            copied(("vec",))
            act.activation(ctanh[:, :], vcol[:, 0:24], ACT.Tanh, scale=0.5).then_inc(S["ctanh_done"], 1)

            def modulate(name, dst, parts):
                for c in parts:
                    copied(("mod", c))
                for k in range(KD):
                    o = ready((name, k))
                    for v in range(2):
                        ins = act.activation(dst[:, k, N * v:N * v + N], o[:, N * v:N * v + N], ACT.Identity,
                                             bias=mcol[:, 0, v * KD + k:v * KD + k + 1],
                                             scale=mcol[:, 1, v * KD + k:v * KD + k + 1])
                    release(ins, (name, k))

            def tanh_tile(job, last_but_one, dst):
                o = ready(job)
                if last_but_one:
                    copied(last_but_one)
                act.activation(dst, o[:, :], ACT.Tanh, scale=0.5).then_inc(S["tanh_done"], 1)

            def gate_rows(c, dst, scale=1.0):
                _, streams, _ = sec.mods[c]
                for v in range(streams):
                    for h in range(2):
                        o = ready(("mod", c, v, h))
                        ins = act.activation(dst[v][:, COLS * h:COLS * h + COLS], o[:, :], ACT.Copy, scale=scale)
                        release(ins, ("mod", c, v, h))

            def copy_out(job, dst, src, scale=1.0):
                release(act.activation(dst, src, ACT.Copy, scale=scale), job)

            modulate("xT", hT_e, (0, 1))
            for m in range(4):
                o = ready(("fin", m))
                copy_out(("fin", m), fT[:, m, :], o[:, :])
            for m in range(4):
                tanh_tile(("fgate", m), ("fgate", m - 2) if m >= 2 else None, tanh_e[:, m % 2, :])
            for g in range(4):
                for h in range(2):
                    o = ready(("f1", g, h))
                    copy_out(("f1", g, h), dft1[:, g % 2, 2 * h:2 * h + 2, :],
                             o[:, :].rearrange("p (t n) -> p t n", t=2))
            for m in range(4):
                tanh_tile(("mgate", m), ("mgate", m - 2) if m >= 2 else ("fgate", m + 2), tanh_e[:, m % 2, :])
            gate_rows(2, grow_e)
            for name, n, col, at in (("qaT", 3, V_QN, 0), ("kvaT", 2, V_KN, 3)):
                for k in range(n):
                    o = ready((name, k))
                    copy_out((name, k), nT[:, at + k, :], o[:, :], scale=vcol[:, col + k:col + k + 1])
            copied(("mgate", 3))
            for h in range(2):
                for i in range(TC, TALL):
                    o = ready(("qb", h, i))
                    copy_out(("qb", h, i), qrow[:, i, 4 * h:4 * h + 4, :],
                             o[:, 0:4 * MHD].rearrange("p (h n) -> p h n", h=4))
            for i in range(TALL):
                for h in range(2):
                    o = ready(("kvb", i, h))[:, :].rearrange("p (h n) -> p h n", h=4)
                    act.activation(krow[:, i, 4 * h:4 * h + 4, 0:NOPE], o[:, :, 0:NOPE], ACT.Copy)
                    copy_out(("kvb", i, h), ev[:, i, NOPE * 4 * h:NOPE * 4 * (h + 1)].rearrange(
                        "p (h n) -> p h n", h=4), o[:, :, NOPE:2 * NOPE])
            for h in range(MH):
                o = ready(("qT", h))
                copy_out(("qT", h), qT_e[:, h, :], o[0:MHD, :], scale=MLA_SCALE)
            for h in range(MH + 2):
                if h < MH:
                    b = h % 2
                    for i in range(TALL):
                        act.wait_ge(S["max_ready"], 3 * h + min(i, 2) + 1)
                        job = ("S", h, min(i, 2))
                        o = ready(job)
                        c0, n = (COLS * i, COLS) if i < 2 else (2 * COLS + N * (i - 2), N)
                        src = o[:, 0:COLS] if i < 2 else o[:, N * (i - 2):N * (i - 1)]
                        ins = act.activation(prob_e[:, b, c0:c0 + n], src, ACT.Exp, bias=negmax[:, b, i:i + 1],
                                             accum_out=esum[:, b, i:i + 1])
                        if i != 2:
                            release(ins, job)
                if 1 <= h <= MH:
                    a = h - 1
                    for i in range(2):
                        o = ready(("PT", a, i))
                        copy_out(("PT", a, i), probT_e[:, a % 2, i, :], o[:, :])

            act.wait_ge(S["xn_ready"], TALL + 1)
            act.dma_start(sink[:, 0, :], t["o_sink"].partition_broadcast(P) if False else
                          t["o_sink"].broadcast_to([P, GH])).then_inc(sink_in, 16)
            gate_rows(5, [grow1])
            modulate("oxT", hT_o, (3, 4))
            act.dma_start(fing, t["final_g"].unsqueeze(0).broadcast_to([P, D])).then_inc(fing_in, 16)
            for i in range(TALL):
                o = ready(("okv", i))
                if i < TC:
                    act.activation(ov[:, i, :], o[:, GKV * HD:2 * GKV * HD], ACT.Copy).then_inc(S["okv_act"], 1)
                else:
                    act.activation(ov[:, i, :], o[:, GKV * HD:2 * GKV * HD], ACT.Copy)
                    k = o[:, 0:GKV * HD].rearrange("p (g n) -> p g n", g=GKV)
                    for dup in range(2):
                        ins = act.activation(okr[:, i, :, dup, :], k, ACT.Copy)
                    release(ins, ("okv", i))
            for m in range(4):
                tanh_tile(("og", m), ("og", m - 2) if m >= 2 else None, otanh[:, m % 2, :])
            for i in range(4):
                o = ready(("oqT", i))
                copy_out(("oqT", i), oqT[:, 2 * i:2 * i + 2, :], o[:, :].rearrange("p (a n) -> p a n", a=2), scale=HEAD_SCALE)
            for h in range(GH + 2):
                if h < GH:
                    b = h % 2
                    act.wait_ge(S["max_ready"], 3 * MH + h + 1)
                    for i in range(TC):
                        o = ready(("OS", h, i))
                        ins = act.activation(oprob[:, b, i, :], o[:, :], ACT.Exp, bias=negmax[:, b, i:i + 1],
                                             accum_out=esum[:, b, i:i + 1])
                        release(ins, ("OS", h, i))
                    act.activation(esink[:, b, :], negmax[:, b, 0:TC], ACT.Exp, bias=sink[:, 0, h:h + 1]
                                   ).then_inc(S["exp_done"], 1)
                if 1 <= h <= GH:
                    a = h - 1
                    o = ready(("OPT", a, 0))
                    copy_out(("OPT", a, 0), oprobT[:, a % 2, 0, :], o[:, :])

            act.wait_ge(S["x_out"], 1)
            act.dma_start(kH[:, :], t["hybrid_constants"]).then_inc(kH_in, 16)
            act.wait_ge(S["angles_ready"], 1)
            act.activation(rotary[:, 5, :], rotary[:, 2, :], ACT.Sin)
            act.activation(rotary[:, 4, :], rotary[:, 3, :], ACT.Sin).then_inc(S["rotary_ready"], 1)
            with act.Fori(0, LAYERS) as l:
                sec = Section(l)
                order.section(sec, ACT_LINKS)
                act.wait_ge(S["x_out"], sec.at("x_out", 0))

                def layer_row(w):
                    return w[bass.ds(l, 1)]

                def rows_of(w, c0, n):
                    return layer_row(w)[:, c0:c0 + n].rearrange("o (k p) -> (o k) p", p=P)

                act.dma_start(lrow[R_CB:R_FQ, :], rows_of(t["b_in_2"], BW, 3 * BW)).then_inc(lrow_in, 16)
                act.dma_start(lrow[R_FQ:R_GT, :], rows_of(t["b_in_2"], 7 * BW, 2 * BW)).then_inc(lrow_in, 16)
                act.dma_start(lrow[R_GT:R_UP, :], rows_of(t["b_in_2"], GATE0, 4 * D)).then_inc(lrow_in, 16)
                act.dma_start(lrow[R_UP:R_CW, :], rows_of(t["b_up_2"], 0, DFF)).then_inc(lrow_in, 16)
                act.dma_start(lrow[R_CW:R_PS, :], layer_row(t["conv_w_2"]).rearrange("o j (m p) -> (o j m) p", p=P)
                              ).then_inc(lrow_in, 16)
                act.dma_start(lrow[R_PS:R_N, :], rows_of(t["pool_scale_2"], 0, BW)).then_inc(lrow_in, 16)
                for b0, c0, n in ((0, 0, 1), (1, 4 * BW, 3), (4, 9 * BW, 1)):
                    act.dma_start(brow[:, b0:b0 + n, :], layer_row(t["b_in_2"])[:, c0:c0 + n * BW].broadcast_to(
                        [P, n * BW]).rearrange("p (b n) -> p b n", b=n)).then_inc(bias_in, 16)
                with nc.allow_non_contiguous_dma(reason="4 forget biases, one to a partition"):
                    act.dma_start(fbias[:, :], layer_row(t["b_in_2"])[:, FORGET0:FORGET0 + FH].rearrange(
                        "o (f u) -> (o f) u", u=1)).then_inc(bias_in, 16)
                act.wait_ge(wpool_zero, 1)
                for g in range(4):
                    r = HD * (g % 2)
                    act.dma_start(wpool[r:r + HD, g // 2, r:r + HD],
                                  layer_row(t["w_pool_2"])[:, g].rearrange("o c d -> (o c) d")).then_inc(wpool_in, 16)
                for i, name in enumerate(("ln1_g_2", "ln1_b_2")):
                    act.dma_start(lnrow[:, i, :], layer_row(t[name]).broadcast_to([P, D])).then_inc(ln_in, 16)

                def modulate_u(name, cols):
                    for i in range(4):
                        o = ready((name, i))
                        for j in range(2):
                            k = 2 * i + j
                            ins = act.activation(uT[:, k, :], o[:, N * j:N * j + N], ACT.Identity,
                                                 bias=cols[:, 0, k:k + 1], scale=cols[:, 1, k:k + 1])
                        release(ins, (name, i))

                modulate_u("xT", mcol)
                act.wait_ge(S["cols_ready"], sec.at("cols_ready", 1))

                def add_columns(job, dst, row):
                    o = ready(job)
                    for m in range(2):
                        ins = act.activation(dst[:, m, :], o[:, N * m:N * m + N], ACT.Identity,
                                             bias=lcol[:, row + m:row + m + 1])
                    release(ins, job)

                add_columns(("cb",), cb, R_CB)
                add_columns(("cc",), cc, R_CB + 2)
                add_columns(("ch",), chh, R_CB + 4)
                add_columns(("fk",), kT[:, 2:4, :], R_FQ + 2)
                act.wait_ge(bias_in, l * (16 * 4) + 16 * 4)
                o = ready(("forget",))
                act.activation(forget[:, 0, :], o[0:FH, 0:N], ACT.Identity, bias=fbias[:, 0:1])
                ins = act.activation(forget[:, 1, :], o[0:FH, 0:N], ACT.Abs, bias=fbias[:, 0:1])
                release(ins, ("forget",))
                copied(("forget",))
                order.link(act.activation(forget[:, 2, :], forget[:, 1, :], ACT.Exp, scale=-1.0))
                act.activation(forget[:, 3, :], forget[:, 2, :], ACT.Ln, bias=1.0).then_inc(S["forget_act"], 1)
                for m in range(2):
                    o = ready(("poolT", m))
                    copy_out(("poolT", m), pooled[:, m, :], o[:, 0:N])
                o = ready(("mkT",))
                copy_out(("mkT",), kT[:, 0:2, :], o[:, :].rearrange("p (a n) -> p a n", a=2))

                def gate_tanh(j):
                    for i in range(2):
                        o = ready(("gate", j, i))
                        if j > 0:
                            copied(("prod", j - 1, i))
                        for m in range(2):
                            c = 4 * j + 2 * i + m
                            ins = act.activation(tanhg[:, i, N * m:N * m + N], o[:, N * m:N * m + N], ACT.Tanh,
                                                 bias=hcol[:, c:c + 1], scale=0.5)
                        release(ins, ("gate", j, i))

                for a in range(10):
                    if a < 8:
                        b = a % 2
                        o = ready(("S", a))
                        act.wait_ge(S["max_ready"], sec.at("max_ready", a + 1))
                        for i in range(TC):
                            c, n = P * i, P * (i + 1)
                            ins = act.activation(prob[:, b, c:c + n], o[:, c:c + n], ACT.Exp,
                                                 bias=negmax[:, b, i:i + 1], accum_out=esum[:, b, i:i + 1])
                        release(ins, ("S", a))
                    if a in GATES_BESIDE:
                        gate_tanh(GATES_BESIDE.index(a))
                    if 1 <= a <= 8:
                        o = ready(("PT", a - 1))
                        copy_out(("PT", a - 1), probT[:, (a - 1) % 2, :], o[:, 0:3 * P])
                    if a == MODS_BESIDE[0]:
                        gate_rows(0, [grow1], scale=0.5)
                gate_tanh(6)
                gate_tanh(7)
                act.wait_ge(S["norm1"], sec.at("norm1", 1))
                for i, name in enumerate(("ln2_g_2", "ln2_b_2")):
                    act.dma_start(lnrow[:, i, :], layer_row(t[name]).broadcast_to([P, D])).then_inc(ln_in, 16)
                copied(("mod", 1))
                copied(("mod", 2))
                modulate_u("x2T", mcol2)
                gate_rows(3, [grow1])
                for j in range(8):
                    for i in range(2):
                        o = ready(("up", j, i))
                        for m in range(2):
                            c = R_UP + 4 * j + 2 * i + m
                            ins = act.activation(hdn[:, j % 2, 2 * i + m, :], o[:, N * m:N * m + N], ACT.Relu,
                                                 bias=lcol[:, c:c + 1])
                        release(ins, ("up", j, i))
                order.end_layer()

        @block.vector
        def _(dve):
            sec = Section()
            order = Order(dve, S["dve_order"])
            order.section(sec)
            link = order.link

            def ready(job):
                b, n = sec.bank(job, 1)
                dve.wait_ge(full[b], n)
                return bank[b]

            def release(ins, job):
                ins.then_inc(free[sec.bank(job, 0)[0]], 1)

            def copied(job):
                b, n = sec.bank(job, 1)
                dve.wait_ge(free[b], n)

            def gemv(c, q):
                b = c % 2
                _, streams, _ = sec.mods[c]
                slot, before = sec.chunk(c, q)
                dve.wait_ge(m_full[slot], before * 16 + 16)
                if q == 0:
                    dve.wait_ge(acc_init[b], sec.part(c, 0) * 16 + 16)
                first_block = sec.layer is None and c < 6
                w = mring[:, slot, :].rearrange("p (k n) -> p k n", k=4)
                for k in range(4):
                    for v in range(streams):
                        a = acc[:, b, v, COLS * (q // 2):COLS * (q // 2) + COLS]
                        col = (V_C + 8 * v if first_block else V_C2) + 4 * (q % 2) + k
                        ins = dve.scalar_tensor_tensor(out=a, in0=w[:, k, :], scalar=ccol[:, col:col + 1], in1=a,
                                                       op0=ALU.mult, op1=ALU.add)
                        if k == 3 and v == streams - 1:
                            ins.then_inc(m_free[slot], 1)
                            dve.wait_ge(m_free[slot], before + 1)
                        elif v == streams - 1:
                            link(ins)

            def rsqrt(n, mean_square, scale=1.0, eps=RMS_EPS):
                v, y, s, _ = (nwt[:, i, 0:n] for i in range(4))
                if mean_square:
                    link(dve.tensor_tensor(v, mv[:, 0:n, 0], mv[:, 0:n, 0], ALU.mult))
                    link(dve.scalar_tensor_tensor(out=v, in0=mv[:, 0:n, 1], scalar=eps, in1=v,
                                                  op0=ALU.add, op1=ALU.add))
                else:
                    link(dve.tensor_scalar(v, mv[:, 0:n, 1], eps, None, ALU.add))
                link(dve.tensor_scalar(nwi[:, 0, 0:n], v.bitcast(I32), 1, None, ALU.logical_shift_right))
                link(dve.tensor_scalar(nwi[:, 1, 0:n], nwi[:, 0, 0:n], -1.0, float(RSQRT_BITS), ALU.mult, ALU.add))
                g = nwi[:, 1, 0:n].bitcast(F32)
                for _ in range(3):
                    link(dve.tensor_tensor(s, g, g, ALU.mult))
                    link(dve.scalar_tensor_tensor(out=s, in0=s, scalar=-0.5, in1=v, op0=ALU.mult, op1=ALU.mult))
                    link(dve.scalar_tensor_tensor(out=y, in0=s, scalar=1.5, in1=g, op0=ALU.add, op1=ALU.mult))
                    g = y
                return y

            def statistics(i, parts):
                for j, p in enumerate(parts):
                    ins = dve.bn_stats(stat[:, i, 6 * j:6 * j + 6], p)
                link(ins)
                if sec.layer is not None:
                    dve.memset(idle[:, 8 + i:9 + i], 0.0)
                return dve.bn_aggr(mv[:, i, :], stat[:, i, 0:6 * len(parts)])

            def norm_x(dst, chunks, mean_square, eps):
                for i in range(chunks):
                    ins = statistics(i, [x[:, i, 0:COLS], x[:, i, COLS:D]])
                link(ins)
                y = rsqrt(chunks, mean_square, eps=eps)
                for i in range(chunks):
                    if mean_square:
                        ins = dve.tensor_scalar(dst[:, i, :], x[:, i, :], y[:, i:i + 1], None, ALU.mult)
                    else:
                        ins = dve.tensor_scalar(dst[:, i, :], x[:, i, :], mv[:, i, 0:1], y[:, i:i + 1],
                                                ALU.subtract, ALU.mult)
                    ins.then_inc(S["xn_ready"], 1)

            def mod_columns(c, dst, scale, gains=None):
                _, streams, _ = sec.mods[c]
                o = ready(("mod", c))
                for v in range(streams):
                    src, d = o[:, KD * v:KD * v + KD], dst[:, scale, KD * v:KD * v + KD]
                    if not scale:
                        ins = dve.tensor_copy(d, src)
                    elif gains is None:
                        ins = dve.tensor_scalar(d, src, 1.0, None, ALU.add)
                    else:
                        ins = dve.scalar_tensor_tensor(out=d, in0=src, scalar=1.0, in1=gains, op0=ALU.add,
                                                       op1=ALU.mult)
                release(ins, ("mod", c))

            def rotate(dst, src, cos, sin, heads, half, products, job=None):
                def over(table):
                    return table.unsqueeze(1).broadcast_to([P, heads, half])
                pc, ps = products
                for i in range(2):
                    dve.tensor_tensor(pc[:, :, i, :], src[:, :, i, :], over(cos), ALU.mult)
                    ins = dve.tensor_tensor(ps[:, :, i, :], src[:, :, i, :], over(sin), ALU.mult)
                if job:
                    release(ins, job)
                    copied(job)
                else:
                    link(ins)
                dve.tensor_tensor(dst[:, :, 0, :], pc[:, :, 0, :], ps[:, :, 1, :], ALU.subtract)
                return dve.tensor_tensor(dst[:, :, 1, :], pc[:, :, 1, :], ps[:, :, 0, :], ALU.add)

            def gated_tile(job, n, dst, src):
                o = ready(job)
                dve.wait_ge(S["tanh_done"], n + 1)
                ins = dve.scalar_tensor_tensor(out=dst, in0=src, scalar=1.0, in1=o[:, :], op0=ALU.add, op1=ALU.mult)
                release(ins, job)

            def maxima(src, h, i, signal=None):
                return dve.tensor_reduce(negmax[:, h % 2, i:i + 1], src, AX_X, ALU.max, negate=True)

            def normalise(blocks, h):
                for i, p in enumerate(blocks):
                    ins = dve.tensor_scalar(p, p, rsum[:, h % 2, i:i + 1], None, ALU.mult)
                ins.then_inc(S["p_ready"], 1)

            def add_output(h, i, job, gate, tmp, n):
                o = ready(job)
                cols = slice(COLS * h, COLS * h + COLS)
                ins = dve.tensor_tensor(tmp, o[:, :], gate[:, cols], ALU.mult)
                release(ins, job)
                copied(job)
                return dve.tensor_tensor(x[:, i, cols], x[:, i, cols], tmp, ALU.add)

            dve.wait_ge(consts_in, 16)
            o = ready(("vec",))
            ins = dve.tensor_copy(vcol[:, :], o[:, 0:V_N])
            release(ins, ("vec",))
            dve.wait_ge(S["ctanh_done"], 1)
            link(dve.scalar_tensor_tensor(out=ccol[:, :], in0=ctanh[:, :], scalar=1.0, in1=vcol[:, 0:24],
                                          op0=ALU.add, op1=ALU.mult))
            link(dve.tensor_scalar(ccol[:, :], ccol[:, :], 0.5, None, ALU.mult))
            for q in range(4):
                gemv(0, q)
            dve.wait_ge(x_in, 32)
            norm_x(xn_e, TALL, True, RMS_EPS)
            for q in range(4):
                gemv(1, q)
            mod_columns(0, mcol, 0)
            mod_columns(1, mcol, 1, vcol[:, V_NG:V_NG + KD])
            for q in range(2):
                gemv(2, q)

            for m in range(4):
                gated_tile(("fgate", m), m, eyT[:, m, :], tanh_e[:, m % 2, :])
            for q in range(2, 4):
                gemv(2, q)
            for job, dst, width in (("qa", qn, QR), ("kva", kvn, KVR)):
                for i in range(TALL):
                    ins = statistics(i, [ready((job, i))[:, 0:width]])
                link(ins)
                y = rsqrt(TALL, True)
                for i in range(TALL):
                    o = bank[sec.bank((job, i), 0)[0]]
                    if job == "kva":
                        dve.tensor_copy(kpe[:, i, 0, :], o[:, KVR:KVR + ROPE])
                    ins = dve.tensor_scalar(dst[:, i, :], o[:, 0:width], y[:, i:i + 1], None, ALU.mult)
                    release(ins, (job, i))
                if job == "qa":
                    gemv(3, 0)
                    gemv(3, 1)
            for g in range(4):
                o = ready(("f2", g))
                ins = dve.scalar_tensor_tensor(out=eyT[:, g, :], in0=o[:, :], scalar=0.5, in1=eyT[:, g, :],
                                               op0=ALU.mult, op1=ALU.mult)
                release(ins, ("f2", g))
            for m in range(4):
                gated_tile(("mgate", m), 4 + m, eyT[:, 4 + m, :], tanh_e[:, m % 2, :])
            for q in range(2, 4):
                gemv(3, q)
            cos16, sin16 = rope_t[:, :, 0:16], rope_t[:, :, 16:32]
            for i in range(TC):
                src = kpe[:, i, 0, :].rearrange("p (h s n) -> p h s n", h=1, s=2)
                ps = [kpe[:, i, 1 + s, :].rearrange("p (h s n) -> p h s n", h=1, s=2) for s in range(2)]
                link(rotate(src, src, cos16[:, i, :], sin16[:, i, :], 1, 16, ps))
            for h in range(2):
                for i in range(TC):
                    o = ready(("qb", h, i))[:, 0:4 * MHD].rearrange("p (h n) -> p h n", h=4)
                    dst = qrow[:, i, 4 * h:4 * h + 4, :]
                    dve.tensor_copy(dst[:, :, 0:NOPE], o[:, :, 0:NOPE])
                    ps = [qrot[:, s, :].rearrange("p (h s n) -> p h s n", h=4, s=2) for s in range(2)]
                    ins = rotate(dst[:, :, NOPE:MHD].rearrange("p h (s n) -> p h s n", s=2),
                                 o[:, :, NOPE:MHD].rearrange("p h (s n) -> p h s n", s=2),
                                 cos16[:, i, :], sin16[:, i, :], 4, 16, ps, job=("qb", h, i))
                    ins.then_inc(S["q_lat"], 1)
                    dve.wait_ge(S["q_lat"], 2 * h + i + 1)
            for i in range(TALL):
                ins = dve.tensor_copy(krow[:, i, :, NOPE:MHD], kpe[:, i, 0, :].unsqueeze(1).broadcast_to(
                    [P, MH, ROPE]))
            ins.then_inc(S["kpe_ready"], 1)
            for h in range(MH):
                o = ready(("kT", h))
                ins = dve.tensor_copy(kT_e[:, h, :], o[0:MHD, :])
                release(ins, ("kT", h))
            for h in range(MH + 2):
                if h < MH:
                    b = h % 2
                    for i in range(TC):
                        maxima(ready(("S", h, i))[:, :], h, i).then_inc(S["max_ready"], 1)
                    dve.tensor_reduce(negmax[:, b, 2:4], ready(("S", h, 2))[:, :].rearrange("p (i n) -> p i n", i=2),
                                      AX_X, ALU.max, negate=True).then_inc(S["max_ready"], 1)
                    if h < 4:
                        gemv(4, h)
                    else:
                        gemv(5, h - 4)
                    copied(("S", h, 2))
                    link(dve.reciprocal(rsum[:, b, :], esum[:, b, :]))
                    normalise([prob_e[:, b, 0:COLS], prob_e[:, b, COLS:2 * COLS],
                               prob_e[:, b, 2 * COLS:2 * COLS + N], prob_e[:, b, 2 * COLS + N:3 * COLS]], h)
                if 1 <= h <= MH:
                    a = h - 1
                    o = ready(("PT", a, 2))
                    ins = dve.tensor_copy(probT_e[:, a % 2, 2, :], o[:, :])
                    release(ins, ("PT", a, 2))
                if h in (1, 5):
                    mod_columns(3 + h // 4, mcol, h // 4, vcol[:, V_NG + KD:V_NG + 2 * KD])
                if h >= 3 and h % 2 == 1:
                    g = (h - 3) // 2
                    o = ready(("PV", g))
                    ins = dve.scalar_tensor_tensor(out=eyT[:, 4 + g, :], in0=o[:, :], scalar=0.5,
                                                   in1=eyT[:, 4 + g, :], op0=ALU.mult, op1=ALU.mult)
                    release(ins, ("PV", g))
            for v in range(2):
                copied(("mod", 2, v, 1))
            for h in range(2):
                for i in range(TALL):
                    last = add_output(h, i, ("eout", h, i), grow_e[i // TC], etmp[:, i % 2, :], i)
            link(last)

            norm_x(xn_o, TALL, True, RMS_EPS)
            cos32, sin32 = rope_t[:, :, 32:64], rope_t[:, :, 64:96]
            dve.wait_ge(sink_in, 16)
            link(dve.tensor_scalar(sink[:, 1, :], sink[:, 0, :], -1.0, None, ALU.mult))
            rot = [orot[:, s, :, :].rearrange("p h n -> p (h n)")[:, 0:8 * HD].rearrange(
                "p (h s n) -> p h s n", h=8, s=2) for s in range(2)]
            rotk = [r[:, 0:GKV] for r in rot]
            for h in range(2):
                for i in range(TC):
                    o = ready(("oq", h, i))[:, :].rearrange("p (h s n) -> p h s n", h=8, s=2)
                    ins = rotate(oq[:, i, COLS * h:COLS * h + COLS].rearrange("p (h s n) -> p h s n", h=8, s=2), o,
                                 cos32[:, i, :], sin32[:, i, :], 8, HD // 2, rot, job=("oq", h, i))
                    ins.then_inc(S["q_lat"], 1)
                    dve.wait_ge(S["q_lat"], 4 + 2 * h + i + 1)
            for i in range(TC):
                o = ready(("okv", i))[:, 0:GKV * HD].rearrange("p (h s n) -> p h s n", h=GKV, s=2)
                dve.wait_ge(S["okv_act"], i + 1)
                ins = rotate(okr[:, i, :, 0, :].rearrange("p g (s n) -> p g s n", s=2), o,
                             cos32[:, i, :], sin32[:, i, :], GKV, HD // 2, rotk, job=("okv", i))
                link(ins)
                dve.tensor_copy(okr[:, i, :, 1, :], okr[:, i, :, 0, :]).then_inc(S["kpe_ready"], 1)
            for m in range(4):
                gated_tile(("og", m), 8 + m, oyT[:, 2 * m:2 * m + 2, :].rearrange("p a n -> p (a n)"),
                           otanh[:, m % 2, :])
            for g in range(GKV):
                o = ready(("okT", g))
                ins = dve.tensor_copy(okT[:, g, :], o[:, :])
                release(ins, ("okT", g))
            for h in range(GH + 2):
                if h < GH:
                    b = h % 2
                    for i in range(TC):
                        ins = maxima(ready(("OS", h, i))[:, :], h, i)
                    link(ins)
                    dve.tensor_scalar(negmax[:, b, 0:TC], negmax[:, b, 0:TC], sink[:, 1, h:h + 1], None, ALU.min
                                      ).then_inc(S["max_ready"], 1)
                    if h < 8:
                        gemv(6 + h // 4, h % 4)
                    dve.wait_ge(S["exp_done"], h + 1)
                    link(dve.tensor_tensor(esum[:, b, 0:TC], esum[:, b, 0:TC], esink[:, b, :], ALU.add))
                    link(dve.reciprocal(rsum[:, b, 0:TC], esum[:, b, 0:TC]))
                    normalise([oprob[:, b, 0, :], oprob[:, b, 1, :]], h)
                if 1 <= h <= GH:
                    a = h - 1
                    o = ready(("OPT", a, 1))
                    ins = dve.tensor_copy(oprobT[:, a % 2, 1, :], o[:, :])
                    release(ins, ("OPT", a, 1))
                if h >= 3 and h % 2 == 1:
                    g = (h - 3) // 2
                    o = ready(("OPV", g))
                    ins = dve.scalar_tensor_tensor(out=oyT[:, g, :], in0=o[:, 0:N], scalar=0.5,
                                                   in1=oyT[:, g, :], op0=ALU.mult, op1=ALU.mult)
                    release(ins, ("OPV", g))
                if h == 7:
                    mod_columns(6, mcol, 0)
            copied(("mod", 5, 0, 1))
            for h in range(2):
                for i in range(TC):
                    last = add_output(h, i, ("oout", h, i), grow1, otmp[:, i % 2, :], i)
            link(last)
            mod_columns(7, mcol, 1)
            for i in range(TC):
                ins = statistics(i, [x[:, i, 0:COLS], x[:, i, COLS:D]])
            link(ins)
            y = rsqrt(TC, True)
            dve.wait_ge(fing_in, 16)
            for i in range(TC):
                ins = dve.scalar_tensor_tensor(out=x[:, i, :], in0=x[:, i, :], scalar=y[:, i:i + 1], in1=fing,
                                               op0=ALU.mult, op1=ALU.mult)
            ins.then_inc(S["x_out"], 1)
            dve.memset(wpool[:, :, :], 0.0).then_inc(wpool_zero, 1)
            link(dve.memset(conv[:, :, :], 0.0))

            dve.wait_ge(pos_in, 16)
            link(dve.tensor_copy(posf[:, :], posi[:, :]))
            for i in range(TC):
                ins = dve.tensor_scalar(rotary[:, 0, 8 * i:8 * i + 8], kst[:, K_INV:K_INV + 8], posf[:, i:i + 1],
                                        None, ALU.mult)
            link(ins)
            link(dve.tensor_scalar(rotary[:, 1, :], rotary[:, 0, :], 1.0 / (2.0 * 3.141592653589793), ROUND,
                                   ALU.mult, ALU.add))
            link(dve.tensor_scalar(rotary[:, 1, :], rotary[:, 1, :], ROUND, None, ALU.subtract))
            for part in (TWO_PI_1, TWO_PI_2, TWO_PI_3):
                src = 0 if part == TWO_PI_1 else 2
                link(dve.scalar_tensor_tensor(out=rotary[:, 2, :], in0=rotary[:, 1, :], scalar=-part,
                                              in1=rotary[:, src, :], op0=ALU.mult, op1=ALU.add))
            link(dve.tensor_scalar(rotary[:, 2, :], rotary[:, 2, :], 3.1415925, -3.1415925, ALU.min, ALU.max))
            link(dve.tensor_scalar(rotary[:, 3, :], rotary[:, 2, :], -1.0, None, ALU.mult))
            link(dve.tensor_tensor(rotary[:, 3, :], rotary[:, 3, :], rotary[:, 2, :], ALU.max))
            dve.tensor_scalar(rotary[:, 3, :], rotary[:, 3, :], -1.0, 1.5707963267948966, ALU.mult, ALU.add
                              ).then_inc(S["angles_ready"], 1)
            dve.wait_ge(S["rotary_ready"], 1)
            cos8 = rotary[:, 4, :].rearrange("p (t n) -> p t n", t=TC)
            sin8 = rotary[:, 5, :].rearrange("p (t n) -> p t n", t=TC)

            with dve.Fori(0, LAYERS) as l:
                sec = Section(l)
                order.section(sec, DVE_LINKS)
                norm_x(xn, TC, False, LN_EPS)
                o = ready(("cols",))
                ins = dve.tensor_copy(lcol[:, :], o[:, 0:R_N])
                release(ins, ("cols",))
                copied(("cols",))
                dve.tensor_scalar(hcol[:, :], lcol[:, R_GT:R_UP], 0.5, None, ALU.mult).then_inc(S["cols_ready"], 1)
                dve.wait_ge(bias_in, l * (16 * 4) + 16 * 4)

                def add_rows(job, dst, b0, nt, n):
                    o = ready(job)
                    ins = dve.tensor_tensor(dst, o[:, 0:nt * n].rearrange("p (t n) -> p t n", t=nt),
                                            brow[:, b0:b0 + n // BW, :].rearrange("p b n -> p (b n)").unsqueeze(1)
                                            .broadcast_to([P, nt, n]), ALU.add)
                    release(ins, job)

                add_rows(("pin",), pin, 0, TC, BW)
                copied(("ch",))
                link(dve.tensor_tensor(conv[:, :, 2:N + 2], cc[:, :, :], chh[:, :, :], ALU.mult))
                for j in range(3):
                    for m in range(2):
                        w = lcol[:, R_CW + 2 * j + m:R_CW + 2 * j + m + 1]
                        if j == 0:
                            ins = dve.tensor_scalar(cc[:, m, :], conv[:, m, 0:N], w, None, ALU.mult)
                        else:
                            ins = dve.scalar_tensor_tensor(out=cc[:, m, :], in0=conv[:, m, j:N + j], scalar=w,
                                                           in1=cc[:, m, :], op0=ALU.mult, op1=ALU.add)
                    link(ins)
                dve.tensor_tensor(yT[:, 1, :, :], cb, cc[:, :, :], ALU.mult).then_inc(S["conv_ready"], 1)
                gemv(0, 0)
                for i in range(TC):
                    add_rows(("mqk", i), mqk[:, i:i + 1, :], 1, 1, COLS)
                    copied(("mqk", i))
                    part = mqk[:, i, :].rearrange("p (h n) -> p h n", h=8)[:, :, 0:16].rearrange(
                        "p h (s n) -> p h s n", s=2)
                    prods = [rtmp[:, s, :, :].rearrange("p h (s n) -> p h s n", s=2) for s in range(2)]
                    ins = rotate(part, part, cos8[:, i, :], sin8[:, i, :], 8, 8, prods)
                    ins.then_inc(S["rotated"], 1)
                    dve.wait_ge(S["rotated"], sec.at("rotated", i + 1))
                gemv(0, 1)
                add_rows(("mv",), vr[:, :, 0:4, :].rearrange("p t h n -> p t (h n)"), 3, TC, BW)
                o = ready(("fq",))
                for m in range(2):
                    ins = dve.tensor_scalar(qT[:, 2 + m, :], o[:, N * m:N * m + N],
                                            lcol[:, R_FQ + m:R_FQ + m + 1], HEAD_SCALE, ALU.add, ALU.mult)
                release(ins, ("fq",))
                gemv(0, 2)
                add_rows(("fv",), vr[:, :, 4:8, :].rearrange("p t h n -> p t (h n)"), 4, TC, BW)
                gemv(0, 3)
                dve.wait_ge(S["forget_act"], sec.at("forget_act", 1))
                link(dve.scalar_tensor_tensor(out=forget[:, 0, :], in0=forget[:, 0, :], scalar=0.0,
                                              in1=forget[:, 3, :], op0=ALU.min, op1=ALU.subtract))
                link(dve.memset(forget[:, 1, :], 1.0))
                link(dve.tensor_tensor_scan(forget[:, 4, :], forget[:, 1, :], forget[:, 0, :], 0.0,
                                            ALU.mult, ALU.add))
                dve.tensor_scalar(forget[:, 5, :], forget[:, 4, :], -1.0, None, ALU.mult
                                  ).then_inc(S["forget_ready"], 1)
                o = ready(("mixT",))
                for m in range(2):
                    ins = dve.tensor_scalar(yT[:, 0, m, :], o[:, N * m:N * m + N],
                                            lcol[:, R_PS + m:R_PS + m + 1], None, ALU.mult)
                release(ins, ("mixT",))
                o = ready(("mqT",))
                ins = dve.tensor_scalar(qT[:, 0:2, :], o[:, :].rearrange("p (a n) -> p a n", a=2), HEAD_SCALE, None,
                                        ALU.mult)
                release(ins, ("mqT",))

                def gate_products(j):
                    for i in range(2):
                        n = 2 * j + i
                        o = ready(("prod", j, i))
                        copied(("gate", j, i))
                        m = 4 * (j % 2) + 2 * i
                        if j < 2:
                            dst = merged[:, m:m + 2, :].rearrange("p m n -> p (m n)")
                        else:
                            dst = term[:, i, :]
                            if j > 2:
                                dve.wait_ge(S["merged"], sec.at("merged", n - 5))
                        ins = dve.scalar_tensor_tensor(out=dst, in0=tanhg[:, i, :], scalar=1.0, in1=o[:, :],
                                                       op0=ALU.add, op1=ALU.mult)
                        release(ins, ("prod", j, i))

                chunk = 0
                for a in range(10):
                    if a < 8:
                        b = a % 2
                        o = ready(("S", a))
                        maxima(o[:, 0:P], a, 0)
                        maxima(o[:, P:3 * P], a, 1).then_inc(S["max_ready"], 1)
                    if a < 8:
                        for _ in range(2 - a % 2):
                            gemv(1 + chunk // 4, chunk % 4)
                            chunk += 1
                        copied(("S", a))
                        link(dve.reciprocal(rsum[:, b, 0:TC], esum[:, b, 0:TC]))
                        normalise([prob[:, b, 0:P], prob[:, b, P:3 * P]], a)
                    if a in GATES_BESIDE:
                        gate_products(GATES_BESIDE.index(a))
                    if a >= 3 and a % 2 == 1:
                        g = (a - 3) // 2
                        o = ready(("PV", g))
                        ins = dve.tensor_copy(yT[:, 2 + g // 2, g % 2, :], o[:, 0:N])
                        release(ins, ("PV", g))
                    if a in MODS_BESIDE[1:]:
                        mod_columns(MODS_BESIDE.index(a), mcol2, MODS_BESIDE.index(a) - 1)
                gate_products(6)
                gate_products(7)

                def residual(jobs, rows_in, signal):
                    for h in range(2):
                        for i in range(TC):
                            o = ready((jobs, h, i) if jobs == "o" else (jobs, i, h))
                            cols = slice(COLS * h, COLS * h + COLS)
                            ins = dve.tensor_tensor(xn[:, i, cols], o[:, :], grow1[:, cols], ALU.mult)
                            release(ins, (jobs, h, i) if jobs == "o" else (jobs, i, h))
                            copied((jobs, h, i) if jobs == "o" else (jobs, i, h))
                            ins = dve.scalar_tensor_tensor(out=x[:, i, cols], in0=x[:, i, cols], scalar=ALPHA,
                                                           in1=xn[:, i, cols], op0=ALU.mult, op1=ALU.add)
                    link(ins)
                    for i in range(TC):
                        ins = statistics(i, [x[:, i, 0:COLS], x[:, i, COLS:D]])
                    link(ins)
                    y = rsqrt(TC, False, eps=LN_EPS)
                    for i in range(TC):
                        ins = dve.tensor_scalar(x[:, i, :], x[:, i, :], mv[:, i, 0:1], y[:, i:i + 1],
                                                ALU.subtract, ALU.mult)
                    link(ins)
                    dve.wait_ge(ln_in, rows_in)
                    for i in range(TC):
                        ins = dve.tensor_tensor(x[:, i, :], x[:, i, :], lnrow[:, 0, :], ALU.mult)
                    link(ins)
                    for i in range(TC):
                        ins = dve.tensor_tensor(x[:, i, :], x[:, i, :], lnrow[:, 1, :], ALU.add)
                    ins.then_inc(S[signal], 1)
                    dve.wait_ge(S[signal], sec.at(signal, 1))

                copied(("mod", 0, 0, 1))
                residual("o", l * 64 + 32, "norm1")
                norm_x(xn, TC, False, LN_EPS)
                for j in range(8):
                    gemv(4 + j // 4, j % 4)
                    copied(("up", j, 1))
                    hid = hdn[:, j % 2, :, :]
                    dve.tensor_tensor(hid, hid, hid, ALU.mult).then_inc(S["hdn_ready"], 1)
                    if j == 6:
                        mod_columns(4, mcol, 0)
                mod_columns(5, mcol, 1)
                copied(("mod", 3, 0, 1))
                residual("down", l * 64 + 64, "x_out")
                order.end_layer()


def tables():
    import numpy as np

    def angles(width):
        rows = N // 64
        row = np.repeat(np.arange(rows, dtype=np.float32), 64)
        col = np.tile(np.arange(64, dtype=np.float32), rows)
        nf = width // 4
        inv = np.float32(10000.0) ** (-np.arange(nf, dtype=np.float32) / np.float32(nf))
        ang = np.concatenate([row[:, None] * inv, col[:, None] * inv], axis=-1).astype(np.float32)
        return np.cos(ang).astype(np.float32), np.sin(ang).astype(np.float32)

    def chunks(a):
        return np.concatenate([a[0:P], a[P:2 * P]], axis=1)

    k = np.zeros((P, K_N), np.float32)
    k[:, K_ID:K_ID + P] = np.eye(P)
    k[:, K_ONE:K_ONE + P] = 1.0
    q, j = np.arange(P)[:, None], np.arange(P)[None, :]
    k[:, K_CAUSAL:K_CAUSAL + P] = np.where(j <= q, 0.0, NEG)
    k[:, K_WIN:K_WIN + P] = np.where(j >= q, 0.0, NEG)
    k[:, K_ROPE:K_INV] = chunks(np.concatenate([*angles(ROPE), *angles(HD)], axis=1))
    k[:, K_INV:K_N] = np.float32(500000.0) ** (-np.arange(0, 16, 2, dtype=np.float32) / np.float32(16))

    e = np.zeros((P, KE_N), np.float32)
    norm = 1.0 / np.sqrt(N * P)
    ang = 2 * np.pi * ((np.arange(P)[:, None] * np.arange(P)[None, :]) % P) / P
    e[:, KE_CH:KE_SEQ] = np.concatenate([np.cos(ang), np.sin(ang)], axis=1) * norm
    ang = 2 * np.pi * ((np.arange(N)[:, None] * np.arange(N)[None, :]) % N) / N
    e[:, KE_SEQ:] = chunks(np.concatenate([np.cos(ang), -np.sin(ang)], axis=1))

    h = np.zeros((P, KH_N), np.float32)
    tok, src = np.arange(N)[None, :], np.arange(N)[:, None]
    pools = [np.where((src <= tok) & (src > tok - w), 1.0 / np.minimum(tok + 1, w), 0.0) - (src == tok)
             for w in POOLW]
    h[:, KH_POOL:KH_SEL] = chunks(np.concatenate(pools, axis=1))
    for f in range(FH):
        h[f, KH_SEL + N * f:KH_SEL + N * f + N] = 1.0
    return {"constants": k, "even_constants": e, "hybrid_constants": h}


_INS = ["x", "c", "ctx", "c_ctx", "w_mod", "b_mod", "norm_g", "e_w_in", "e_q_norm", "e_w_qb", "e_kv_norm",
        "e_w_kvb", "e_w_out", "o_w_in", "o_sink", "o_w_out", "final_g", "c_2", "positions_2", "w_ada_2",
        "b_ada_2", "w_in_2", "b_in_2", "w_pool_2", "pool_scale_2", "conv_w_2", "w_branch_2", "w_o_2",
        "ln1_g_2", "ln1_b_2", "w_up_2", "b_up_2", "w_down_2", "ln2_g_2", "ln2_b_2"]


def kernel(**inputs):
    import numpy as _np
    import concourse.bacc as _bacc
    from concourse import mybir as _mybir
    from concourse.bass_utils import run_bass_kernel_spmd as _run

    nc = _bacc.Bacc("TRN2", target_bir_lowering=False, num_devices=1)
    arrays, args = {}, {}
    for name, a in [(n, inputs[n]) for n in _INS] + list(tables().items()):
        a = _np.ascontiguousarray(a)
        arrays[f"in_{name}_dram"] = a
        args[name] = nc.dram_tensor(f"in_{name}_dram", a.shape, _mybir.dt.from_np(a.dtype), kind="ExternalInput").ap()
    out = nc.dram_tensor("out_0_dram", (1, N, D), F32, kind="ExternalOutput").ap()
    program(nc, args, out)
    r = _run(nc, [arrays], core_ids=[0])
    return r.results[0]["out_0_dram"]
```

```python
from contextlib import ExitStack

import concourse.bass as bass
from concourse import mybir

F32 = mybir.dt.float32
F32R = mybir.dt.float32r
I32 = mybir.dt.int32
ALU = mybir.AluOpType
ACT = mybir.ActivationFunctionType
AX_X = mybir.AxisListType.X

P = 128
D = 1024
KD = D // P
N = 256
TC = N // P
TALL = 2 * TC
COLS = 512
FW, QR, KVR, ROPE = 512, 384, 256, 32
MH, NOPE = 8, 64
MHD = NOPE + ROPE
GH, GKV, HD = 16, 4, 64
BW = 256
FH = 4
FORGET0 = 10 * BW
GATE0 = FORGET0 + FH
DFF = 4 * D
LAYERS = 2
POOLW = (2, 4, 8, 16)
RMS_EPS, LN_EPS = 1e-6, 1e-5
ALPHA = (2 * LAYERS) ** 0.25
MLA_SCALE = float(MHD) ** -0.5
HEAD_SCALE = float(HD) ** -0.5
NEG = -1e30
RSQRT_BITS = 0x5F3759DF
TWO_PI_1 = 6.28125
TWO_PI_2 = 0.0019350051879882812
TWO_PI_3 = 3.0198696e-07
ROUND = 1.5 * 2.0 ** 23

V_C, V_CC, V_C2, V_NG, V_QN, V_KN, V_BM, V_N = 0, 8, 16, 24, 40, 43, 45, 61
R_CB, R_FQ, R_GT, R_UP, R_CW, R_PS, R_N = 0, 6, 10, 42, 74, 80, 82

K_ID, K_ONE, K_CAUSAL, K_WIN, K_ROPE = 0, 128, 256, 384, 512
K_INV = K_ROPE + TC * 96
K_N = K_INV + 8
KE_CH, KE_SEQ = 0, 2 * P
KE_N = KE_SEQ + TC * 2 * N
KH_POOL, KH_SEL = 0, TC * 4 * N
KH_N = KH_SEL + FH * N

WSLOTS, WCOLS = 3, 4 * COLS


def halves(*names):
    return [(name, h) for name in names for h in range(2)]


FIRST_SLABS = (halves("fin", "fgate", "qa", "kva", "mgate", "qb") + [("kvb", 0)]
               + halves("eout0", "eout1", "oq0", "oq1", "okv", "og0", "og1", "oout0", "oout1"))
LAYER_SLABS = (halves("in0", "in1", "in2", "in3", "in4", "forget")
               + [s for j in range(8) for s in halves(f"gate{j}") + [(f"branch{j}", 0)]]
               + halves("o0", "o1", "up0") + [s for j in range(1, 8) for s in halves(f"up{j}", f"down{j - 1}")]
               + halves("down7"))
assert len(LAYER_SLABS) % WSLOTS == 0

SSLOTS = 2
SPLIT_SLABS = [s for s in LAYER_SLABS if s[0][:6] != "branch"]
FIRST_SPLIT = halves("oq0", "oq1", "okv", "og0", "og1")
assert len(SPLIT_SLABS) % SSLOTS == len(FIRST_SPLIT) % SSLOTS == 0

FIRST_MODS = [("shift0", 2, False), ("scale0", 2, False), ("shift1", 2, False),
              ("scale1", 2, False), ("gate0", 2, True), ("gate1", 1, True),
              ("next shift", 1, False), ("next scale", 1, False)]
PE_MODS = 2
LAYER_MODS = [("g1", 1, True), ("sh2", 1, False), ("sc2", 1, False), ("g2", 1, True),
              ("next shift", 1, False), ("next scale", 1, False)]


def mod_jobs(mods, c, group):
    _, streams, rows = mods[c]
    if not rows:
        return [(("mod", c), group)]
    return [(("mod", c, v, h), group) for v in range(streams) for h in range(2)]


def first_jobs():
    lo, hi, last = (0, 1, 2, 3), (4, 5, 6, 7), (7,)
    jobs = [(("vec",), last)] + [(("mod rows", c, h), lo) for c in range(PE_MODS) for h in range(2)]
    jobs += mod_jobs(FIRST_MODS, 0, (5,)) + mod_jobs(FIRST_MODS, 1, (6,))
    jobs += [(("xT", k), lo) for k in range(KD)]
    jobs += [(("fin", m), hi) for m in range(4)] + [(("fgate", m), lo) for m in range(4)]
    jobs += mod_jobs(FIRST_MODS, 2, lo)
    jobs += [(("qa", t), hi) for t in range(TALL)] + [(("kva", t), lo) for t in range(TALL)]
    jobs += mod_jobs(FIRST_MODS, 3, last)
    for g in range(5):
        if g < 4:
            jobs += [(("f1", g, h), (4, 5)) for h in range(2)]
        if g > 0:
            jobs += [(("f2", g - 1), (6,))]
    jobs += [(("mgate", m), lo) for m in range(4)]
    jobs += [(("qaT", k), (4, 5)) for k in range(3)] + [(("kvaT", k), (4, 5)) for k in range(2)]
    jobs += [(("qb", h, t), lo) for h in range(2) for t in range(TALL)]
    jobs += [(("kvb", t, h), (6, 7)) for t in range(TALL) for h in range(2)]
    for h in range(MH):
        jobs += [(("qT", h), (0, 1)), (("kT", h), (2, 3))]
    for h in range(MH + 2):
        if h < MH:
            jobs += [(("S", h, i), (0, 1)) for i in range(3)]
        if 1 <= h <= MH:
            jobs += [(("PT", h - 1, i), (2, 3, 4)) for i in range(3)]
        if h >= 2 and h % 2 == 0:
            jobs += [(("PV", (h - 2) // 2), (5, 6))]
        if h == 3:
            jobs += mod_jobs(FIRST_MODS, 4, last)
    jobs += [(("eout", h, t), lo) for h in range(2) for t in range(TALL)]
    jobs += mod_jobs(FIRST_MODS, 5, last)
    jobs += [(("oxT", k), lo) for k in range(KD)]
    jobs += [(("oq", h, t), hi) for h in range(2) for t in range(TC)]
    jobs += [(("okv", t), lo) for t in range(TALL)] + [(("og", m), hi) for m in range(4)]
    jobs += [(("oqT", i), lo) for i in range(4)] + [(("okT", g), lo) for g in range(GKV)]
    for h in range(GH + 2):
        if h < GH:
            jobs += [(("OS", h, i), (0, 1)) for i in range(2)]
        if 1 <= h <= GH:
            jobs += [(("OPT", h - 1, i), (2, 3, 4)) for i in range(2)]
        if h >= 2 and h % 2 == 0:
            jobs += [(("OPV", (h - 2) // 2), (5, 6))]
        if h == 6:
            jobs += mod_jobs(FIRST_MODS, 6, last)
    jobs += [(("oout", h, t), lo) for h in range(2) for t in range(TC)]
    return jobs + mod_jobs(FIRST_MODS, 7, last)


def layer_jobs():
    lo, hi = (0, 1, 2, 3), (4, 5, 6, 7)
    jobs = [(("xT", i), lo) for i in range(4)] + [(("cols",), (7,))]
    jobs += [((s,), lo) for s in ("pin", "cb", "cc", "ch")] + [(("mqk", t), lo) for t in range(TC)]
    jobs += [((s,), lo) for s in ("mv", "fq", "fk", "fv", "forget")]
    jobs += [(("poolT", m), (4, 5)) for m in range(2)] + [(("mixT",), (6,))]
    jobs += [(("mqT",), (4,)), (("mkT",), (5,))]
    for a in range(10):
        if a < 8:
            jobs += [(("S", a), (4, 5))]
        if a in GATES_BESIDE:
            jobs += gate_jobs(GATES_BESIDE.index(a), lo)
        if 1 <= a <= 8:
            jobs += [(("PT", a - 1), (6,))]
        if a >= 2 and a % 2 == 0:
            jobs += [(("PV", (a - 2) // 2), (7,))]
        if a in MODS_BESIDE:
            jobs += mod_jobs(LAYER_MODS, MODS_BESIDE.index(a), lo)
    jobs += gate_jobs(6, lo) + gate_jobs(7, lo)
    jobs += [(("o", h, t), lo) for h in range(2) for t in range(TC)]
    jobs += [(("x2T", i), hi) for i in range(4)] + mod_jobs(LAYER_MODS, 3, lo)
    for j in range(9):
        if j < 8:
            jobs += [(("up", j, i), lo) for i in range(2)]
        if j == 1:
            jobs += [(("down", t, h), (4 + 2 * t + h,)) for t in range(TC) for h in range(2)]
        if j in (6, 8):
            jobs += mod_jobs(LAYER_MODS, j // 2 + 1, lo)
    return jobs


GATES_BESIDE = (0, 1, 3, 5, 7, 8)
MODS_BESIDE = (1, 5, 9)
CHUNKS_BESIDE = (2, 2, 0, 2, 0, 2, 0, 2, 2, 2)


def gate_jobs(j, group):
    return [((s, j, i), group) for s in ("gate", "prod") for i in range(2)]


def place_jobs(jobs):
    turn, held, place = {}, [0] * 8, {}
    for name, group in jobs:
        n = turn.get(group, 0)
        turn[group] = n + 1
        bank = group[n % len(group)]
        assert name not in place, name
        place[name] = (bank, held[bank])
        held[bank] += 1
    return place, held


FIRST_PLACE, FIRST_HELD = place_jobs(first_jobs())
LAYER_PLACE, LAYER_HELD = place_jobs(layer_jobs())

COUNTS = {
    "dve_order": (0, 0), "act_order": (0, 0), "pool_order": (0, 0),
    "xn_ready": (2 * TALL, 2 * TC), "acc_used": (len(FIRST_MODS), len(LAYER_MODS)),
    "tanh_done": (12, 0), "q_lat": (4 + 4, 0), "kpe_ready": (1 + 2, 0), "okv_act": (2, 0),
    "max_ready": (3 * MH + GH, 8), "exp_done": (GH, 0), "p_ready": (MH + GH, 8),
    "x_out": (1, 1), "cols_ready": (0, 1), "angles_ready": (1, 0), "rotary_ready": (1, 0),
    "ctanh_done": (1, 0), "rotated": (0, 2), "forget_act": (0, 1), "forget_ready": (0, 1),
    "silu_ready": (1, 0), "split_free": (len(FIRST_SPLIT), len(SPLIT_SLABS)),
    "high_ready": (len(FIRST_SPLIT), len(SPLIT_SLABS)), "u_ready": (KD, 12),
    "conv_ready": (0, 1), "merged": (0, 12), "norm1": (0, 1), "hdn_ready": (0, 8),
}


class Section:

    def __init__(self, layer=None):
        self.layer = layer
        self.place = FIRST_PLACE if layer is None else LAYER_PLACE
        self.mods = FIRST_MODS if layer is None else LAYER_MODS
        self.slabs = FIRST_SLABS if layer is None else LAYER_SLABS
        self.splits = FIRST_SPLIT if layer is None else SPLIT_SLABS

    def of(self, before, per, n):
        return n if self.layer is None else self.layer * per + (before + n)

    def at(self, name, n):
        return self.of(*COUNTS[name], n)

    def bank(self, job, n):
        b, i = self.place[job]
        return b, self.of(FIRST_HELD[b], LAYER_HELD[b], i + n)

    def slab(self, name):
        n = self.slabs.index(name)
        if self.layer is None:
            return n % WSLOTS, n // WSLOTS
        s = (len(FIRST_SLABS) + n) % WSLOTS
        return s, self.of(len(FIRST_SLABS[s::WSLOTS]), len(LAYER_SLABS) // WSLOTS, n // WSLOTS)

    def chunk(self, c, q):
        return q % 2, self.of(2 * len(FIRST_MODS), 2 * len(LAYER_MODS), 2 * c + q // 2)

    def split(self, name):
        n = self.splits.index(name)
        return n, n % SSLOTS

    def biases(self, c):
        def count(mods, n):
            first = c % 2 + (PE_MODS if mods is FIRST_MODS else 0)
            return sum(m[1] for m in mods[first:n:2])
        return self.of(count(FIRST_MODS, len(FIRST_MODS)), count(LAYER_MODS, len(LAYER_MODS)),
                       count(self.mods, c + 1))


class Order:

    def __init__(self, eng, sem):
        self.eng, self.sem, self.n, self.start, self.sec = eng, sem, 0, 0, None

    def section(self, sec, per=0):
        self.sec, self.per = sec, per
        self.start, self.n = self.start + self.n, 0

    def link(self, ins):
        self.n += 1
        ins.then_inc(self.sem, 1)
        self.eng.wait_ge(self.sem, self.sec.of(self.start, self.per, self.n))

    def end_layer(self, layer_body=True):
        assert self.n == self.per, f"{self.sem}: {self.n} links in a layer, not {self.per}"


DVE_LINKS, ACT_LINKS, POOL_LINKS = 181, 1, 6


def program(nc, t, out):
    ctx = ExitStack()
    with ctx:
        def sb(name, shape, dt=F32, where=ctx):
            return where.enter_context(nc.sbuf_tensor(name, shape, dt))

        def sem(name):
            return ctx.enter_context(nc.semaphore(name))

        bank = [ctx.enter_context(nc.psum_tensor(f"bank{b}", [P, COLS], F32)) for b in range(8)]

        kst = sb("constants", [P, K_N])
        wring = sb("weight_ring", [P, WSLOTS, WCOLS])
        mring = sb("modulation_ring", [P, 2, 4 * COLS])
        acc0 = sb("modulation_sums", [P, 2, D])
        x = sb("x", [P, TALL, D])
        vcol = sb("vector_columns", [P, V_N])
        ccol = sb("silu_c_columns", [P, 24])
        ctanh = sb("silu_c_tanh", [P, 24])
        mcol = sb("modulation_columns", [P, 2, 2 * KD])
        mcol2 = sb("modulation_columns_2", [P, 2, KD])
        grow1 = sb("gate_row", [P, D])
        stat = sb("statistics", [P, TALL, 12])
        mv = sb("mean_variance", [P, TALL, 2])
        nwt = sb("newton", [P, 4, TALL])
        nwi = sb("newton_bits", [P, 2, TALL], I32)
        negmax = sb("negated_maxima", [P, 2, TALL])
        esum = sb("exp_sums", [P, 2, TALL])
        rsum = sb("reciprocal_sums", [P, 2, TALL])
        esink = sb("exp_sinks", [P, 2, TC])
        rotary = sb("rotary_angles", [P, 6, TC * 8])
        posi = sb("positions", [P, TC], I32)
        idle = sb("carriers_of_waits", [P, 8 + TALL])
        posf = sb("positions_float", [P, TC])

        ident = kst[:, K_ID:K_ID + P]
        ones = kst[:, K_ONE:K_ONE + P]
        causal = kst[:, K_CAUSAL:K_CAUSAL + P]
        window = kst[:, K_WIN:K_WIN + P]
        rope_t = kst[:, K_ROPE:K_INV].rearrange("p (t n) -> p t n", t=TC)

        even = ExitStack()
        bigA = sb("even_A", [P, 4 * D], where=even)
        bigB = sb("even_B", [P, 4 * D], where=even)
        bigC = sb("even_C", [P, 4 * D], where=even)
        bigE = sb("even_E", [P, 4 * D], where=even)
        nT = sb("even_latentsT", [P, 5, 2 * N], where=even)
        ev = sb("even_v", [P, TALL, MH * NOPE], where=even)
        eyT = sb("even_yT", [P, 8, 2 * N], where=even)
        kE = sb("even_constants", [P, KE_N], where=even)
        acc1 = sb("modulation_sums_of_context", [P, 2, D], where=even)
        even.close()
        acc = [acc0, acc1]
        A3, B3, C3, E3 = (v[:, :] for v in (bigA, bigB, bigC, bigE))
        xn_e = A3.rearrange("p (t n) -> p t n", t=TALL)
        hT_e = B3.rearrange("p (k n) -> p k n", k=KD)
        fT = C3[:, 0:4 * 2 * N].rearrange("p (k n) -> p k n", k=4)
        dft1 = C3[:, 4 * 2 * N:].rearrange("p (b t n) -> p b t n", b=2, t=TALL)
        qrow = A3[:, 0:TALL * MH * MHD].rearrange("p (t h n) -> p t h n", t=TALL, h=MH)
        krow = B3[:, 0:TALL * MH * MHD].rearrange("p (t h n) -> p t h n", t=TALL, h=MH)
        grow_e = [A3[:, 3 * D:4 * D], B3[:, 3 * D:4 * D]]
        qn = E3[:, 0:TALL * QR].rearrange("p (t n) -> p t n", t=TALL)
        kvn = E3[:, TALL * QR:TALL * (QR + KVR)].rearrange("p (t n) -> p t n", t=TALL)
        kpe = E3[:, TALL * (QR + KVR):TALL * (QR + KVR + 3 * ROPE)].rearrange(
            "p (t s n) -> p t s n", t=TALL, s=3)
        vrow = bigE
        modrow = bigC[0:2, 0:PE_MODS * D].rearrange("p (c n) -> p c n", c=PE_MODS)
        qT_e = bigC[0:MHD, :].rearrange("p (h n) -> p h n", h=MH)
        kT_e = bigE[0:MHD, :].rearrange("p (h n) -> p h n", h=MH)
        prob_e = A3[:, 0:2 * 3 * COLS].rearrange("p (b n) -> p b n", b=2)
        probT_e = B3[:, 0:2 * 3 * COLS].rearrange("p (b i n) -> p b i n", b=2, i=3)
        tanh_e = A3[:, 0:2 * COLS].rearrange("p (b n) -> p b n", b=2)
        etmp = A3[:, 0:2 * COLS].rearrange("p (b n) -> p b n", b=2)
        qrot = E3[:, TALL * (QR + KVR + 3 * ROPE):TALL * (QR + KVR + 3 * ROPE) + 2 * 4 * ROPE].rearrange(
            "p (s n) -> p s n", s=2)

        odd = ExitStack()
        xn_o = sb("odd_xn", [P, TALL, D], where=odd)
        hhigh_o = sb("odd_hT_high", [P, KD, 2 * N], F32R, where=odd)
        hlow_o = sb("odd_hT_low", [P, KD, 2 * N], F32R, where=odd)
        oq = sb("odd_q", [P, TC, D], where=odd)
        okr = sb("odd_k", [P, TALL, GKV, 2, HD], where=odd)
        ov = sb("odd_v", [P, TALL, GKV * HD], where=odd)
        oyT = sb("odd_yT", [P, KD, N], where=odd)
        orot = sb("odd_rotary_products", [P, 2, GH, HD // 2], where=odd)
        sink = sb("sinks", [P, 2, GH], where=odd)
        inputs = ExitStack()
        whigh_o = sb("odd_weights_high", [P, SSLOTS, WCOLS], F32R, where=inputs)
        wlow_o = sb("odd_weights_low", [P, SSLOTS, WCOLS], F32R, where=inputs)
        inputs.close()
        oqT = sb("odd_qT", [P, KD, N], where=odd)
        okT = sb("odd_kT", [P, GKV, 2 * N], where=odd)
        oprobT = sb("odd_probT", [P, 2, 2, 2 * N], where=odd)
        odd.close()

        def whole_o(k):
            return orot[:, k % 2, :, :].rearrange("p h n -> p (h n)")

        oflat = xn_o[:, :, :].rearrange("p t n -> p (t n)")
        oprob = oflat[:, 0:2 * 2 * COLS].rearrange("p (b i n) -> p b i n", b=2, i=2)
        otanh = oflat[:, 2 * 2 * COLS:3 * 2 * COLS].rearrange("p (b n) -> p b n", b=2)
        otmp = oflat[:, 2 * 2 * COLS:3 * 2 * COLS].rearrange("p (b n) -> p b n", b=2)
        fing = oflat[:, 3 * 2 * COLS:4 * 2 * COLS]

        hyb = ExitStack()
        xn = sb("xn", [P, TC, D], where=hyb)
        whigh = sb("weights_high", [P, SSLOTS, WCOLS], F32R, where=hyb)
        wlow = sb("weights_low", [P, SSLOTS, WCOLS], F32R, where=hyb)
        uhigh = sb("uT_high", [P, KD, N], F32R, where=hyb)
        ulow = sb("uT_low", [P, KD, N], F32R, where=hyb)
        merged = sb("mergedT", [P, KD, N], where=hyb)
        lnrow = sb("norm_rows", [P, 2, D], where=hyb)
        brow = sb("bias_rows", [P, 5, BW], where=hyb)
        lrow = sb("layer_rows", [R_N, P], where=hyb)
        lcol = sb("layer_columns", [P, R_N], where=hyb)
        hcol = sb("halved_gate_bias", [P, 32], where=hyb)
        fbias = sb("forget_bias", [FH, 1], where=hyb)
        wpool = sb("pool_weights", [P, 2, P], where=hyb)
        conv = sb("conv_v", [P, 2, N + 2], where=hyb)
        pooled = sb("pooledT", [P, 2, N], where=hyb)
        qT = sb("qT", [P, 4, N], where=hyb)
        kT = sb("kT", [P, 4, N], where=hyb)
        vr = sb("v", [P, TC, 8, HD], where=hyb)
        forget = sb("forget", [FH, 6, N], where=hyb)
        prob = sb("prob", [P, 2, 3 * P], where=hyb)
        probT = sb("probT", [P, 2, 3 * P], where=hyb)
        tanhg = sb("gate_tanh", [P, 2, COLS], where=hyb)
        term = sb("branch_terms", [P, 2, COLS], where=hyb)
        rtmp = sb("rotary_products", [P, 2, 8, 16], where=hyb)
        mlp = ExitStack()
        hhigh = sb("hidden_high", [P, 2, 4, N], F32R, where=mlp)
        hlow = sb("hidden_low", [P, 2, 4, N], F32R, where=mlp)
        mlp.close()
        kH = sb("hybrid_constants", [P, KH_N], where=hyb)
        hyb.close()
        chh, cc = (term[:, i, :].rearrange("p (m n) -> p m n", m=2) for i in range(2))
        whole = merged
        hdn = merged[:, :, :].rearrange("p (b i) n -> p b i n", b=2)
        xflat = xn[:, :, :].rearrange("p t n -> p (t n)")
        mqk = xflat[:, 0:TC * COLS].rearrange("p (t n) -> p t n", t=TC)
        pin = xflat[:, TC * COLS:TC * COLS + TC * BW].rearrange("p (t n) -> p t n", t=TC)
        cb = xflat[:, TC * (COLS + BW):TC * (COLS + 2 * BW)].rearrange("p (m n) -> p m n", m=2)
        yT = x[:, TC:TALL, :].rearrange("p t n -> p (t n)").rearrange("p (b m n) -> p b m n", b=4, m=2)
        selh = kH[0:FH, KH_SEL:KH_N].rearrange("p (h n) -> p h n", h=FH)
        poolm = kH[:, KH_POOL:KH_SEL].rearrange("p (t g n) -> p t g n", t=TC, g=4)

        w_full = [sem(f"w_full{s}") for s in range(WSLOTS)]
        w_free = [sem(f"w_free{s}") for s in range(WSLOTS)]
        m_full = [sem(f"m_full{s}") for s in range(2)]
        m_free = [sem(f"m_free{s}") for s in range(2)]
        acc_init = [sem(f"acc_init{s}") for s in range(2)]
        full = [sem(f"bank_full{b}") for b in range(8)]
        free = [sem(f"bank_free{b}") for b in range(8)]
        consts_in, vecs_in, x_in, sink_in, fing_in, kE_in, kH_in, pos_in = (sem(s) for s in (
            "consts_in", "vecs_in", "x_in", "sink_in", "fing_in", "kE_in", "kH_in", "pos_in"))
        out_stored, wpool_zero, wpool_in, ln_in, bias_in, lrow_in = (sem(s) for s in (
            "out_stored", "wpool_zero", "wpool_in", "ln_in", "bias_in", "lrow_in"))
        S = {name: sem(name) for name in COUNTS}

        def w_slab(name, h, l):
            def cut(w, c0, n, k0, kn):
                return w.rearrange("(k p) n -> p k n", p=P)[:, k0:k0 + kn, c0:c0 + n], kn, n

            def layer(w):
                return w[bass.ds(l, 1)].rearrange("o k n -> (o k) n")

            e, o = t["e_w_in"][0], t["o_w_in"][0]
            split = [0, FW, 2 * FW, 2 * FW + QR, 2 * FW + QR + KVR + ROPE]
            if name in ("fin", "fgate", "qa", "kva", "mgate"):
                i = ("fin", "fgate", "qa", "kva", "mgate").index(name)
                return cut(e, split[i], (FW, FW, QR, KVR + ROPE, FW)[i], 4 * h, 4)
            if name == "qb":
                return cut(t["e_w_qb"][0], 4 * MHD * h, 4 * MHD, 0, 3)
            if name == "kvb":
                return cut(t["e_w_kvb"][0], 0, 2 * COLS, 0, 2)
            if name[:4] in ("eout", "oout"):
                w = t["e_w_out"][0] if name[0] == "e" else t["o_w_out"][0]
                return cut(w, COLS * int(name[4]), COLS, 4 * h, 4)
            if name in ("oq0", "oq1", "okv", "og0", "og1"):
                return cut(o, COLS * ("oq0", "oq1", "okv", "og0", "og1").index(name), COLS, 4 * h, 4)
            if name[:2] == "in":
                return cut(layer(t["w_in_2"]), COLS * int(name[2]), COLS, 4 * h, 4)
            if name == "forget":
                return cut(layer(t["w_in_2"]), FORGET0, FH, 4 * h, 4)
            if name[:4] == "gate":
                return cut(layer(t["w_in_2"]), GATE0 + COLS * int(name[4]), COLS, 4 * h, 4)
            if name[:6] == "branch":
                j = int(name[6])
                w = t["w_branch_2"][bass.ds(l, 1)].rearrange("o b k n -> (o b k) n")
                return cut(w, COLS * (j % 2), COLS, 2 * (j // 2), 2)
            if name[0] == "o":
                return cut(layer(t["w_o_2"]), COLS * int(name[1]), COLS, 4 * h, 4)
            if name[:2] == "up":
                return cut(layer(t["w_up_2"]), COLS * int(name[2]), COLS, 4 * h, 4)
            return cut(layer(t["w_down_2"]), 0, D, 4 * int(name[4]) + 2 * h, 2)

        def w_view(sec, name, h):
            slot = sec.slab((name, h))[0]
            _, kn, n = w_slab(name, h, 0)
            return wring[:, slot, 0:kn * n].rearrange("p (k n) -> p k n", k=kn)

        def split_view(sec, name, h):
            slot = sec.split((name, h))[1]
            _, kn, n = w_slab(name, h, 0)
            rings = (whigh_o, wlow_o) if sec.layer is None else (whigh, wlow)
            return [ring[:, slot, 0:kn * n].rearrange("p (k n) -> p k n", k=kn) for ring in rings]

        def mod_source(sec, c):
            name = sec.mods[c][0]
            if sec.layer is None and c < 6:
                n, at = int(name[-1]), D * ("shift", "scale", "gate").index(name[:-1])
                return t["w_mod"][n], t["b_mod"][n], at
            at = {"next shift": 0, "next scale": 1, "g1": 2, "sh2": 3, "sc2": 4, "g2": 5}[name]
            if sec.layer is None:
                return t["w_ada_2"][0], t["b_ada_2"][0], D * at
            l = sec.next_layer if at < 2 else sec.layer
            return (t["w_ada_2"][bass.ds(l, 1)].rearrange("o k n -> (o k) n"),
                    t["b_ada_2"][bass.ds(l, 1)].rearrange("o n -> (o n)"), D * at)

        block = ctx.enter_context(nc.Block())

        @block.sync
        def _(sp):
            def load(sec, name, h):
                slot, before = sec.slab((name, h))
                if sec.layer is not None or before > 0:
                    sp.wait_ge(w_free[slot], before)
                src, _, _ = w_slab(name, h, sec.layer)
                sp.dma_start(w_view(sec, name, h), src).then_inc(w_full[slot], 16)

            sec = Section()
            sp.dma_start(vrow[0:V_NG, 0:P][V_C:V_CC], t["c"].rearrange("o (k p) -> (o k) p", p=P)).then_inc(vecs_in, 16)
            sp.dma_start(vrow[V_CC:V_C2, 0:P], t["c_ctx"].rearrange("(k p) -> k p", p=P)).then_inc(vecs_in, 16)
            sp.dma_start(vrow[V_C2:V_NG, 0:P], t["c_2"].rearrange("o (k p) -> (o k) p", p=P)).then_inc(vecs_in, 16)
            sp.dma_start(vrow[V_NG:V_QN, 0:P], t["norm_g"].rearrange("l (k p) -> (l k) p", p=P)).then_inc(vecs_in, 16)
            sp.dma_start(vrow[V_QN:V_KN, 0:P], t["e_q_norm"].rearrange("o (k p) -> (o k) p", p=P)).then_inc(vecs_in, 16)
            sp.dma_start(vrow[V_KN:V_BM, 0:P], t["e_kv_norm"].rearrange("o (k p) -> (o k) p", p=P)).then_inc(vecs_in, 16)
            sp.dma_start(vrow[V_BM:V_N, 0:P], t["b_mod"][0, 0:PE_MODS * D].rearrange("(k p) -> k p", p=P)).then_inc(vecs_in, 16)
            sp.dma_start(x[:, 0:TC, :], t["x"][0].rearrange("(t p) n -> p t n", p=P)).then_inc(x_in, 16)
            sp.dma_start(x[:, TC:TALL, :], t["ctx"][0].rearrange("(t p) n -> p t n", p=P)).then_inc(x_in, 16)
            for name, h in FIRST_SLABS:
                load(sec, name, h)
            with sp.Fori(0, LAYERS) as l:
                sec = Section(l)
                for name, h in LAYER_SLABS:
                    load(sec, name, h)
            sp.wait_ge(S["x_out"], COUNTS["x_out"][0] + LAYERS)
            sp.dma_start(out[0].rearrange("(t p) n -> p t n", p=P), x[:, 0:TC, :]).then_inc(out_stored, 16)
            sp.wait_ge(out_stored, 16)

        @block.gpsimd
        def _(pool):
            order = Order(pool, S["pool_order"])

            def take_wait(n):
                if sec.layer is not None:
                    pool.tensor_tensor(idle[:, n:n + 1], ones[:, 0:1], ones[:, 0:1], ALU.mult)

            def mod_start(sec, c):
                b = c % 2
                if sec.layer is not None or c >= PE_MODS + 2:
                    pool.wait_ge(S["acc_used"], sec.at("acc_used", c - 1))
                take_wait(0)
                w, bias, c0 = mod_source(sec, c)
                for v in range(sec.mods[c][1] if sec.layer is not None or c >= PE_MODS else 0):
                    order.link(pool.memset(acc[v][:, b, :], 0.0))
                    take_wait(1)
                    pool.dma_start(acc[v][0:1, b, :], bias[c0:c0 + D].unsqueeze(0)).then_inc(acc_init[b], 16)

            def mod_chunks(sec, c, *chunks):
                w, _, c0 = mod_source(sec, c)
                for q in chunks or range(4):
                    slot, before = sec.chunk(c, q)
                    if sec.layer is not None or 2 * c + q // 2 > 0:
                        pool.wait_ge(m_free[slot], before)
                    take_wait(2 + q)
                    col = c0 + COLS * (q // 2)
                    pool.dma_start(mring[:, slot, :].rearrange("p (k n) -> p k n", k=4),
                                   w.rearrange("(k p) n -> p k n", p=P)[:, 4 * (q % 2):4 * (q % 2) + 4, col:col + COLS]
                                   ).then_inc(m_full[slot], 16)

            def mod_part(sec, c):
                mod_start(sec, c)
                mod_chunks(sec, c)

            sec = Section()
            order.section(sec)
            for c in range(len(FIRST_MODS)):
                mod_part(sec, c)
            with pool.Fori(0, LAYERS) as l:
                sec = Section(l)
                sec.next_layer = l * 0 + (LAYERS - 1)
                order.section(sec, POOL_LINKS)

                def add_terms(j, i):
                    n = 2 * (j - 2) + i
                    m = 4 * (j % 2) + 2 * i
                    b, done_ = sec.bank(("prod", j, i), 1)
                    pool.wait_ge(free[b], done_)
                    pool.tensor_tensor(merged[:, m:m + 2, :], merged[:, m:m + 2, :],
                                       term[:, i, :].rearrange("p (m n) -> p m n", m=2), ALU.add
                                       ).then_inc(S["merged"], 1)

                mod_part(sec, 0)
                mod_part(sec, 1)
                mod_start(sec, 2)
                mod_chunks(sec, 2, 0, 1)
                for j in range(2, 8):
                    for i in range(2):
                        add_terms(j, i)
                    if j == 3:
                        mod_chunks(sec, 2, 2, 3)
                        mod_start(sec, 3)
                        mod_chunks(sec, 3, 0)
                    if j == 4:
                        mod_chunks(sec, 3, 1)
                    if j == 5:
                        mod_chunks(sec, 3, 2, 3)
                mod_part(sec, 4)
                mod_part(sec, 5)
                order.end_layer()

        @block.tensor
        def _(pe):
            sec = Section()

            def start(job):
                b, before = sec.bank(job, 0)
                if sec.layer is not None or before > 0:
                    pe.wait_ge(free[b], before)
                return bank[b]

            owed, last = [], [None, True]

            def track(ins):
                if owed and not last[1]:
                    last[0].then_inc(owed.pop(0), 1)
                last[0], last[1] = ins, False
                return ins

            def product(*args, **kw):
                return track(pe.matmul(*args, **kw))

            def signal(ins, sem):
                assert ins is last[0]
                if last[1]:
                    owed.append(sem)
                else:
                    ins.then_inc(sem, 1)
                    last[1] = True

            def done(ins, job):
                signal(ins, full[sec.bank(job, 0)[0]])

            def copied(job):
                b, n = sec.bank(job, 1)
                pe.wait_ge(free[b], n)

            def pay_owed(job):
                copied(job)
                o = bank[sec.bank(job, 0)[0]]
                while owed:
                    product(o[:, 0:1], ones, ones[:, 0:1], start=True, stop=True)
                    last[0].then_inc(owed.pop(0), 1)
                    last[1] = True

            def is_split(name, h):
                return (name, h) in sec.splits

            def slab(name, h):
                slot, before = sec.slab((name, h))
                if is_split(name, h):
                    pe.wait_ge(w_free[slot], before + 1)
                    return split_view(sec, name, h)
                pe.wait_ge(w_full[slot], before * 16 + 16)
                return w_view(sec, name, h)

            def product_of_parts(o, a, b, start, stop, skip_group_check=False):
                product(o, a[0], b[0], start=start, stop=False, skip_group_check=skip_group_check)
                product(o, a[0], b[1], start=False, stop=False, skip_group_check=skip_group_check)
                return product(o, a[1], b[0], start=False, stop=stop, skip_group_check=skip_group_check)

            def multiply(o, a, b, **kw):
                if isinstance(a, list):
                    return product_of_parts(o, a, b, **kw)
                return product(o, a, b, **kw)

            def cut(w, k, c0, n):
                if isinstance(w, list):
                    return [part[:, k, c0:c0 + n] for part in w]
                return w[:, k, c0:c0 + n]

            def used(ins, name, h):
                if is_split(name, h):
                    signal(ins, S["split_free"])
                    return
                signal(ins, w_free[sec.slab((name, h))[0]])

            def reduce_part(c):
                _, streams, rows = sec.mods[c]
                slot, before = sec.chunk(c, 3)
                pe.wait_ge(m_free[slot], before + 1)
                if rows:
                    for v in range(streams):
                        for h in range(2):
                            o = start(("mod", c, v, h))
                            ins = product(o[:, :], ones, acc[v][:, c % 2, COLS * h:COLS * h + COLS],
                                            start=True, stop=True)
                            done(ins, ("mod", c, v, h))
                else:
                    o = start(("mod", c))
                    for v in range(streams):
                        for k in range(KD):
                            ins = product(o[:, v * KD + k:v * KD + k + 1], acc[v][:, c % 2, P * k:P * k + P],
                                            ones[:, 0:1], start=True, stop=True)
                    done(ins, ("mod", c))
                signal(ins, S["acc_used"])

            def features_out(names, jobs, src, ntok, per, width=P, wait=lambda k: None):
                outs = [start(j) for j in jobs]
                for h in range(2):
                    w = slab(*names[h])
                    for m in range(len(jobs) * per):
                        o = outs[m // per][0:width, (m % per) * ntok:(m % per + 1) * ntok]
                        for k in range(4):
                            if m == 0:
                                wait(4 * h + k)
                            ins = multiply(o, cut(w, k, m * width, width), src(4 * h + k),
                                            start=(h + k + m % per == 0), stop=(h == 1 and k == 3),
                                            skip_group_check=per > 1)
                        if h == 1 and m % per == per - 1:
                            done(ins, jobs[m // per])
                    used(ins, *names[h])

            def tokens_out(names, jobs, src, width, c0=0, kn=4, wait=lambda k: None):
                outs = [start(j) for j in jobs]
                nh = len(names)
                for h in range(nh):
                    w = slab(*names[h])
                    for i, o in enumerate(outs):
                        for k in range(kn):
                            if i == 0:
                                wait(kn * h + k)
                            ins = multiply(o[:, 0:width], src(kn * h + k, i), cut(w, k, c0, width),
                                            start=(h == 0 and k == 0), stop=(h == nh - 1 and k == kn - 1))
                        if h == nh - 1:
                            done(ins, jobs[i])
                    used(ins, *names[h])

            def turn(o, src, n, rows=P):
                return track(pe.transpose(o, src, ident[0:rows, 0:rows]))

            pe.wait_ge(consts_in, 16)
            pe.wait_ge(vecs_in, 16 * 7)
            done(turn(start(("vec",))[:, 0:V_N], vrow[0:V_N, 0:P], P, rows=V_N), ("vec",))
            pe.wait_ge(S["silu_ready"], 1)
            for c in range(PE_MODS):
                for q in range(4):
                    if q % 2 == 0:
                        o = start(("mod rows", c, q // 2))
                    slot, before = sec.chunk(c, q)
                    pe.wait_ge(m_full[slot], before * 16 + 16)
                    w = mring[:, slot, :].rearrange("p (k n) -> p k n", k=4)
                    for k in range(4):
                        both_c = ccol[:, 0:V_C2].rearrange("p (v k) -> p k v", v=2)[:, 4 * (q % 2) + k, :]
                        ins = product(o[0:2, :], both_c, w[:, k, :], start=(q % 2 + k == 0),
                                      stop=(q % 2 == 1 and k == 3))
                    signal(ins, m_free[slot])
                    if q % 2 == 1:
                        done(ins, ("mod rows", c, q // 2))
                signal(ins, S["acc_used"])
            for c in range(PE_MODS):
                o = start(("mod", c))
                for h in range(2):
                    copied(("mod rows", c, h))
                for k in range(KD):
                    ins = turn(o[:, 2 * k:2 * k + 2], modrow[:, c, P * k:P * k + P], P, rows=2)
                done(ins, ("mod", c))

            def turn_x(name, src, k0, n0):
                pe.wait_ge(S["xn_ready"], sec.at("xn_ready", n0))
                for k in range(KD):
                    o = start((name, k))
                    for i in range(TALL):
                        ins = turn(o[:, P * i:P * i + P], src[:, i, P * k:P * k + P], P)
                    done(ins, (name, k))

            turn_x("xT", xn_e, 0, TALL)
            for k in range(KD):
                copied(("xT", k))

            def both(h):
                return [(h, 0), (h, 1)]

            features_out(both("fin"), [("fin", m) for m in range(4)], lambda k: hT_e[:, k, :], 2 * N, 1)
            features_out(both("fgate"), [("fgate", m) for m in range(4)], lambda k: hT_e[:, k, :], 2 * N, 1)
            reduce_part(2)
            tokens_out(both("qa"), [("qa", i) for i in range(TALL)], lambda k, i: hT_e[:, k, P * i:P * i + P], QR)
            tokens_out(both("kva"), [("kva", i) for i in range(TALL)], lambda k, i: hT_e[:, k, P * i:P * i + P],
                       KVR + ROPE)
            reduce_part(3)
            pe.wait_ge(kE_in, 16)
            for g in range(5):
                if g < 4:
                    copied(("fin", g))
                    for h in range(2):
                        o = start(("f1", g, h))
                        for i in range(2):
                            tt = 2 * h + i
                            ins = product(o[:, 2 * P * i:2 * P * (i + 1)], fT[:, g, P * tt:P * tt + P],
                                            kE[:, KE_CH:KE_CH + 2 * P], start=True, stop=True)
                        done(ins, ("f1", g, h))
                if g > 0:
                    copied(("f1", g - 1, 0))
                    copied(("f1", g - 1, 1))
                    o = start(("f2", g - 1))
                    for s in range(2):
                        for i in range(TC):
                            for part in range(2):
                                seq = KE_SEQ + (2 * i + part) * N
                                ins = product(o[:, N * s:N * s + N],
                                                dft1[:, (g - 1) % 2, TC * s + i, P * part:P * part + P],
                                                kE[:, seq:seq + N], start=(i + part == 0), stop=(i + part == 2))
                    done(ins, ("f2", g - 1))
            features_out(both("mgate"), [("mgate", m) for m in range(4)], lambda k: hT_e[:, k, :], 2 * N, 1)
            for i in range(TALL):
                copied(("qa", i))
                copied(("kva", i))
            for name, n, src in (("qaT", 3, qn), ("kvaT", 2, kvn)):
                for k in range(n):
                    o = start((name, k))
                    for i in range(TALL):
                        ins = turn(o[:, P * i:P * i + P], src[:, i, P * k:P * k + P], P)
                    done(ins, (name, k))
            for k in range(3):
                copied(("qaT", k))
            for h in range(2):
                tokens_out([("qb", h)], [("qb", h, i) for i in range(TALL)],
                           lambda k, i: nT[:, k, P * i:P * i + P], 4 * MHD, kn=3)
            for k in range(2):
                copied(("kvaT", k))
            w = slab("kvb", 0)
            for i in range(TALL):
                for h in range(2):
                    o = start(("kvb", i, h))
                    for k in range(2):
                        ins = product(o[:, :], nT[:, 3 + k, P * i:P * i + P], w[:, k, COLS * h:COLS * h + COLS],
                                        start=(k == 0), stop=(k == 1))
                    done(ins, ("kvb", i, h))
            used(ins, "kvb", 0)
            pe.wait_ge(S["q_lat"], 4)
            for h in range(2):
                for i in range(TC, TALL):
                    copied(("qb", h, i))
                for i in range(TALL):
                    copied(("kvb", i, h))
            pe.wait_ge(S["kpe_ready"], 1)
            for h in range(MH):
                for name, src in (("qT", qrow), ("kT", krow)):
                    o = start((name, h))
                    for i in range(TALL):
                        ins = turn(o[0:MHD, P * i:P * i + P], src[:, i, h, :], P)
                    done(ins, (name, h))
            for h in range(MH + 2):
                if h < MH:
                    copied(("qT", h))
                    copied(("kT", h))
                    for i in range(TC):
                        o = start(("S", h, i))
                        done(product(o[:, :], qT_e[:, h, P * i:P * i + P], kT_e[:, h, :], start=True, stop=True),
                             ("S", h, i))
                    o = start(("S", h, 2))
                    for i in range(TC):
                        ins = product(o[:, N * i:N * i + N], qT_e[:, h, N + P * i:N + P * i + P],
                                        kT_e[:, h, N:2 * N], start=True, stop=True)
                    done(ins, ("S", h, 2))
                if 1 <= h <= MH:
                    a = h - 1
                    pe.wait_ge(S["p_ready"], a + 1)
                    for i in range(3):
                        o = start(("PT", a, i))
                        for j in range(2):
                            for q in range(2):
                                c = COLS * q + P * (2 * i + j) if i < 2 else 2 * COLS + N * q + P * j
                                ins = turn(o[:, N * j + P * q:N * j + P * q + P], prob_e[:, a % 2, c:c + P], P)
                        done(ins, ("PT", a, i))
                if h >= 2:
                    a = h - 2
                    r = HD * (a % 2)
                    if a % 2 == 0:
                        pv = start(("PV", a // 2))
                    copied(("PT", a, 0))
                    copied(("PT", a, 1))
                    for kb in range(TALL):
                        ins = product(pv[r:r + HD, 0:N], ev[:, kb, NOPE * a:NOPE * a + NOPE],
                                        probT_e[:, a % 2, kb // 2, N * (kb % 2):N * (kb % 2) + N],
                                        start=(kb == 0), stop=(kb == 3))
                    copied(("PT", a, 2))
                    for j in range(2):
                        ins = product(pv[r:r + HD, N:2 * N], ev[:, TC + j, NOPE * a:NOPE * a + NOPE],
                                        probT_e[:, a % 2, 2, N * j:N * j + N], start=(j == 0), stop=(j == 1))
                    if a % 2 == 1:
                        done(ins, ("PV", a // 2))
                if h == 3:
                    reduce_part(4)
            for g in range(4):
                copied(("f2", g))
                copied(("PV", g))
            for h in range(2):
                tokens_out(both(f"eout{h}"), [("eout", h, i) for i in range(TALL)],
                           lambda k, i: eyT[:, k, P * i:P * i + P], COLS)
            reduce_part(5)

            turn_x("oxT", xn_o, KD, 2 * TALL)

            def h_tokens(k, i):
                return [part[:, k, P * i:P * i + P] for part in (hhigh_o, hlow_o)]

            def h_split(k):
                pe.wait_ge(S["u_ready"], k + 1)

            for h in range(2):
                tokens_out(both(f"oq{h}"), [("oq", h, i) for i in range(TC)], h_tokens, COLS,
                           wait=h_split if h == 0 else lambda k: None)
            tokens_out(both("okv"), [("okv", i) for i in range(TALL)], h_tokens, COLS)
            for g in range(2):
                features_out(both(f"og{g}"), [("og", 2 * g), ("og", 2 * g + 1)],
                             lambda k: [hhigh_o[:, k, 0:N], hlow_o[:, k, 0:N]], N, 2)
            pe.wait_ge(S["q_lat"], 8)
            for i in range(4):
                o = start(("oqT", i))
                for pr in range(2):
                    for tt in range(TC):
                        ins = turn(o[:, N * pr + P * tt:N * pr + P * tt + P],
                                   oq[:, tt, P * (2 * i + pr):P * (2 * i + pr) + P], P)
                done(ins, ("oqT", i))
            pe.wait_ge(S["kpe_ready"], 3)
            for i in range(TALL):
                copied(("okv", i))
            for g in range(GKV):
                o = start(("okT", g))
                for i in range(TALL):
                    ins = turn(o[:, P * i:P * i + P], okr[:, i, g, :, :].rearrange("p a b -> p (a b)"), P)
                done(ins, ("okT", g))
            for h in range(GH + 2):
                if h < GH:
                    r, g = HD * (h % 2), h // (GH // GKV)
                    copied(("oqT", h // 4))
                    copied(("okT", g))
                    for i in range(TC):
                        o = start(("OS", h, i))
                        product(o[:, :], oqT[r:r + HD, h // 2, P * i:P * i + P], okT[r:r + HD, g, :],
                                  start=True, stop=True)
                        other = P * (1 - i)
                        ins = product(o[:, other:other + P], ident, causal if i == 0 else window,
                                        start=False, stop=True, skip_group_check=True)
                        done(ins, ("OS", h, i))
                if 1 <= h <= GH:
                    a = h - 1
                    pe.wait_ge(S["p_ready"], MH + a + 1)
                    for i in range(2):
                        o = start(("OPT", a, i))
                        for j in range(2):
                            for q in range(2):
                                c = P * (2 * i + j)
                                ins = turn(o[:, N * j + P * q:N * j + P * q + P], oprob[:, a % 2, q, c:c + P], P)
                        done(ins, ("OPT", a, i))
                if h >= 2:
                    a = h - 2
                    r, g = HD * (a % 2), a // (GH // GKV)
                    if a % 2 == 0:
                        pv = start(("OPV", a // 2))
                    copied(("OPT", a, 0))
                    copied(("OPT", a, 1))
                    for kb in range(TALL):
                        ins = product(pv[r:r + HD, 0:N], ov[:, kb, HD * g:HD * g + HD],
                                        oprobT[:, a % 2, kb // 2, N * (kb % 2):N * (kb % 2) + N],
                                        start=(kb == 0), stop=(kb == 3))
                    if a % 2 == 1:
                        done(ins, ("OPV", a // 2))
                if h == 6:
                    reduce_part(6)
            for g in range(8):
                copied(("OPV", g))
            for h in range(2):
                tokens_out(both(f"oout{h}"), [("oout", h, i) for i in range(TC)],
                           lambda k, i: oyT[:, k, P * i:P * i + P], COLS)
            reduce_part(7)
            pay_owed(("mod", 7))

            with pe.Fori(0, LAYERS) as l:
                sec = Section(l)
                u = lambda k: [uhigh[:, k, :], ulow[:, k, :]]
                ui = lambda k, i: [uhigh[:, k, P * i:P * i + P], ulow[:, k, P * i:P * i + P]]

                def u_split(n):
                    def wait(k):
                        if k % 2 == 0:
                            pe.wait_ge(S["u_ready"], sec.at("u_ready", 4 * n + k // 2 + 1))
                    return wait

                def turn_xn(name, n0):
                    pe.wait_ge(S["xn_ready"], sec.at("xn_ready", n0))
                    for i in range(4):
                        o = start((name, i))
                        for j in range(2):
                            for tt in range(TC):
                                ins = turn(o[:, N * j + P * tt:N * j + P * tt + P],
                                           xn[:, tt, P * (2 * i + j):P * (2 * i + j) + P], P)
                        done(ins, (name, i))

                turn_xn("xT", TC)
                pe.wait_ge(lrow_in, l * (16 * 6) + 16 * 6)
                done(turn(start(("cols",))[:, 0:R_N], lrow[:, :], P, rows=R_N), ("cols",))

                def mixed_tile(name, parts, wait=lambda k: None):
                    outs = [start(p[0]) for p in parts]
                    for h in range(2):
                        w = slab(name, h)
                        for (job, c0, n, tok), o in zip(parts, outs):
                            for m in range(2):
                                for k in range(4):
                                    first, final = h + k == 0, h == 1 and k == 3
                                    if m == 0 and c0 == 0:
                                        wait(4 * h + k)
                                    if tok:
                                        ins = multiply(o[:, n * m:n * m + n], ui(4 * h + k, m), cut(w, k, c0, n),
                                                        start=first and m == 0, stop=final, skip_group_check=True)
                                    else:
                                        ins = multiply(o[:, N * m:N * m + N], cut(w, k, c0 + P * m, P),
                                                        u(4 * h + k), start=first and m == 0, stop=final,
                                                        skip_group_check=True)
                            if h == 1:
                                done(ins, job)
                        used(ins, name, h)

                mixed_tile("in0", [(("pin",), 0, BW, True), (("cb",), BW, BW, False)], u_split(0))
                mixed_tile("in1", [(("cc",), 0, BW, False), (("ch",), BW, BW, False)])
                tokens_out(both("in2"), [("mqk", i) for i in range(TC)], ui, COLS)
                mixed_tile("in3", [(("mv",), 0, BW, True), (("fq",), BW, BW, False)])
                mixed_tile("in4", [(("fk",), 0, BW, False), (("fv",), BW, BW, True)])
                o = start(("forget",))
                for h in range(2):
                    w = slab("forget", h)
                    for k in range(4):
                        ins = multiply(o[0:FH, 0:N], cut(w, k, 0, FH), u(4 * h + k), start=(h + k == 0),
                                        stop=(h == 1 and k == 3))
                    if h == 1:
                        done(ins, ("forget",))
                    used(ins, "forget", h)
                pe.wait_ge(kH_in, l * 16 + 16)
                copied(("pin",))
                for m in range(2):
                    o = start(("poolT", m))
                    for g in range(2):
                        for i in range(TC):
                            c = HD * (2 * m + g)
                            ins = product(o[HD * g:HD * g + HD, 0:N], pin[:, i, c:c + HD],
                                            poolm[:, i, 2 * m + g, :], start=(i == 0), stop=(i == TC - 1))
                    done(ins, ("poolT", m))
                pe.wait_ge(wpool_in, l * (16 * 4) + 16 * 4)
                copied(("poolT", 0))
                copied(("poolT", 1))
                o = start(("mixT",))
                for m in range(2):
                    ins = product(o[:, N * m:N * m + N], wpool[:, m, :], pooled[:, m, :], start=True, stop=True)
                done(ins, ("mixT",))
                pe.wait_ge(S["rotated"], sec.at("rotated", 2))
                for n, name in enumerate(("mqT", "mkT")):
                    o = start((name,))
                    for pr in range(2):
                        for tt in range(TC):
                            c = BW * n + P * pr
                            ins = turn(o[:, N * pr + P * tt:N * pr + P * tt + P], mqk[:, tt, c:c + P], P)
                    done(ins, (name,))

                def gate_tile(j):
                    features_out(both(f"gate{j}"), [("gate", j, 0), ("gate", j, 1)], u, N, 2)
                    n = j // 2
                    w = slab(f"branch{j}", 0)
                    if n == 1:
                        pe.wait_ge(S["conv_ready"], sec.at("conv_ready", 1))
                    for job in ([("mixT",)], [], [("PV", 1)], [("PV", 3)])[n]:
                        copied(job)
                    for i in range(2):
                        o = start(("prod", j, i))
                        for m in range(2):
                            for k in range(2):
                                c = P * (2 * i + m)
                                ins = product(o[:, N * m:N * m + N], w[:, k, c:c + P], yT[:, n, k, :],
                                                start=(k == 0), stop=(k == 1))
                        done(ins, ("prod", j, i))
                    used(ins, f"branch{j}", 0)

                for a in range(10):
                    if a < 8:
                        r, pr = HD * (a % 2), a // 2
                        if a == 0:
                            copied(("mqT",))
                            copied(("mkT",))
                        if a == 4:
                            pe.wait_ge(S["forget_ready"], sec.at("forget_ready", 1))
                        o = start(("S", a))
                        for i in range(TC):
                            c, n = P * i, P * (i + 1)
                            product(o[:, c:c + n], qT[r:r + HD, pr, P * i:P * i + P], kT[r:r + HD, pr, 0:n],
                                      start=(i == 0), stop=True, skip_group_check=True)
                            if a >= 4:
                                f = a - 4
                                product(o[:, c:c + n], forget[:, 4, P * i:P * i + P], selh[:, f, 0:n],
                                          start=False, stop=True, skip_group_check=True)
                                product(o[:, c:c + n], selh[:, f, 0:P], forget[:, 5, 0:n],
                                          start=False, stop=True, skip_group_check=True)
                            ins = product(o[:, c + n - P:c + n], ident, causal, start=False, stop=True,
                                            skip_group_check=True)
                        done(ins, ("S", a))
                    if a in GATES_BESIDE:
                        gate_tile(GATES_BESIDE.index(a))
                    if 1 <= a <= 8:
                        b = a - 1
                        pe.wait_ge(S["p_ready"], sec.at("p_ready", b + 1))
                        o = start(("PT", b))
                        for i in range(3):
                            ins = turn(o[:, P * i:P * i + P], prob[:, b % 2, P * i:P * i + P], P)
                        done(ins, ("PT", b))
                    if a >= 2:
                        b = a - 2
                        r = HD * (b % 2)
                        if b % 2 == 0:
                            pv = start(("PV", b // 2))
                        copied(("PT", b))
                        product(pv[r:r + HD, 0:N], vr[:, 0, b, :], probT[:, b % 2, 0:N],
                                  start=True, stop=True, skip_group_check=True)
                        ins = product(pv[r:r + HD, P:N], vr[:, 1, b, :], probT[:, b % 2, N:N + P],
                                        start=False, stop=True, skip_group_check=True)
                        if b % 2 == 1:
                            done(ins, ("PV", b // 2))
                    if a in MODS_BESIDE:
                        reduce_part(MODS_BESIDE.index(a))
                gate_tile(6)
                gate_tile(7)
                for h in range(2):
                    tokens_out(both(f"o{h}"), [("o", h, i) for i in range(TC)], ui, COLS,
                               wait=u_split(1) if h == 0 else lambda k: None)
                turn_xn("x2T", 2 * TC)
                reduce_part(3)
                for j in range(9):
                    if j < 8:
                        features_out(both(f"up{j}"), [("up", j, 0), ("up", j, 1)], u, N, 2,
                                     wait=u_split(2) if j == 0 else lambda k: None)
                    if j == 8:
                        reduce_part(5)
                    if j == 1:
                        downs = {(i, h): start(("down", i, h)) for i in range(TC) for h in range(2)}
                    if j >= 1:
                        d = j - 1
                        pe.wait_ge(S["hdn_ready"], sec.at("hdn_ready", d + 1))
                        for s in range(2):
                            w = slab(f"down{d}", s)
                            for i in range(TC):
                                for h in range(2):
                                    for k in range(2):
                                        hid = [part[:, d % 2, 2 * s + k, P * i:P * i + P]
                                               for part in (hhigh, hlow)]
                                        ins = multiply(downs[i, h][:, :], hid, cut(w, k, COLS * h, COLS),
                                                        start=(d + s + k == 0), stop=(d == 7 and s + k == 2))
                                    if d == 7 and s == 1:
                                        done(ins, ("down", i, h))
                            used(ins, f"down{d}", s)
                    if j == 6:
                        reduce_part(4)
                pay_owed(("mod", 5))

        @block.scalar
        def _(act):
            sec = Section()
            order = Order(act, S["act_order"])
            order.section(sec)

            def ready(job):
                b, n = sec.bank(job, 1)
                act.wait_ge(full[b], n)
                return bank[b]

            def release(ins, job):
                ins.then_inc(free[sec.bank(job, 0)[0]], 1)

            act.dma_start(kst[:, :], t["constants"]).then_inc(consts_in, 16)
            act.dma_start(kE[:, :], t["even_constants"]).then_inc(kE_in, 16)
            with nc.allow_non_contiguous_dma(reason="256 positions, one to a partition"):
                act.dma_start(posi[:, :], t["positions_2"].rearrange("o (t p) -> p (o t)", p=P)).then_inc(pos_in, 16)

            def copied(job):
                b, n = sec.bank(job, 1)
                act.wait_ge(free[b], n)

            def high(*names):
                for name in names:
                    for h in range(2):
                        slot, before = sec.slab((name, h))
                        n, s = sec.split((name, h))
                        act.wait_ge(w_full[slot], before * 16 + 16)
                        if sec.layer is not None or n >= SSLOTS:
                            act.wait_ge(S["split_free"], sec.at("split_free", n + 1 - SSLOTS))
                        _, kn, cols = w_slab(name, h, 0)
                        ring = whigh_o if sec.layer is None else whigh
                        act.activation(ring[:, s, 0:kn * cols], wring[:, slot, 0:kn * cols], ACT.Copy
                                       ).then_inc(S["high_ready"], 1)

            copied(("vec",))
            act.activation(ctanh[:, :], vcol[:, 0:24], ACT.Tanh, scale=0.5).then_inc(S["ctanh_done"], 1)

            def modulate(name, dst, parts):
                for c in parts:
                    copied(("mod", c))
                for k in range(KD):
                    o = ready((name, k))
                    if name == "oxT" and k >= 2:
                        act.wait_ge(S["u_ready"], k - 1)
                    for v in range(2):
                        ins = act.activation(dst(k)[:, N * v:N * v + N], o[:, N * v:N * v + N], ACT.Identity,
                                             bias=mcol[:, 0, v * KD + k:v * KD + k + 1],
                                             scale=mcol[:, 1, v * KD + k:v * KD + k + 1])
                    release(ins, (name, k))

            def tanh_tile(job, last_but_one, dst):
                o = ready(job)
                if last_but_one:
                    copied(last_but_one)
                act.activation(dst, o[:, :], ACT.Tanh, scale=0.5).then_inc(S["tanh_done"], 1)

            def gate_rows(c, dst, scale=1.0):
                _, streams, _ = sec.mods[c]
                for v in range(streams):
                    for h in range(2):
                        o = ready(("mod", c, v, h))
                        ins = act.activation(dst[v][:, COLS * h:COLS * h + COLS], o[:, :], ACT.Copy, scale=scale)
                        release(ins, ("mod", c, v, h))

            def copy_out(job, dst, src, scale=1.0):
                release(act.activation(dst, src, ACT.Copy, scale=scale), job)

            for c in range(PE_MODS):
                for h in range(2):
                    o = ready(("mod rows", c, h))
                    copy_out(("mod rows", c, h), modrow[:, c, COLS * h:COLS * h + COLS], o[0:2, :])

            modulate("xT", lambda k: hT_e[:, k, :], (0, 1))
            for m in range(4):
                o = ready(("fin", m))
                copy_out(("fin", m), fT[:, m, :], o[:, :])
            for m in range(4):
                tanh_tile(("fgate", m), ("fgate", m - 2) if m >= 2 else None, tanh_e[:, m % 2, :])
            for g in range(4):
                for h in range(2):
                    o = ready(("f1", g, h))
                    copy_out(("f1", g, h), dft1[:, g % 2, 2 * h:2 * h + 2, :],
                             o[:, :].rearrange("p (t n) -> p t n", t=2))
            for m in range(4):
                tanh_tile(("mgate", m), ("mgate", m - 2) if m >= 2 else ("fgate", m + 2), tanh_e[:, m % 2, :])
            for name, n, col, at in (("qaT", 3, V_QN, 0), ("kvaT", 2, V_KN, 3)):
                for k in range(n):
                    o = ready((name, k))
                    copy_out((name, k), nT[:, at + k, :], o[:, :], scale=vcol[:, col + k:col + k + 1])
            copied(("mgate", 3))
            for h in range(2):
                for i in range(TC, TALL):
                    o = ready(("qb", h, i))
                    copy_out(("qb", h, i), qrow[:, i, 4 * h:4 * h + 4, :],
                             o[:, 0:4 * MHD].rearrange("p (h n) -> p h n", h=4))
            for i in range(TALL):
                for h in range(2):
                    o = ready(("kvb", i, h))[:, :].rearrange("p (h n) -> p h n", h=4)
                    act.activation(krow[:, i, 4 * h:4 * h + 4, 0:NOPE], o[:, :, 0:NOPE], ACT.Copy)
                    copy_out(("kvb", i, h), ev[:, i, NOPE * 4 * h:NOPE * 4 * (h + 1)].rearrange(
                        "p (h n) -> p h n", h=4), o[:, :, NOPE:2 * NOPE])
            for h in range(MH):
                o = ready(("qT", h))
                copy_out(("qT", h), qT_e[:, h, :], o[0:MHD, :], scale=MLA_SCALE)
            for h in range(MH + 2):
                if h < MH:
                    b = h % 2
                    for i in range(TALL):
                        act.wait_ge(S["max_ready"], 3 * h + min(i, 2) + 1)
                        job = ("S", h, min(i, 2))
                        o = ready(job)
                        c0, n = (COLS * i, COLS) if i < 2 else (2 * COLS + N * (i - 2), N)
                        src = o[:, 0:COLS] if i < 2 else o[:, N * (i - 2):N * (i - 1)]
                        ins = act.activation(prob_e[:, b, c0:c0 + n], src, ACT.Exp, bias=negmax[:, b, i:i + 1],
                                             accum_out=esum[:, b, i:i + 1])
                        if i != 2:
                            release(ins, job)
                if 1 <= h <= MH:
                    a = h - 1
                    for i in range(2):
                        o = ready(("PT", a, i))
                        copy_out(("PT", a, i), probT_e[:, a % 2, i, :], o[:, :])
                if h == 3:
                    gate_rows(4, grow_e)

            act.wait_ge(S["xn_ready"], TALL + 1)
            act.dma_start(sink[:, 0, :], t["o_sink"].partition_broadcast(P) if False else
                          t["o_sink"].broadcast_to([P, GH])).then_inc(sink_in, 16)
            gate_rows(5, [grow1])
            high("oq0")
            modulate("oxT", whole_o, (2, 3))
            high("oq1", "okv", "og0")
            act.dma_start(fing, t["final_g"].unsqueeze(0).broadcast_to([P, D])).then_inc(fing_in, 16)
            for i in range(TALL):
                o = ready(("okv", i))
                if i < TC:
                    act.activation(ov[:, i, :], o[:, GKV * HD:2 * GKV * HD], ACT.Copy).then_inc(S["okv_act"], 1)
                else:
                    act.activation(ov[:, i, :], o[:, GKV * HD:2 * GKV * HD], ACT.Copy)
                    k = o[:, 0:GKV * HD].rearrange("p (g n) -> p g n", g=GKV)
                    for dup in range(2):
                        ins = act.activation(okr[:, i, :, dup, :], k, ACT.Copy)
                    release(ins, ("okv", i))
            high("og1")
            for m in range(4):
                tanh_tile(("og", m), ("og", m - 2) if m >= 2 else None, otanh[:, m % 2, :])
            for i in range(4):
                o = ready(("oqT", i))
                copy_out(("oqT", i), oqT[:, 2 * i:2 * i + 2, :], o[:, :].rearrange("p (a n) -> p a n", a=2), scale=HEAD_SCALE)
            for h in range(GH + 2):
                if h < GH:
                    b = h % 2
                    act.wait_ge(S["max_ready"], 3 * MH + h + 1)
                    for i in range(TC):
                        o = ready(("OS", h, i))
                        ins = act.activation(oprob[:, b, i, :], o[:, :], ACT.Exp, bias=negmax[:, b, i:i + 1],
                                             accum_out=esum[:, b, i:i + 1])
                        release(ins, ("OS", h, i))
                    act.activation(esink[:, b, :], negmax[:, b, 0:TC], ACT.Exp, bias=sink[:, 0, h:h + 1]
                                   ).then_inc(S["exp_done"], 1)
                if 1 <= h <= GH:
                    a = h - 1
                    o = ready(("OPT", a, 0))
                    copy_out(("OPT", a, 0), oprobT[:, a % 2, 0, :], o[:, :])

            act.wait_ge(S["x_out"], 1)
            act.wait_ge(S["angles_ready"], 1)
            act.activation(rotary[:, 5, :], rotary[:, 2, :], ACT.Sin)
            act.activation(rotary[:, 4, :], rotary[:, 3, :], ACT.Sin).then_inc(S["rotary_ready"], 1)
            with act.Fori(0, LAYERS) as l:
                sec = Section(l)
                order.section(sec, ACT_LINKS)
                high("in0")
                act.wait_ge(S["x_out"], sec.at("x_out", 0))
                act.dma_start(kH[:, :], t["hybrid_constants"]).then_inc(kH_in, 16)

                def layer_row(w):
                    return w[bass.ds(l, 1)]

                def rows_of(w, c0, n):
                    return layer_row(w)[:, c0:c0 + n].rearrange("o (k p) -> (o k) p", p=P)

                act.dma_start(lrow[R_CB:R_FQ, :], rows_of(t["b_in_2"], BW, 3 * BW)).then_inc(lrow_in, 16)
                act.dma_start(lrow[R_FQ:R_GT, :], rows_of(t["b_in_2"], 7 * BW, 2 * BW)).then_inc(lrow_in, 16)
                act.dma_start(lrow[R_GT:R_UP, :], rows_of(t["b_in_2"], GATE0, 4 * D)).then_inc(lrow_in, 16)
                act.dma_start(lrow[R_UP:R_CW, :], rows_of(t["b_up_2"], 0, DFF)).then_inc(lrow_in, 16)
                act.dma_start(lrow[R_CW:R_PS, :], layer_row(t["conv_w_2"]).rearrange("o j (m p) -> (o j m) p", p=P)
                              ).then_inc(lrow_in, 16)
                act.dma_start(lrow[R_PS:R_N, :], rows_of(t["pool_scale_2"], 0, BW)).then_inc(lrow_in, 16)
                for b0, c0, n in ((0, 0, 1), (1, 4 * BW, 3), (4, 9 * BW, 1)):
                    act.dma_start(brow[:, b0:b0 + n, :], layer_row(t["b_in_2"])[:, c0:c0 + n * BW].broadcast_to(
                        [P, n * BW]).rearrange("p (b n) -> p b n", b=n)).then_inc(bias_in, 16)
                with nc.allow_non_contiguous_dma(reason="4 forget biases, one to a partition"):
                    act.dma_start(fbias[:, :], layer_row(t["b_in_2"])[:, FORGET0:FORGET0 + FH].rearrange(
                        "o (f u) -> (o f) u", u=1)).then_inc(bias_in, 16)
                act.wait_ge(wpool_zero, 1)
                for g in range(4):
                    r = HD * (g % 2)
                    act.dma_start(wpool[r:r + HD, g // 2, r:r + HD],
                                  layer_row(t["w_pool_2"])[:, g].rearrange("o c d -> (o c) d")).then_inc(wpool_in, 16)
                for i, name in enumerate(("ln1_g_2", "ln1_b_2")):
                    act.dma_start(lnrow[:, i, :], layer_row(t[name]).broadcast_to([P, D])).then_inc(ln_in, 16)

                def modulate_u(name, cols):
                    for i in range(4):
                        o = ready((name, i))
                        for j in range(2):
                            k = 2 * i + j
                            ins = act.activation(whole[:, k, :], o[:, N * j:N * j + N], ACT.Identity,
                                                 bias=cols[:, 0, k:k + 1], scale=cols[:, 1, k:k + 1])
                        release(ins, (name, i))

                modulate_u("xT", mcol)
                high("in1")
                act.wait_ge(S["cols_ready"], sec.at("cols_ready", 1))

                def add_columns(job, dst, row):
                    o = ready(job)
                    for m in range(2):
                        ins = act.activation(dst[:, m, :], o[:, N * m:N * m + N], ACT.Identity,
                                             bias=lcol[:, row + m:row + m + 1])
                    release(ins, job)

                add_columns(("cb",), cb, R_CB)
                high("in2")
                add_columns(("cc",), cc, R_CB + 2)
                add_columns(("ch",), chh, R_CB + 4)
                high("in3", "in4", "forget")
                add_columns(("fk",), kT[:, 2:4, :], R_FQ + 2)
                high("gate0")
                act.wait_ge(bias_in, l * (16 * 4) + 16 * 4)
                o = ready(("forget",))
                act.activation(forget[:, 0, :], o[0:FH, 0:N], ACT.Identity, bias=fbias[:, 0:1])
                ins = act.activation(forget[:, 1, :], o[0:FH, 0:N], ACT.Abs, bias=fbias[:, 0:1])
                release(ins, ("forget",))
                copied(("forget",))
                order.link(act.activation(forget[:, 2, :], forget[:, 1, :], ACT.Exp, scale=-1.0))
                act.activation(forget[:, 3, :], forget[:, 2, :], ACT.Ln, bias=1.0).then_inc(S["forget_act"], 1)
                for m in range(2):
                    o = ready(("poolT", m))
                    copy_out(("poolT", m), pooled[:, m, :], o[:, 0:N])
                o = ready(("mkT",))
                copy_out(("mkT",), kT[:, 0:2, :], o[:, :].rearrange("p (a n) -> p a n", a=2))

                def gate_tanh(j):
                    for i in range(2):
                        o = ready(("gate", j, i))
                        if j > 0:
                            copied(("prod", j - 1, i))
                        for m in range(2):
                            c = 4 * j + 2 * i + m
                            ins = act.activation(tanhg[:, i, N * m:N * m + N], o[:, N * m:N * m + N], ACT.Tanh,
                                                 bias=hcol[:, c:c + 1], scale=0.5)
                        release(ins, ("gate", j, i))

                for a in range(10):
                    if a < 8:
                        b = a % 2
                        o = ready(("S", a))
                        act.wait_ge(S["max_ready"], sec.at("max_ready", a + 1))
                        for i in range(TC):
                            c, n = P * i, P * (i + 1)
                            ins = act.activation(prob[:, b, c:c + n], o[:, c:c + n], ACT.Exp,
                                                 bias=negmax[:, b, i:i + 1], accum_out=esum[:, b, i:i + 1])
                        release(ins, ("S", a))
                    if a in GATES_BESIDE:
                        high(f"gate{GATES_BESIDE.index(a) + 1}")
                        gate_tanh(GATES_BESIDE.index(a))
                    if 1 <= a <= 8:
                        o = ready(("PT", a - 1))
                        copy_out(("PT", a - 1), probT[:, (a - 1) % 2, :], o[:, 0:3 * P])
                    if a == MODS_BESIDE[0]:
                        gate_rows(0, [grow1], scale=0.5)
                high("gate7")
                gate_tanh(6)
                high("o0")
                gate_tanh(7)
                high("o1", "up0")
                act.wait_ge(S["norm1"], sec.at("norm1", 1))
                for i, name in enumerate(("ln2_g_2", "ln2_b_2")):
                    act.dma_start(lnrow[:, i, :], layer_row(t[name]).broadcast_to([P, D])).then_inc(ln_in, 16)
                copied(("mod", 1))
                copied(("mod", 2))
                modulate_u("x2T", mcol2)
                gate_rows(3, [grow1])
                for j in range(8):
                    high(f"down{j - 1}" if j > 0 else "up1")
                    for i in range(2):
                        o = ready(("up", j, i))
                        for m in range(2):
                            c = R_UP + 4 * j + 2 * i + m
                            ins = act.activation(hdn[:, j % 2, 2 * i + m, :], o[:, N * m:N * m + N], ACT.Relu,
                                                 bias=lcol[:, c:c + 1])
                        release(ins, ("up", j, i))
                    if j > 0:
                        high(f"up{j + 1}" if j < 7 else "down7")
                order.end_layer()

        @block.vector
        def _(dve):
            sec = Section()
            order = Order(dve, S["dve_order"])
            order.section(sec)
            link = order.link

            def ready(job):
                b, n = sec.bank(job, 1)
                dve.wait_ge(full[b], n)
                return bank[b]

            def release(ins, job):
                ins.then_inc(free[sec.bank(job, 0)[0]], 1)

            def copied(job):
                b, n = sec.bank(job, 1)
                dve.wait_ge(free[b], n)

            def gemv(c, q):
                b = c % 2
                _, streams, _ = sec.mods[c]
                slot, before = sec.chunk(c, q)
                dve.wait_ge(m_full[slot], before * 16 + 16)
                if q == 0:
                    dve.wait_ge(acc_init[b], sec.biases(c) * 16)
                first_block = sec.layer is None and c < 6
                w = mring[:, slot, :].rearrange("p (k n) -> p k n", k=4)
                for k in range(4):
                    for v in range(streams):
                        a = acc[v][:, b, COLS * (q // 2):COLS * (q // 2) + COLS]
                        col = (V_C + 8 * v if first_block else V_C2) + 4 * (q % 2) + k
                        ins = dve.scalar_tensor_tensor(out=a, in0=w[:, k, :], scalar=ccol[:, col:col + 1], in1=a,
                                                       op0=ALU.mult, op1=ALU.add)
                        if k == 3 and v == streams - 1:
                            ins.then_inc(m_free[slot], 1)
                            dve.wait_ge(m_free[slot], before + 1)
                        elif v == streams - 1:
                            link(ins)

            def rsqrt(n, mean_square, scale=1.0, eps=RMS_EPS):
                v, y, s, _ = (nwt[:, i, 0:n] for i in range(4))
                if mean_square:
                    link(dve.tensor_tensor(v, mv[:, 0:n, 0], mv[:, 0:n, 0], ALU.mult))
                    link(dve.scalar_tensor_tensor(out=v, in0=mv[:, 0:n, 1], scalar=eps, in1=v,
                                                  op0=ALU.add, op1=ALU.add))
                else:
                    link(dve.tensor_scalar(v, mv[:, 0:n, 1], eps, None, ALU.add))
                link(dve.tensor_scalar(nwi[:, 0, 0:n], v.bitcast(I32), 1, None, ALU.logical_shift_right))
                link(dve.tensor_scalar(nwi[:, 1, 0:n], nwi[:, 0, 0:n], -1.0, float(RSQRT_BITS), ALU.mult, ALU.add))
                g = nwi[:, 1, 0:n].bitcast(F32)
                for _ in range(3):
                    link(dve.tensor_tensor(s, g, g, ALU.mult))
                    link(dve.scalar_tensor_tensor(out=s, in0=s, scalar=-0.5, in1=v, op0=ALU.mult, op1=ALU.mult))
                    link(dve.scalar_tensor_tensor(out=y, in0=s, scalar=1.5, in1=g, op0=ALU.add, op1=ALU.mult))
                    g = y
                return y

            def statistics(i, parts):
                for j, p in enumerate(parts):
                    ins = dve.bn_stats(stat[:, i, 6 * j:6 * j + 6], p)
                link(ins)
                if sec.layer is not None:
                    dve.memset(idle[:, 8 + i:9 + i], 0.0)
                return dve.bn_aggr(mv[:, i, :], stat[:, i, 0:6 * len(parts)])

            def norm_x(dst, chunks, mean_square, eps):
                for i in range(chunks):
                    ins = statistics(i, [x[:, i, 0:COLS], x[:, i, COLS:D]])
                link(ins)
                y = rsqrt(chunks, mean_square, eps=eps)
                for i in range(chunks):
                    if mean_square:
                        ins = dve.tensor_scalar(dst[:, i, :], x[:, i, :], y[:, i:i + 1], None, ALU.mult)
                    else:
                        ins = dve.tensor_scalar(dst[:, i, :], x[:, i, :], mv[:, i, 0:1], y[:, i:i + 1],
                                                ALU.subtract, ALU.mult)
                    ins.then_inc(S["xn_ready"], 1)

            def mod_columns(c, dst, scale, gains=None):
                _, streams, _ = sec.mods[c]
                o = ready(("mod", c))
                if sec.layer is None and c < PE_MODS:
                    cols = dst[:, scale, :]
                    bias = vcol[:, V_BM + KD * c:V_BM + KD * c + KD].unsqueeze(1).broadcast_to([P, 2, KD])
                    ins = dve.tensor_tensor(cols.rearrange("p (v k) -> p v k", v=2),
                                            o[:, 0:2 * KD].rearrange("p (k v) -> p v k", v=2), bias, ALU.add)
                    if scale:
                        link(ins)
                        for v in range(2):
                            d = dst[:, scale, KD * v:KD * v + KD]
                            ins = dve.scalar_tensor_tensor(out=d, in0=d, scalar=1.0, in1=gains, op0=ALU.add,
                                                           op1=ALU.mult)
                    release(ins, ("mod", c))
                    return
                for v in range(streams):
                    src, d = o[:, KD * v:KD * v + KD], dst[:, scale, KD * v:KD * v + KD]
                    if not scale:
                        ins = dve.tensor_copy(d, src)
                    elif gains is None:
                        ins = dve.tensor_scalar(d, src, 1.0, None, ALU.add)
                    else:
                        ins = dve.scalar_tensor_tensor(out=d, in0=src, scalar=1.0, in1=gains, op0=ALU.add,
                                                       op1=ALU.mult)
                release(ins, ("mod", c))

            def rotate(dst, src, cos, sin, heads, half, products, job=None):
                def over(table):
                    return table.unsqueeze(1).broadcast_to([P, heads, half])
                pc, ps = products
                for i in range(2):
                    dve.tensor_tensor(pc[:, :, i, :], src[:, :, i, :], over(cos), ALU.mult)
                    ins = dve.tensor_tensor(ps[:, :, i, :], src[:, :, i, :], over(sin), ALU.mult)
                if job:
                    release(ins, job)
                    copied(job)
                else:
                    link(ins)
                dve.tensor_tensor(dst[:, :, 0, :], pc[:, :, 0, :], ps[:, :, 1, :], ALU.subtract)
                return dve.tensor_tensor(dst[:, :, 1, :], pc[:, :, 1, :], ps[:, :, 0, :], ALU.add)

            def gated_tile(job, n, dst, src):
                o = ready(job)
                dve.wait_ge(S["tanh_done"], n + 1)
                ins = dve.scalar_tensor_tensor(out=dst, in0=src, scalar=1.0, in1=o[:, :], op0=ALU.add, op1=ALU.mult)
                release(ins, job)

            def maxima(src, h, i, signal=None):
                return dve.tensor_reduce(negmax[:, h % 2, i:i + 1], src, AX_X, ALU.max, negate=True)

            def normalise(blocks, h):
                for i, p in enumerate(blocks):
                    ins = dve.tensor_scalar(p, p, rsum[:, h % 2, i:i + 1], None, ALU.mult)
                ins.then_inc(S["p_ready"], 1)

            def add_output(h, i, job, gate, tmp, n):
                o = ready(job)
                cols = slice(COLS * h, COLS * h + COLS)
                ins = dve.tensor_tensor(tmp, o[:, :], gate[:, cols], ALU.mult)
                release(ins, job)
                copied(job)
                return dve.tensor_tensor(x[:, i, cols], x[:, i, cols], tmp, ALU.add)

            def low(name, *parts):
                for h in parts or range(2):
                    slot, _ = sec.slab((name, h))
                    n, s = sec.split((name, h))
                    dve.wait_ge(S["high_ready"], sec.at("high_ready", n + 1))
                    _, kn, cols = w_slab(name, h, 0)
                    hi, lo = (whigh_o, wlow_o) if sec.layer is None else (whigh, wlow)
                    dve.tensor_tensor(lo[:, s, 0:kn * cols], wring[:, slot, 0:kn * cols],
                                      hi[:, s, 0:kn * cols].bitcast(F32), ALU.subtract
                                      ).then_inc(w_free[slot], 1)

            dve.wait_ge(consts_in, 16)
            o = ready(("vec",))
            ins = dve.tensor_copy(vcol[:, :], o[:, 0:V_N])
            release(ins, ("vec",))
            dve.wait_ge(S["ctanh_done"], 1)
            link(dve.scalar_tensor_tensor(out=ccol[:, :], in0=ctanh[:, :], scalar=1.0, in1=vcol[:, 0:24],
                                          op0=ALU.add, op1=ALU.mult))
            dve.tensor_scalar(ccol[:, :], ccol[:, :], 0.5, None, ALU.mult).then_inc(S["silu_ready"], 1)
            dve.wait_ge(S["silu_ready"], 1)
            dve.wait_ge(x_in, 32)
            norm_x(xn_e, TALL, True, RMS_EPS)
            mod_columns(0, mcol, 0)
            mod_columns(1, mcol, 1, vcol[:, V_NG:V_NG + KD])
            for q in range(4):
                gemv(2, q)

            for m in range(4):
                gated_tile(("fgate", m), m, eyT[:, m, :], tanh_e[:, m % 2, :])
            gemv(3, 0)
            gemv(3, 1)
            mod_columns(2, mcol, 0)
            for job, dst, width in (("qa", qn, QR), ("kva", kvn, KVR)):
                for i in range(TALL):
                    ins = statistics(i, [ready((job, i))[:, 0:width]])
                link(ins)
                y = rsqrt(TALL, True)
                for i in range(TALL):
                    o = bank[sec.bank((job, i), 0)[0]]
                    if job == "kva":
                        dve.tensor_copy(kpe[:, i, 0, :], o[:, KVR:KVR + ROPE])
                    ins = dve.tensor_scalar(dst[:, i, :], o[:, 0:width], y[:, i:i + 1], None, ALU.mult)
                    release(ins, (job, i))
                if job == "qa":
                    gemv(3, 2)
                    gemv(3, 3)
            mod_columns(3, mcol, 1, vcol[:, V_NG + KD:V_NG + 2 * KD])
            gemv(4, 0)
            for g in range(4):
                o = ready(("f2", g))
                ins = dve.scalar_tensor_tensor(out=eyT[:, g, :], in0=o[:, :], scalar=0.5, in1=eyT[:, g, :],
                                               op0=ALU.mult, op1=ALU.mult)
                release(ins, ("f2", g))
            for m in range(4):
                gated_tile(("mgate", m), 4 + m, eyT[:, 4 + m, :], tanh_e[:, m % 2, :])
            gemv(4, 1)
            cos16, sin16 = rope_t[:, :, 0:16], rope_t[:, :, 16:32]
            for i in range(TC):
                src = kpe[:, i, 0, :].rearrange("p (h s n) -> p h s n", h=1, s=2)
                ps = [kpe[:, i, 1 + s, :].rearrange("p (h s n) -> p h s n", h=1, s=2) for s in range(2)]
                link(rotate(src, src, cos16[:, i, :], sin16[:, i, :], 1, 16, ps))
            for h in range(2):
                for i in range(TC):
                    o = ready(("qb", h, i))[:, 0:4 * MHD].rearrange("p (h n) -> p h n", h=4)
                    dst = qrow[:, i, 4 * h:4 * h + 4, :]
                    dve.tensor_copy(dst[:, :, 0:NOPE], o[:, :, 0:NOPE])
                    ps = [qrot[:, s, :].rearrange("p (h s n) -> p h s n", h=4, s=2) for s in range(2)]
                    ins = rotate(dst[:, :, NOPE:MHD].rearrange("p h (s n) -> p h s n", s=2),
                                 o[:, :, NOPE:MHD].rearrange("p h (s n) -> p h s n", s=2),
                                 cos16[:, i, :], sin16[:, i, :], 4, 16, ps, job=("qb", h, i))
                    ins.then_inc(S["q_lat"], 1)
                    dve.wait_ge(S["q_lat"], 2 * h + i + 1)
            for i in range(TALL):
                ins = dve.tensor_copy(krow[:, i, :, NOPE:MHD], kpe[:, i, 0, :].unsqueeze(1).broadcast_to(
                    [P, MH, ROPE]))
            ins.then_inc(S["kpe_ready"], 1)
            gemv(4, 2)
            gemv(4, 3)
            for h in range(MH):
                o = ready(("kT", h))
                ins = dve.tensor_copy(kT_e[:, h, :], o[0:MHD, :])
                release(ins, ("kT", h))
            for h in range(MH + 2):
                if h < MH:
                    b = h % 2
                    for i in range(TC):
                        maxima(ready(("S", h, i))[:, :], h, i).then_inc(S["max_ready"], 1)
                    dve.tensor_reduce(negmax[:, b, 2:4], ready(("S", h, 2))[:, :].rearrange("p (i n) -> p i n", i=2),
                                      AX_X, ALU.max, negate=True).then_inc(S["max_ready"], 1)
                    if h >= 4:
                        gemv(5, h - 4)
                    copied(("S", h, 2))
                    link(dve.reciprocal(rsum[:, b, :], esum[:, b, :]))
                    normalise([prob_e[:, b, 0:COLS], prob_e[:, b, COLS:2 * COLS],
                               prob_e[:, b, 2 * COLS:2 * COLS + N], prob_e[:, b, 2 * COLS + N:3 * COLS]], h)
                if 1 <= h <= MH:
                    a = h - 1
                    o = ready(("PT", a, 2))
                    ins = dve.tensor_copy(probT_e[:, a % 2, 2, :], o[:, :])
                    release(ins, ("PT", a, 2))
                if h >= 3 and h % 2 == 1:
                    g = (h - 3) // 2
                    o = ready(("PV", g))
                    ins = dve.scalar_tensor_tensor(out=eyT[:, 4 + g, :], in0=o[:, :], scalar=0.5,
                                                   in1=eyT[:, 4 + g, :], op0=ALU.mult, op1=ALU.mult)
                    release(ins, ("PV", g))
            for v in range(2):
                copied(("mod", 4, v, 1))
            for h in range(2):
                for i in range(TALL):
                    last = add_output(h, i, ("eout", h, i), grow_e[i // TC], etmp[:, i % 2, :], i)
            link(last)

            norm_x(xn_o, TALL, True, RMS_EPS)
            low("oq0", 0)
            for k in range(KD):
                copied(("oxT", k))
                link(dve.tensor_copy(hhigh_o[:, k, :], whole_o(k)))
                dve.tensor_tensor(hlow_o[:, k, :], whole_o(k), hhigh_o[:, k, :].bitcast(F32), ALU.subtract
                                  ).then_inc(S["u_ready"], 1)
            low("oq0", 1)
            cos32, sin32 = rope_t[:, :, 32:64], rope_t[:, :, 64:96]
            dve.wait_ge(sink_in, 16)
            link(dve.tensor_scalar(sink[:, 1, :], sink[:, 0, :], -1.0, None, ALU.mult))
            rot = [orot[:, s, :, :].rearrange("p h n -> p (h n)")[:, 0:8 * HD].rearrange(
                "p (h s n) -> p h s n", h=8, s=2) for s in range(2)]
            rotk = [r[:, 0:GKV] for r in rot]
            for h in range(2):
                low(("oq1", "okv")[h])
                for i in range(TC):
                    o = ready(("oq", h, i))[:, :].rearrange("p (h s n) -> p h s n", h=8, s=2)
                    ins = rotate(oq[:, i, COLS * h:COLS * h + COLS].rearrange("p (h s n) -> p h s n", h=8, s=2), o,
                                 cos32[:, i, :], sin32[:, i, :], 8, HD // 2, rot, job=("oq", h, i))
                    ins.then_inc(S["q_lat"], 1)
                    dve.wait_ge(S["q_lat"], 4 + 2 * h + i + 1)
            low("og0")
            for i in range(TC):
                o = ready(("okv", i))[:, 0:GKV * HD].rearrange("p (h s n) -> p h s n", h=GKV, s=2)
                dve.wait_ge(S["okv_act"], i + 1)
                ins = rotate(okr[:, i, :, 0, :].rearrange("p g (s n) -> p g s n", s=2), o,
                             cos32[:, i, :], sin32[:, i, :], GKV, HD // 2, rotk, job=("okv", i))
                link(ins)
                dve.tensor_copy(okr[:, i, :, 1, :], okr[:, i, :, 0, :]).then_inc(S["kpe_ready"], 1)
            low("og1")
            for m in range(4):
                gated_tile(("og", m), 8 + m, oyT[:, 2 * m:2 * m + 2, :].rearrange("p a n -> p (a n)"),
                           otanh[:, m % 2, :])
            for g in range(GKV):
                o = ready(("okT", g))
                ins = dve.tensor_copy(okT[:, g, :], o[:, :])
                release(ins, ("okT", g))
            for h in range(GH + 2):
                if h < GH:
                    b = h % 2
                    for i in range(TC):
                        ins = maxima(ready(("OS", h, i))[:, :], h, i)
                    link(ins)
                    dve.tensor_scalar(negmax[:, b, 0:TC], negmax[:, b, 0:TC], sink[:, 1, h:h + 1], None, ALU.min
                                      ).then_inc(S["max_ready"], 1)
                    if h < 8:
                        gemv(6 + h // 4, h % 4)
                    dve.wait_ge(S["exp_done"], h + 1)
                    link(dve.tensor_tensor(esum[:, b, 0:TC], esum[:, b, 0:TC], esink[:, b, :], ALU.add))
                    link(dve.reciprocal(rsum[:, b, 0:TC], esum[:, b, 0:TC]))
                    normalise([oprob[:, b, 0, :], oprob[:, b, 1, :]], h)
                if 1 <= h <= GH:
                    a = h - 1
                    o = ready(("OPT", a, 1))
                    ins = dve.tensor_copy(oprobT[:, a % 2, 1, :], o[:, :])
                    release(ins, ("OPT", a, 1))
                if h >= 3 and h % 2 == 1:
                    g = (h - 3) // 2
                    o = ready(("OPV", g))
                    ins = dve.scalar_tensor_tensor(out=oyT[:, g, :], in0=o[:, 0:N], scalar=0.5,
                                                   in1=oyT[:, g, :], op0=ALU.mult, op1=ALU.mult)
                    release(ins, ("OPV", g))
                if h == 7:
                    mod_columns(6, mcol, 0)
            copied(("mod", 5, 0, 1))
            for h in range(2):
                for i in range(TC):
                    last = add_output(h, i, ("oout", h, i), grow1, otmp[:, i % 2, :], i)
            link(last)
            mod_columns(7, mcol, 1)
            for i in range(TC):
                ins = statistics(i, [x[:, i, 0:COLS], x[:, i, COLS:D]])
            link(ins)
            y = rsqrt(TC, True)
            dve.wait_ge(fing_in, 16)
            for i in range(TC):
                ins = dve.scalar_tensor_tensor(out=x[:, i, :], in0=x[:, i, :], scalar=y[:, i:i + 1], in1=fing,
                                               op0=ALU.mult, op1=ALU.mult)
            ins.then_inc(S["x_out"], 1)
            dve.memset(wpool[:, :, :], 0.0).then_inc(wpool_zero, 1)
            link(dve.memset(conv[:, :, :], 0.0))

            dve.wait_ge(pos_in, 16)
            link(dve.tensor_copy(posf[:, :], posi[:, :]))
            for i in range(TC):
                ins = dve.tensor_scalar(rotary[:, 0, 8 * i:8 * i + 8], kst[:, K_INV:K_INV + 8], posf[:, i:i + 1],
                                        None, ALU.mult)
            link(ins)
            link(dve.tensor_scalar(rotary[:, 1, :], rotary[:, 0, :], 1.0 / (2.0 * 3.141592653589793), ROUND,
                                   ALU.mult, ALU.add))
            link(dve.tensor_scalar(rotary[:, 1, :], rotary[:, 1, :], ROUND, None, ALU.subtract))
            for part in (TWO_PI_1, TWO_PI_2, TWO_PI_3):
                src = 0 if part == TWO_PI_1 else 2
                link(dve.scalar_tensor_tensor(out=rotary[:, 2, :], in0=rotary[:, 1, :], scalar=-part,
                                              in1=rotary[:, src, :], op0=ALU.mult, op1=ALU.add))
            link(dve.tensor_scalar(rotary[:, 2, :], rotary[:, 2, :], 3.1415925, -3.1415925, ALU.min, ALU.max))
            link(dve.tensor_scalar(rotary[:, 3, :], rotary[:, 2, :], -1.0, None, ALU.mult))
            link(dve.tensor_tensor(rotary[:, 3, :], rotary[:, 3, :], rotary[:, 2, :], ALU.max))
            dve.tensor_scalar(rotary[:, 3, :], rotary[:, 3, :], -1.0, 1.5707963267948966, ALU.mult, ALU.add
                              ).then_inc(S["angles_ready"], 1)
            dve.wait_ge(S["rotary_ready"], 1)
            cos8 = rotary[:, 4, :].rearrange("p (t n) -> p t n", t=TC)
            sin8 = rotary[:, 5, :].rearrange("p (t n) -> p t n", t=TC)

            with dve.Fori(0, LAYERS) as l:
                sec = Section(l)
                order.section(sec, DVE_LINKS)

                def split_u(i):
                    src, hi, lo = (v[:, 2 * i:2 * i + 2, :] for v in (whole, uhigh, ulow))
                    link(dve.tensor_copy(hi, src))
                    dve.tensor_tensor(lo, src, hi.bitcast(F32), ALU.subtract).then_inc(S["u_ready"], 1)

                norm_x(xn, TC, False, LN_EPS)
                low("in0", 0)
                for i in range(4):
                    copied(("xT", i))
                    split_u(i)
                low("in0", 1)
                low("in1", 0)
                o = ready(("cols",))
                ins = dve.tensor_copy(lcol[:, :], o[:, 0:R_N])
                release(ins, ("cols",))
                copied(("cols",))
                dve.tensor_scalar(hcol[:, :], lcol[:, R_GT:R_UP], 0.5, None, ALU.mult).then_inc(S["cols_ready"], 1)
                dve.wait_ge(bias_in, l * (16 * 4) + 16 * 4)
                low("in1", 1)

                def add_rows(job, dst, b0, nt, n):
                    o = ready(job)
                    ins = dve.tensor_tensor(dst, o[:, 0:nt * n].rearrange("p (t n) -> p t n", t=nt),
                                            brow[:, b0:b0 + n // BW, :].rearrange("p b n -> p (b n)").unsqueeze(1)
                                            .broadcast_to([P, nt, n]), ALU.add)
                    release(ins, job)

                add_rows(("pin",), pin, 0, TC, BW)
                low("in2")
                copied(("ch",))
                link(dve.tensor_tensor(conv[:, :, 2:N + 2], cc[:, :, :], chh[:, :, :], ALU.mult))
                for j in range(3):
                    for m in range(2):
                        w = lcol[:, R_CW + 2 * j + m:R_CW + 2 * j + m + 1]
                        if j == 0:
                            ins = dve.tensor_scalar(cc[:, m, :], conv[:, m, 0:N], w, None, ALU.mult)
                        else:
                            ins = dve.scalar_tensor_tensor(out=cc[:, m, :], in0=conv[:, m, j:N + j], scalar=w,
                                                           in1=cc[:, m, :], op0=ALU.mult, op1=ALU.add)
                    link(ins)
                dve.tensor_tensor(yT[:, 1, :, :], cb, cc[:, :, :], ALU.mult).then_inc(S["conv_ready"], 1)
                low("in3")
                gemv(0, 0)
                for i in range(TC):
                    add_rows(("mqk", i), mqk[:, i:i + 1, :], 1, 1, COLS)
                    copied(("mqk", i))
                    part = mqk[:, i, :].rearrange("p (h n) -> p h n", h=8)[:, :, 0:16].rearrange(
                        "p h (s n) -> p h s n", s=2)
                    prods = [rtmp[:, s, :, :].rearrange("p h (s n) -> p h s n", s=2) for s in range(2)]
                    ins = rotate(part, part, cos8[:, i, :], sin8[:, i, :], 8, 8, prods)
                    ins.then_inc(S["rotated"], 1)
                    dve.wait_ge(S["rotated"], sec.at("rotated", i + 1))
                low("in4")
                add_rows(("mv",), vr[:, :, 0:4, :].rearrange("p t h n -> p t (h n)"), 3, TC, BW)
                o = ready(("fq",))
                for m in range(2):
                    ins = dve.tensor_scalar(qT[:, 2 + m, :], o[:, N * m:N * m + N],
                                            lcol[:, R_FQ + m:R_FQ + m + 1], HEAD_SCALE, ALU.add, ALU.mult)
                release(ins, ("fq",))
                low("forget")
                low("gate0")
                gemv(0, 1)
                add_rows(("fv",), vr[:, :, 4:8, :].rearrange("p t h n -> p t (h n)"), 4, TC, BW)
                dve.wait_ge(S["forget_act"], sec.at("forget_act", 1))
                link(dve.scalar_tensor_tensor(out=forget[:, 0, :], in0=forget[:, 0, :], scalar=0.0,
                                              in1=forget[:, 3, :], op0=ALU.min, op1=ALU.subtract))
                link(dve.memset(forget[:, 1, :], 1.0))
                link(dve.tensor_tensor_scan(forget[:, 4, :], forget[:, 1, :], forget[:, 0, :], 0.0,
                                            ALU.mult, ALU.add))
                dve.tensor_scalar(forget[:, 5, :], forget[:, 4, :], -1.0, None, ALU.mult
                                  ).then_inc(S["forget_ready"], 1)
                o = ready(("mixT",))
                for m in range(2):
                    ins = dve.tensor_scalar(yT[:, 0, m, :], o[:, N * m:N * m + N],
                                            lcol[:, R_PS + m:R_PS + m + 1], None, ALU.mult)
                release(ins, ("mixT",))
                o = ready(("mqT",))
                ins = dve.tensor_scalar(qT[:, 0:2, :], o[:, :].rearrange("p (a n) -> p a n", a=2), HEAD_SCALE, None,
                                        ALU.mult)
                release(ins, ("mqT",))

                def gate_products(j):
                    for i in range(2):
                        n = 2 * j + i
                        o = ready(("prod", j, i))
                        copied(("gate", j, i))
                        m = 4 * (j % 2) + 2 * i
                        if j < 2:
                            dst = merged[:, m:m + 2, :].rearrange("p m n -> p (m n)")
                        else:
                            dst = term[:, i, :]
                            if j > 2:
                                dve.wait_ge(S["merged"], sec.at("merged", n - 5))
                        ins = dve.scalar_tensor_tensor(out=dst, in0=tanhg[:, i, :], scalar=1.0, in1=o[:, :],
                                                       op0=ALU.add, op1=ALU.mult)
                        release(ins, ("prod", j, i))

                chunk = 2
                for a in range(10):
                    if a < 8:
                        b = a % 2
                        o = ready(("S", a))
                        maxima(o[:, 0:P], a, 0)
                        maxima(o[:, P:3 * P], a, 1).then_inc(S["max_ready"], 1)
                        copied(("S", a))
                        link(dve.reciprocal(rsum[:, b, 0:TC], esum[:, b, 0:TC]))
                        normalise([prob[:, b, 0:P], prob[:, b, P:3 * P]], a)
                    if a in GATES_BESIDE:
                        low(f"gate{GATES_BESIDE.index(a) + 1}")
                        gate_products(GATES_BESIDE.index(a))
                    if a >= 3 and a % 2 == 1:
                        g = (a - 3) // 2
                        o = ready(("PV", g))
                        ins = dve.tensor_copy(yT[:, 2 + g // 2, g % 2, :], o[:, 0:N])
                        release(ins, ("PV", g))
                    if a in MODS_BESIDE[1:]:
                        mod_columns(MODS_BESIDE.index(a), mcol2, MODS_BESIDE.index(a) - 1)
                    for _ in range(CHUNKS_BESIDE[a]):
                        gemv(chunk // 4, chunk % 4)
                        chunk += 1
                low("gate7")
                gate_products(6)
                low("o0")
                gate_products(7)
                for i in range(4):
                    dve.wait_ge(S["merged"], sec.at("merged", 8 + i + 1))
                    split_u(i)
                low("o1")

                def residual(jobs, rows_in, signal):
                    for a in range(2):
                        if jobs == "o" and a == 1:
                            low("up0", 0)
                        for b in range(2):
                            job = (jobs, a, b)
                            h, i = (a, b) if jobs == "o" else (b, a)
                            o = ready(job)
                            cols = slice(COLS * h, COLS * h + COLS)
                            ins = dve.tensor_tensor(xn[:, i, cols], o[:, :], grow1[:, cols], ALU.mult)
                            release(ins, job)
                            copied(job)
                            ins = dve.scalar_tensor_tensor(out=x[:, i, cols], in0=x[:, i, cols], scalar=ALPHA,
                                                           in1=xn[:, i, cols], op0=ALU.mult, op1=ALU.add)
                            if h == 1:
                                link(ins)
                                last = statistics(i, [x[:, i, 0:COLS], x[:, i, COLS:D]])
                    link(last)
                    dve.wait_ge(ln_in, rows_in)
                    for i in range(TC):
                        ins = dve.scalar_tensor_tensor(out=x[:, i, :], in0=x[:, i, :], scalar=mv[:, i, 0:1],
                                                       in1=lnrow[:, 0, :], op0=ALU.subtract, op1=ALU.mult)
                    y = rsqrt(TC, False, eps=LN_EPS)
                    for i in range(TC):
                        ins = dve.scalar_tensor_tensor(out=x[:, i, :], in0=x[:, i, :], scalar=y[:, i:i + 1],
                                                       in1=lnrow[:, 1, :], op0=ALU.mult, op1=ALU.add)
                    ins.then_inc(S[signal], 1)
                    dve.wait_ge(S[signal], sec.at(signal, 1))

                copied(("mod", 0, 0, 1))
                residual("o", l * 64 + 32, "norm1")
                norm_x(xn, TC, False, LN_EPS)
                for i in range(4):
                    copied(("x2T", i))
                    split_u(i)
                low("up0", 1)
                for j in range(8):
                    gemv(4 + j // 4, j % 4)
                    low(f"down{j - 1}" if j > 0 else "up1")
                    copied(("up", j, 1))
                    hid, hi, lo = (v[:, j % 2, :, :] for v in (hdn, hhigh, hlow))
                    link(dve.tensor_tensor(hid, hid, hid, ALU.mult))
                    link(dve.tensor_copy(hi, hid))
                    dve.tensor_tensor(lo, hid, hi.bitcast(F32), ALU.subtract).then_inc(S["hdn_ready"], 1)
                    if j > 0:
                        low(f"up{j + 1}" if j < 7 else "down7")
                    if j == 6:
                        mod_columns(4, mcol, 0)
                mod_columns(5, mcol, 1)
                copied(("mod", 3, 0, 1))
                residual("down", l * 64 + 64, "x_out")
                order.end_layer()


def tables():
    import numpy as np

    def angles(width):
        rows = N // 64
        row = np.repeat(np.arange(rows, dtype=np.float32), 64)
        col = np.tile(np.arange(64, dtype=np.float32), rows)
        nf = width // 4
        inv = np.float32(10000.0) ** (-np.arange(nf, dtype=np.float32) / np.float32(nf))
        ang = np.concatenate([row[:, None] * inv, col[:, None] * inv], axis=-1).astype(np.float32)
        return np.cos(ang).astype(np.float32), np.sin(ang).astype(np.float32)

    def chunks(a):
        return np.concatenate([a[0:P], a[P:2 * P]], axis=1)

    k = np.zeros((P, K_N), np.float32)
    k[:, K_ID:K_ID + P] = np.eye(P)
    k[:, K_ONE:K_ONE + P] = 1.0
    q, j = np.arange(P)[:, None], np.arange(P)[None, :]
    k[:, K_CAUSAL:K_CAUSAL + P] = np.where(j <= q, 0.0, NEG)
    k[:, K_WIN:K_WIN + P] = np.where(j >= q, 0.0, NEG)
    k[:, K_ROPE:K_INV] = chunks(np.concatenate([*angles(ROPE), *angles(HD)], axis=1))
    k[:, K_INV:K_N] = np.float32(500000.0) ** (-np.arange(0, 16, 2, dtype=np.float32) / np.float32(16))

    e = np.zeros((P, KE_N), np.float32)
    norm = 1.0 / np.sqrt(N * P)
    ang = 2 * np.pi * ((np.arange(P)[:, None] * np.arange(P)[None, :]) % P) / P
    e[:, KE_CH:KE_SEQ] = np.concatenate([np.cos(ang), np.sin(ang)], axis=1) * norm
    ang = 2 * np.pi * ((np.arange(N)[:, None] * np.arange(N)[None, :]) % N) / N
    e[:, KE_SEQ:] = chunks(np.concatenate([np.cos(ang), -np.sin(ang)], axis=1))

    h = np.zeros((P, KH_N), np.float32)
    tok, src = np.arange(N)[None, :], np.arange(N)[:, None]
    pools = [np.where((src <= tok) & (src > tok - w), 1.0 / np.minimum(tok + 1, w), 0.0) - (src == tok)
             for w in POOLW]
    h[:, KH_POOL:KH_SEL] = chunks(np.concatenate(pools, axis=1))
    for f in range(FH):
        h[f, KH_SEL + N * f:KH_SEL + N * f + N] = 1.0
    return {"constants": k, "even_constants": e, "hybrid_constants": h}


_INS = ["x", "c", "ctx", "c_ctx", "w_mod", "b_mod", "norm_g", "e_w_in", "e_q_norm", "e_w_qb", "e_kv_norm",
        "e_w_kvb", "e_w_out", "o_w_in", "o_sink", "o_w_out", "final_g", "c_2", "positions_2", "w_ada_2",
        "b_ada_2", "w_in_2", "b_in_2", "w_pool_2", "pool_scale_2", "conv_w_2", "w_branch_2", "w_o_2",
        "ln1_g_2", "ln1_b_2", "w_up_2", "b_up_2", "w_down_2", "ln2_g_2", "ln2_b_2"]


def kernel(**inputs):
    import numpy as _np
    import concourse.bacc as _bacc
    from concourse import mybir as _mybir
    from concourse.bass_utils import run_bass_kernel_spmd as _run

    nc = _bacc.Bacc("TRN2", target_bir_lowering=False, num_devices=1)
    arrays, args = {}, {}
    for name, a in [(n, inputs[n]) for n in _INS] + list(tables().items()):
        a = _np.ascontiguousarray(a)
        arrays[f"in_{name}_dram"] = a
        args[name] = nc.dram_tensor(f"in_{name}_dram", a.shape, _mybir.dt.from_np(a.dtype), kind="ExternalInput").ap()
    out = nc.dram_tensor("out_0_dram", (1, N, D), F32, kind="ExternalOutput").ap()
    program(nc, args, out)
    r = _run(nc, [arrays], core_ids=[0])
    return r.results[0]["out_0_dram"]
```
